# Optimizing a Trainium2 kernel written in Bass

```python
import math
import jax, jax.numpy as jnp
from jax import lax
import numpy as np

"""One inference step (DEPTH trunk layers) of a hybrid causal decoder with Hymba-style
parallel head groups: forgetting-attention heads (FoX) next to LongNet-style dilated
sliding-window heads, between two half-step SwiGLU FFNs (macaron), all sub-layers
adaLN-modulated (shift/scale/gate) by a per-sequence conditioning vector.

Inputs: x_prompt (BATCH, SEQ, D_MODEL), x_sample (DEC_BATCH, DEC_SEQ, D_MODEL),
  cache_fox_k / cache_fox_v (DEPTH, N_POOL, PAGE_SIZE, H_FOX, HEAD_DIM) paged,
  cache_fox_logf (DEPTH, N_POOL, PAGE_SIZE, H_FOX) paged log-forget values,
  cache_win_k / cache_win_v (DEPTH, DEC_BATCH, min(MAX_WINDOW, PAST_LEN), H_DIL, HEAD_DIM),
  page_table (DEC_BATCH, PAST_LEN // PAGE_SIZE) int32, c_prompt (BATCH, D_MODEL),
  c_sample (DEC_BATCH, D_MODEL), then the weights.
Returns the tuple:
  y_prompt (BATCH, SEQ, D_MODEL), y_sample (DEC_BATCH, DEC_SEQ, D_MODEL),
  fox_k_prompt, fox_v_prompt (DEPTH, BATCH, SEQ, H_FOX, HEAD_DIM), fox_logf_prompt (DEPTH, BATCH, SEQ, H_FOX),
  win_k_prompt, win_v_prompt (DEPTH, BATCH, min(MAX_WINDOW, SEQ), H_DIL, HEAD_DIM),
  fox_k_sample, fox_v_sample (DEPTH, DEC_BATCH, DEC_SEQ, H_FOX, HEAD_DIM), fox_logf_sample (DEPTH, DEC_BATCH, DEC_SEQ, H_FOX),
  win_k_sample, win_v_sample (DEPTH, DEC_BATCH, DEC_SEQ, H_DIL, HEAD_DIM).
"""

D_MODEL = 2048
BATCH = 1
SEQ = 256
DEPTH = 1
DEC_BATCH = 8
DEC_SEQ = 4
PAST_LEN = 1024
PAGE_SIZE = 128

HEAD_DIM = 128
N_HEADS = D_MODEL // HEAD_DIM
H_FOX = N_HEADS // 2
H_DIL = N_HEADS - H_FOX
W_FOX = H_FOX * HEAD_DIM
W_DIL = H_DIL * HEAD_DIM
SPLITS = (W_FOX, 2 * W_FOX, 3 * W_FOX, 3 * W_FOX + H_FOX,
          3 * W_FOX + H_FOX + W_DIL, 3 * W_FOX + H_FOX + 2 * W_DIL)
D_IN = 3 * W_FOX + H_FOX + 3 * W_DIL
D_FF = ((8 * D_MODEL // 3 + 127) // 128) * 128
DILATED_PATTERNS = ((128, 1), (512, 4), (2048, 16))
MAX_WINDOW = 2048
NUM_BUCKETS = 32
MAX_EXACT = NUM_BUCKETS // 2
BLOCK = 128
EPS = 1e-6
N_SUBLAYERS = 3
MACARON = 0.5
FORGET_BIAS = 2.0
ATTN_SCALE = HEAD_DIM ** -0.5

kernel_name = "fox_dilated_macaron_adaln_decode_step"

def rmsnorm(x, g):
    x32 = x.astype(jnp.float32)
    y = x32 * lax.rsqrt(jnp.mean(x32 * x32, axis=-1, keepdims=True) + EPS)
    return (y * g.astype(jnp.float32)).astype(x.dtype)

def modulate(x, g, shift, scale):
    return rmsnorm(x, g) * (1.0 + scale) + shift

def adaln_params(c, w_ada, b_ada):
    m = jax.nn.silu(c) @ w_ada + b_ada
    return jnp.split(m[:, None, :], 3 * N_SUBLAYERS, axis=-1)

def swiglu(h, w1, w3, w2):
    return (jax.nn.silu(h @ w1) * (h @ w3)) @ w2

def t5_bucket(dist):
    d = dist.astype(jnp.float32)
    log_b = MAX_EXACT + jnp.log(jnp.maximum(d, MAX_EXACT) / MAX_EXACT) / math.log(MAX_WINDOW / MAX_EXACT) * (NUM_BUCKETS - MAX_EXACT)
    log_b = jnp.minimum(log_b.astype(jnp.int32), NUM_BUCKETS - 1)
    return jnp.where(dist < MAX_EXACT, dist, log_b)

def dilation_bias(rel_bias, window, dil):
    nk = window // dil
    return rel_bias[t5_bucket(dil * jnp.arange(nk + 1))]

def project_mix(h, w_in, b_forget, qn_fox, kn_fox, qn_dil, kn_dil):
    B, S, _ = h.shape
    z = h @ w_in
    qa, ka, va, fa, qb, kb, vb = jnp.split(z, SPLITS, axis=-1)
    qa = rmsnorm(qa.reshape(B, S, H_FOX, HEAD_DIM), qn_fox)
    ka = rmsnorm(ka.reshape(B, S, H_FOX, HEAD_DIM), kn_fox)
    va = va.reshape(B, S, H_FOX, HEAD_DIM)
    logf = jax.nn.log_sigmoid((fa + b_forget).astype(jnp.float32))
    qb = rmsnorm(qb.reshape(B, S, H_DIL, HEAD_DIM), qn_dil)
    kb = rmsnorm(kb.reshape(B, S, H_DIL, HEAD_DIM), kn_dil)
    vb = vb.reshape(B, S, H_DIL, HEAD_DIM)
    return qa, ka, va, logf, qb, kb, vb

def fox_attend(q, k, v, cq, ck, qpos, kpos):
    s = jnp.einsum('bqhd,bkhd->bhqk', q, k).astype(jnp.float32) * ATTN_SCALE
    s = s + (jnp.swapaxes(cq, 1, 2)[..., :, None] - jnp.swapaxes(ck, 1, 2)[..., None, :])
    s = jnp.where(kpos[None, :] <= qpos[:, None], s, -jnp.inf)
    p = jax.nn.softmax(s, axis=-1)
    return jnp.einsum('bhqk,bkhd->bqhd', p.astype(v.dtype), v)

def fox_prompt(q, k, v, cum):
    B, S, H, D = q.shape
    nb = S // BLOCK
    qb = jnp.swapaxes(q.reshape(B, nb, BLOCK, H, D), 0, 1)
    cb = jnp.swapaxes(cum.reshape(B, nb, BLOCK, H), 0, 1)
    kpos = jnp.arange(S)

    def one_block(args):
        i, qi, ci = args
        return fox_attend(qi, k, v, ci, cum, i * BLOCK + jnp.arange(BLOCK), kpos)

    o = lax.map(one_block, (jnp.arange(nb), qb, cb))
    return jnp.swapaxes(o, 0, 1).reshape(B, S, H, D)

def dilated_branch_prompt(q, k, v, bias, dil):
    B, S, H, D = q.shape
    nk = bias.shape[0] - 1
    unit = dil * BLOCK
    s_pad = -(-S // unit) * unit
    L = s_pad // dil
    nb = L // BLOCK

    def strided(x):
        x = jnp.pad(x, ((0, 0), (0, s_pad - S), (0, 0), (0, 0)))
        x = jnp.swapaxes(x.reshape(B, L, dil, H, D), 1, 2)
        return x.reshape(B, dil, nb, BLOCK, H, D)

    def with_prev(x):
        prev = jnp.pad(x, ((0, 0), (0, 0), (1, 0), (0, 0), (0, 0), (0, 0)))[:, :, :-1]
        return jnp.concatenate([prev, x], axis=3)

    qs = strided(q)
    ks = with_prev(strided(k))
    vs = with_prev(strided(v))
    s = jnp.einsum('brnqhd,brnkhd->brnhqk', qs, ks).astype(jnp.float32) * ATTN_SCALE
    delta = jnp.arange(BLOCK)[:, None] + BLOCK - jnp.arange(2 * BLOCK)[None, :]
    band = (delta >= 0) & (delta <= nk)
    exists = (jnp.arange(nb)[:, None] > 0) | (jnp.arange(2 * BLOCK)[None, :] >= BLOCK)
    valid = band[None] & exists[:, None, :]
    b = bias[jnp.clip(delta, 0, nk)].astype(jnp.float32)
    s = s + jnp.transpose(b, (2, 0, 1))
    s = jnp.where(valid[:, None], s, -jnp.inf)
    lse = jax.nn.logsumexp(s, axis=-1)
    p = jnp.exp(s - lse[..., None])
    o = jnp.einsum('brnhqk,brnkhd->brnqhd', p.astype(v.dtype), vs)
    o = jnp.swapaxes(o.reshape(B, dil, L, H, D), 1, 2).reshape(B, s_pad, H, D)[:, :S]
    lse = jnp.swapaxes(lse, -1, -2).reshape(B, dil, L, H)
    lse = jnp.swapaxes(lse, 1, 2).reshape(B, s_pad, H)[:, :S]
    return o, lse

def dilated_branch_sample(q, kx, vx, bias, dil, q_idx):
    nk = bias.shape[0] - 1
    idx = q_idx[:, None] - dil * jnp.arange(nk + 1)[None, :]
    valid = idx >= 0
    idx = jnp.maximum(idx, 0)
    kg = kx[:, idx]
    vg = vx[:, idx]
    s = jnp.einsum('bqhd,bqjhd->bhqj', q, kg).astype(jnp.float32) * ATTN_SCALE
    s = s + bias.astype(jnp.float32).T[:, None, :]
    s = jnp.where(valid[None, None], s, -jnp.inf)
    lse = jax.nn.logsumexp(s, axis=-1)
    p = jnp.exp(s - lse[..., None])
    o = jnp.einsum('bhqj,bqjhd->bqhd', p.astype(vx.dtype), vg)
    return o, jnp.swapaxes(lse, 1, 2)

def combine_dilations(outs, lses):
    w = jax.nn.softmax(jnp.stack(lses).astype(jnp.float32), axis=0)
    return jnp.einsum('pbsh,pbshd->bshd', w, jnp.stack(outs).astype(jnp.float32))

def mix_prompt(h, w_in, b_forget, qn_fox, kn_fox, qn_dil, kn_dil, rel_bias):
    B, S, _ = h.shape
    qa, ka, va, logf, qb, kb, vb = project_mix(h, w_in, b_forget, qn_fox, kn_fox, qn_dil, kn_dil)
    cum = jnp.cumsum(logf, axis=1)
    oa = fox_prompt(qa, ka, va, cum)
    outs, lses = [], []
    for window, dil in DILATED_PATTERNS:
        o, l = dilated_branch_prompt(qb, kb, vb, dilation_bias(rel_bias, window, dil), dil)
        outs.append(o)
        lses.append(l)
    ob = combine_dilations(outs, lses)
    heads = jnp.concatenate([oa.reshape(B, S, W_FOX).astype(h.dtype), ob.reshape(B, S, W_DIL).astype(h.dtype)], axis=-1)
    win = min(MAX_WINDOW, S)
    return heads, (ka, va, logf, kb[:, S - win:], vb[:, S - win:])

def mix_sample(h, cache_k, cache_v, cache_lf, win_k, win_v, page_table,
               w_in, b_forget, qn_fox, kn_fox, qn_dil, kn_dil, rel_bias):
    B, S, _ = h.shape
    qa, ka, va, logf, qb, kb, vb = project_mix(h, w_in, b_forget, qn_fox, kn_fox, qn_dil, kn_dil)

    def gather(pool):
        g = pool[page_table]
        return g.reshape((B, g.shape[1] * g.shape[2]) + pool.shape[2:])

    k_all = jnp.concatenate([gather(cache_k).astype(ka.dtype), ka], axis=1)
    v_all = jnp.concatenate([gather(cache_v).astype(va.dtype), va], axis=1)
    lf_all = jnp.concatenate([gather(cache_lf).astype(jnp.float32), logf], axis=1)
    cum = jnp.cumsum(lf_all, axis=1)
    past = k_all.shape[1] - S
    oa = fox_attend(qa, k_all, v_all, cum[:, past:], cum, past + jnp.arange(S), jnp.arange(past + S))
    kx = jnp.concatenate([win_k.astype(kb.dtype), kb], axis=1)
    vx = jnp.concatenate([win_v.astype(vb.dtype), vb], axis=1)
    q_idx = win_k.shape[1] + jnp.arange(S)
    outs, lses = [], []
    for window, dil in DILATED_PATTERNS:
        o, l = dilated_branch_sample(qb, kx, vx, dilation_bias(rel_bias, window, dil), dil, q_idx)
        outs.append(o)
        lses.append(l)
    ob = combine_dilations(outs, lses)
    heads = jnp.concatenate([oa.reshape(B, S, W_FOX).astype(h.dtype), ob.reshape(B, S, W_DIL).astype(h.dtype)], axis=-1)
    return heads, (ka, va, logf, kb, vb)

def run_layer(x, c, mixer, w_ada, b_ada, g_ffn1, w1_ffn1, w3_ffn1, w2_ffn1, g_mix, w_out,
              g_ffn2, w1_ffn2, w3_ffn2, w2_ffn2):
    sh1, sc1, gt1, sh2, sc2, gt2, sh3, sc3, gt3 = adaln_params(c, w_ada, b_ada)
    x = x + MACARON * gt1 * swiglu(modulate(x, g_ffn1, sh1, sc1), w1_ffn1, w3_ffn1, w2_ffn1)
    heads, state = mixer(modulate(x, g_mix, sh2, sc2))
    x = x + gt2 * (heads @ w_out)
    x = x + MACARON * gt3 * swiglu(modulate(x, g_ffn2, sh3, sc3), w1_ffn2, w3_ffn2, w2_ffn2)
    return x, state

def setup_inputs(seed: int = 0) -> dict:
    key = jax.random.key(seed)
    ks = list(jax.random.split(key, 32))

    def nrm(i, shape, scale):
        return scale * jax.random.normal(ks[i], shape, jnp.float32)

    n_pages = PAST_LEN // PAGE_SIZE
    n_used = DEC_BATCH * n_pages
    n_pool = n_used + (n_used + 3) // 4
    win_buf = min(MAX_WINDOW, PAST_LEN)
    page_table = jax.random.permutation(ks[0], n_pool)[:n_used].reshape(DEC_BATCH, n_pages).astype(jnp.int32)
    L = DEPTH
    return {
        'x_prompt': nrm(1, (BATCH, SEQ, D_MODEL), 1.0),
        'x_sample': nrm(2, (DEC_BATCH, DEC_SEQ, D_MODEL), 1.0),
        'cache_fox_k': nrm(3, (L, n_pool, PAGE_SIZE, H_FOX, HEAD_DIM), 1.0),
        'cache_fox_v': nrm(4, (L, n_pool, PAGE_SIZE, H_FOX, HEAD_DIM), 1.0),
        'cache_fox_logf': jax.nn.log_sigmoid(FORGET_BIAS + nrm(5, (L, n_pool, PAGE_SIZE, H_FOX), 1.0)),
        'cache_win_k': nrm(6, (L, DEC_BATCH, win_buf, H_DIL, HEAD_DIM), 1.0),
        'cache_win_v': nrm(7, (L, DEC_BATCH, win_buf, H_DIL, HEAD_DIM), 1.0),
        'page_table': page_table,
        'c_prompt': nrm(8, (BATCH, D_MODEL), 1.0),
        'c_sample': nrm(9, (DEC_BATCH, D_MODEL), 1.0),
        'w_ada': nrm(10, (L, D_MODEL, 3 * N_SUBLAYERS * D_MODEL), 0.5 * D_MODEL ** -0.5),
        'b_ada': nrm(11, (L, 3 * N_SUBLAYERS * D_MODEL), 0.02),
        'g_ffn1': 1.0 + nrm(12, (L, D_MODEL), 0.02),
        'w1_ffn1': nrm(13, (L, D_MODEL, D_FF), D_MODEL ** -0.5),
        'w3_ffn1': nrm(14, (L, D_MODEL, D_FF), D_MODEL ** -0.5),
        'w2_ffn1': nrm(15, (L, D_FF, D_MODEL), D_FF ** -0.5),
        'g_mix': 1.0 + nrm(16, (L, D_MODEL), 0.02),
        'w_in': nrm(17, (L, D_MODEL, D_IN), D_MODEL ** -0.5),
        'b_forget': FORGET_BIAS + nrm(18, (L, H_FOX), 0.1),
        'qn_fox': 1.0 + nrm(19, (L, HEAD_DIM), 0.02),
        'kn_fox': 1.0 + nrm(20, (L, HEAD_DIM), 0.02),
        'qn_dil': 1.0 + nrm(21, (L, HEAD_DIM), 0.02),
        'kn_dil': 1.0 + nrm(22, (L, HEAD_DIM), 0.02),
        'rel_bias': nrm(23, (NUM_BUCKETS, H_DIL), 0.5),
        'w_out': nrm(24, (L, D_MODEL, D_MODEL), D_MODEL ** -0.5),
        'g_ffn2': 1.0 + nrm(25, (L, D_MODEL), 0.02),
        'w1_ffn2': nrm(26, (L, D_MODEL, D_FF), D_MODEL ** -0.5),
        'w3_ffn2': nrm(27, (L, D_MODEL, D_FF), D_MODEL ** -0.5),
        'w2_ffn2': nrm(28, (L, D_FF, D_MODEL), D_FF ** -0.5),
    }

def reference(x_prompt, x_sample, cache_fox_k, cache_fox_v, cache_fox_logf, cache_win_k, cache_win_v,
              page_table, c_prompt, c_sample, w_ada, b_ada, g_ffn1, w1_ffn1, w3_ffn1, w2_ffn1, g_mix,
              w_in, b_forget, qn_fox, kn_fox, qn_dil, kn_dil, rel_bias, w_out, g_ffn2, w1_ffn2,
              w3_ffn2, w2_ffn2):
    yp, ys = x_prompt, x_sample
    prompt_states, sample_states = [], []
    for l in range(DEPTH):
        shared = (w_ada[l], b_ada[l], g_ffn1[l], w1_ffn1[l], w3_ffn1[l], w2_ffn1[l], g_mix[l], w_out[l],
                  g_ffn2[l], w1_ffn2[l], w3_ffn2[l], w2_ffn2[l])
        proj = (w_in[l], b_forget[l], qn_fox[l], kn_fox[l], qn_dil[l], kn_dil[l], rel_bias)
        yp, stp = run_layer(yp, c_prompt, lambda h: mix_prompt(h, *proj), *shared)
        ys, sts = run_layer(ys, c_sample,
                            lambda h: mix_sample(h, cache_fox_k[l], cache_fox_v[l], cache_fox_logf[l],
                                                 cache_win_k[l], cache_win_v[l], page_table, *proj),
                            *shared)
        prompt_states.append(stp)
        sample_states.append(sts)

    def stack(states, i):
        return jnp.stack([s[i] for s in states])

    fox_k_p, fox_v_p, fox_lf_p = stack(prompt_states, 0), stack(prompt_states, 1), stack(prompt_states, 2)
    win_k_p, win_v_p = stack(prompt_states, 3), stack(prompt_states, 4)
    fox_k_s, fox_v_s, fox_lf_s = stack(sample_states, 0), stack(sample_states, 1), stack(sample_states, 2)
    win_k_s, win_v_s = stack(sample_states, 3), stack(sample_states, 4)
    return (yp, ys, fox_k_p, fox_v_p, fox_lf_p, win_k_p, win_v_p, fox_k_s, fox_v_s, fox_lf_s, win_k_s, win_v_s)


_drawn_inputs = setup_inputs


def setup_inputs(seed=0):
    import zlib

    import numpy as np

    out = dict(_drawn_inputs(seed))
    spreads = {}
    factors = {'cache_fox_logf': 25.39,
     'cache_win_k': 2.955,
     'g_ffn1': 8.0,
     'g_mix': 3.014,
     'qn_fox': 60.548,
     'kn_fox': 8.598,
     'qn_dil': 48.009,
     'kn_dil': 10.915,
     'rel_bias': 21.84,
     'g_ffn2': 22.288,
     'cache_fox_v': 2.752}
    for name, (base, spread) in spreads.items():
        noise = np.random.default_rng([zlib.crc32(name.encode()), seed]).standard_normal(out[name].shape)
        drawn = base * np.exp(spread * noise) if base else spread * noise
        out[name] = __import__('jax').numpy.asarray(drawn.astype(out[name].dtype))
    for name, factor in factors.items():
        out[name] = (out[name] * factor).astype(out[name].dtype)
    return out
```

```python
from contextlib import ExitStack

import numpy as np

import concourse.bass as bass
from concourse import mybir

F32 = mybir.dt.float32
F32R = mybir.dt.float32r
I32 = mybir.dt.int32
ALU = mybir.AluOpType
ACT = mybir.ActivationFunctionType
AX = mybir.AxisListType

P = 128
D = 2048
KT = D // P
HEADS, HD = 8, 128
TP, NB, NS = 256, 8, 4
TS = NB * NS
T = TP + TS
FF = 43
CHUNKS = ((0, 15), (15, 14), (29, 14))
NPAR = 9
ADA = NPAR * KT
NC = NB + 1
PAGE, PAGES = 128, 8
POOL = 80
WT = 5
GB = 4
EPS = 1e-6
SCALE = HD ** -0.5
NEG = -1.0e30
SQR, SQL = KT // 4, 4
SHIFT, SCL, GATE = 0, 1, 2

C_ID, C_ONE, C_SEL, C_SMALL = 0, 128, 256, 272
W_MAIN = WT * P
C_BAND = 0
C_BUCKET = C_BAND + PAGES * PAGE
C_LOGN = C_BUCKET + W_MAIN + TS
C_NEW_DIL = C_LOGN + W_MAIN
C_NEW_FOX = C_NEW_DIL + 2 * TS
C_CAUSAL = C_NEW_FOX + 2 * TS
C_NEGTRI = C_CAUSAL + 2 * P
C_DELTA = C_NEGTRI + 2 * P
C_NTRI = C_DELTA + NS
C_BIG = C_NTRI + TS
REV = 383
GROUPS = NB // GB


class Seg:

    def __init__(self, kind, bodies, src, f=0, c=0, nk=KT, ada=False, moving="h", gate=None, ff0=0, d0=0,
                 k0=0, z0=0):
        self.kind, self.bodies, self.src = kind, bodies, src
        self.f, self.c, self.nk, self.ada = f, c, nk, ada
        self.moving, self.gate = moving, gate
        self.ff0, self.d0, self.k0, self.z0 = ff0, d0, k0, z0


def plan():
    segs = []

    def ffn(f):
        for c, (t0, n) in enumerate(CHUNKS):
            segs.append(Seg("up", n, f=f, c=c, ff0=t0, ada=f == 0, src=("w13", f)))
            runs = [(0, 8, False)] if f or c == 2 else [(0, 8, True)] if c == 0 else [(0, 5, True), (5, 3, False)]
            for b, m, ada in runs:
                segs.append(Seg("down", m, f=f, c=c, nk=n, moving="g", ada=ada, d0=2 * b, k0=t0,
                                gate=2 if f == 0 else 8, src=("w2", f)))

    ffn(0)
    segs.append(Seg("fa", 0, src=("w_in", 0)))
    segs.append(Seg("win", 16, src=("w_in", 0), z0=0))
    segs.append(Seg("win", 8, src=("w_in", 0), z0=32))
    segs.append(Seg("down", 8, f=0, gate=5, src=("w_out", 0), k0=0))
    ffn(1)
    slot = body = ra = rb = pair = ups = 0
    for s in segs:
        s.n0, s.b0, s.ra, s.rb, s.pair0, s.up0 = slot, body, ra, rb, pair, ups
        slot += 2 * s.bodies + (s.kind == "fa")
        body += s.bodies
        ra += s.bodies
        rb += s.bodies
        pair += s.bodies if s.ada else 0
        ups += s.bodies if s.kind == "up" else 0
    assert 2 * pair == ADA - 2 * KT
    return segs


class Chain:

    def __init__(self, eng, sem):
        self.eng, self.sem, self.n, self.i, self.per = eng, sem, 0, None, 0

    def link(self, ins):
        ins.then_inc(self.sem, 1)
        self.n += 1
        self.eng.wait_ge(self.sem, self.n if self.i is None else self.n + self.i * self.per)

    def loop(self, i, first, per):
        self.i, self.per, self.first, self.start = i, per, first, self.n
        self.n = self.start - first * per if not isinstance(i, int) else self.n
        return self

    def end(self, last):
        assert self.n - (self.start - self.first * self.per) == self.per, (self.n, self.start, self.per)
        self.n = self.start + self.per * (last - self.first)
        self.i = None


def decoder_layer(nc, xT, cT, gT, bada, nwT, bfg, relb, pt, cst, cst2, ohrev, addrev, selh,
                  w_ada, w13_1, w2_1, w_in, w_out, w13_2, w2_2, kpool, vpool, lfpool, wink, winv,
                  y_out, kv_out, lf_out):
    segs = plan()
    ffn1 = [s for s in segs if s.kind in ("up", "down") and s.b0 < 67]
    WS = {("w13", 0): w13_1, ("w13", 1): w13_2, ("w2", 0): w2_1, ("w2", 1): w2_2,
          ("w_in", 0): w_in, ("w_out", 0): w_out}

    with ExitStack() as ctx:
        base = 16512
        top = [base]

        def at(name, shape, dt, off):
            return nc.alloc_sbuf_tensor_at(name, shape, dt, offset=off)

        def sb(name, shape, dt=F32):
            n = int(np.prod(shape[1:])) * 4
            t = at(name, shape, dt, top[0])
            top[0] += -(-n // 32) * 32
            return t

        def sem(name):
            return ctx.enter_context(nc.semaphore(name))

        x = sb("x", [P, KT, T])
        h_hi, h_lo = sb("h_hi", [P, KT, T], F32R), sb("h_lo", [P, KT, T], F32R)
        par = sb("par", [P, ADA * NC])
        sc32 = sb("sc32", [P, KT, 32])
        cs = sb("cs", [P, C_SMALL])
        gv = sb("gv", [P, 3, KT])
        ba = sb("ba", [P, ADA])
        nw4 = sb("nw4", [P, 4])
        nw = sb("nw", [P, 32])
        eps = sb("eps", [P, 1])
        ident, ones, sel9 = cs[:, C_ID:C_ID + P], cs[:, C_ONE:C_ONE + P], cs[:, C_SEL:C_SEL + NC]
        rings0 = top[0]
        raw = sb("raw", [P, 2, KT * P])
        w_hi, w_lo = sb("w_hi", [P, 2, KT * P], F32R), sb("w_lo", [P, 2, KT * P], F32R)
        mix0 = top[0]
        g_hi, g_lo = sb("g_hi", [P, 15, T], F32R), sb("g_lo", [P, 15, T], F32R)
        adaw = sb("adaw", [P, 2, KT * P])
        part_sb = sb("part_sb", [P, 4 * P])
        su, gf = sb("su", [P, T]), sb("gf", [P, T])
        hf = sb("hf", [P, 2, SQL, T])
        sq = sb("sq", [P, 2, SQL, T])
        tmps = sb("tmps", [P, 2, NB, NS])
        sq0 = top[0] - 2 * SQL * T * 4 - 2 * TS * 4
        y0, ms, tt = (at(n, [P, T], F32, sq0 + k * T * 4) for k, n in enumerate(("y0", "ms", "tt")))
        rev = at("rev", [HEADS, REV], F32, sq0 + 3 * T * 4)
        fa_sb, fe = at("fa_sb", [HEADS, T], F32, sq0 + T * 4), at("fe", [HEADS, T], F32, sq0 + 2 * T * 4)
        adax = at("adax", [P, 4, KT * P], F32, mix0)
        assert 4 * KT * P * 4 <= 2 * 15 * T * 4
        big = sb("big", [P, C_BIG])
        lfc = sb("lfc", [P, NB * PAGES, HEADS])
        pages = sb("pages", [1, NB * PAGES], I32)
        rbr = sb("rbr", [P, HEADS])
        bias_w = sb("bias_w", [P, P])
        v_new = sb("v_new", [TS, 2 * HEADS * HD])
        vn0 = top[0] - 2 * HEADS * HD * 4
        selw = at("selw", [HEADS, HEADS * P], F32, vn0)
        ohr = at("ohr", [32, REV], F32, vn0 + 4096)
        adr = at("adr", [HEADS, REV], F32, vn0 + 5632)
        z = at("z", [P, 6 * HEADS, T], F32, mix0)
        hf0 = mix0 + 6 * HEADS * T * 4
        assert hf0 <= top[0]
        small = [hf0 + 2 * 2 * SQL * T * 4]
        yh = at("yh", [P, 2, T], F32, hf0)
        mh = at("mh", [P, 2, T], F32, hf0 + 2 * T * 4)
        th = at("th", [P, 2, T], F32, hf0 + 4 * T * 4)
        toe = at("toe", [P, HEADS, 2 * P], F32, hf0)
        pr = at("pr", [P, 2, 3 * P], F32, hf0 + 8192)
        prt = at("prt", [P, 2, 3 * P], F32, hf0 + 8192 + 3072)
        vnat = at("vnat", [P, 2, 2 * P], F32, hf0 + 8192 + 6144)
        qbd = at("qbd", [P, GB, 288], F32, hf0)
        kv = at("kv", [P, 2, GB, HEADS * P], F32, rings0)
        ps = at("ps", [P, 1024 + TS], F32, rings0 + 32768)
        pst = at("pst", [P, 9, P], F32, rings0 + 32768 + 4224)
        lfr = at("lfr", [P, PAGES, P], F32, rings0 + 32768 + 4224 + 4608)
        lfn_w = at("lfn_w", [TS, P], F32, rings0 + 32768 + 4224 + 4608 + 4096)
        assert 32768 + 4224 + 4608 + 4096 + 512 <= 6 * KT * P * 4
        lf = sb("lf", [HEADS, T])
        lft = sb("lft", [P, 3, HEADS])
        ncum = at("ncum", [HEADS, TP], F32, vn0 + 7168)
        bfs = sb("bfs", [HEADS, 1])
        rbs = sb("rbs", [32, HEADS])
        mx, nm, sm, rs = sb("mx", [P, 2]), sb("nm", [P, 2]), sb("sm", [P, 2]), sb("rs", [P, 2])
        pmx, psm = sb("pmx", [P, 2, 2]), sb("psm", [P, 2, 2])
        rev_dram = nc.dram_tensor("rev_dram", [HEADS, P, REV], F32).ap()

        pairs = [ctx.enter_context(nc.psum_tensor(f"banks{i}", [P, 2, 512], F32)) for i in range(4)]
        bank = [pairs[i // 2][:, i % 2, :] for i in range(8)]
        acc_a, acc_b, ada_part, ada_selp, ssb = bank[0], bank[1], bank[2], bank[3], bank[4]
        ss2 = pairs[2]

        names = """ld_small ld_x w_landed0 w_landed1 hi_ready lo_ready w_used acc_a_ready acc_b_ready
            acc_a_read acc_b_read ada_landed0 ada_landed1 adax_landed0 adax_landed1 adax_landed2
            adax_landed3 ada_used ada_sb ada_sel ada_fin c_ready par_ready sq_ready sq_used ss_ready
            y0_ready hf_ready hhi_ready h_ready su_ready g_ready act_chain dve_chain st_done x_done
            ld_att ld_pages lf_landed rev_sum rev_ready rev_stored toe_landed fa_ready fe_ready lf_ready
            hsq_ready hss_ready hy_ready head_ready lft_sum lft_ready ncum_sum ncum_ready
            p_s p_max p_exp p_scaled p_v p_vcopy p_t p_tcopy p_o p_high p_low
            vn_sum vn_ready kv_landed0 kv_landed1 kv_used qbd_ready sc_ready nm_ready exp_ready
            r_ready pt_sum pt_ready o_ready os_ready ot_ready oh_ready ol_ready"""
        S = {n: sem(n) for n in names.split()}
        block = ctx.enter_context(nc.Block())

        def run(seg, eng, body, first=0, chain=None, per=0):
            if first >= seg.bodies:
                return
            with eng.Fori(first, seg.bodies) as i:
                if chain:
                    chain.loop(i, first, per)
                body(i)
            if chain:
                chain.end(seg.bodies)

        KIND = (dict(n=PAGES, q=0, k=8, v=32, new=C_NEW_FOX), dict(n=WT, q=16, k=24, v=40, new=C_NEW_DIL))
        quad0 = (0, GROUPS * 2 * PAGES)
        QUADS = GROUPS * 2 * (PAGES + WT)
        fa = next(s for s in segs if s.kind == "fa")
        out = next(s for s in segs if s.kind == "down" and s.moving == "h")
        ffn2 = segs[segs.index(out) + 1]
        PAIRS = 8 + (ADA - 2 * KT) // 2
        WIN = (("one", 0, 1), ("one", 1, 2), ("loop", 2, 16), ("one", 16, 17), ("one", 17, 18), ("loop", 18, 24))

        def win_bodies(eng, body, chain=None, per=(0, 0), extra=None):
            for n, (how, a, b) in enumerate(WIN):
                if how == "one":
                    body(a, a)
                else:
                    with eng.Fori(a, b) as i:
                        if chain:
                            chain.loop(i, a, per[0] if a < 16 else per[1])
                        body(i, a)
                    if chain:
                        chain.end(b)
                if extra and a == 1:
                    extra()

        def own_rows(c):
            b = bank[3 + c]
            return bass.AP(b.tensor, b.offset + 16 * c, [[1024, P], [P + NS, 4], [32, GB], [1, NS]])

        @block.sync
        def _(sp):
            sp.dma_start(sc32[:, :, 0:NC], cT).then_inc(S["ld_small"], 16)
            sp.dma_start(cs[:, :], cst).then_inc(S["ld_small"], 16)
            sp.dma_start(gv[:, :, :], gT).then_inc(S["ld_small"], 16)
            sp.dma_start(ba[:, :], bada).then_inc(S["ld_small"], 16)
            sp.dma_start(nw4[:, :], nwT).then_inc(S["ld_small"], 16)
            sp.dma_start(bfs[:, :], bfg).then_inc(S["ld_small"], 16)

            def ada_group(i, first):
                for j in range(4):
                    if not first:
                        sp.wait_ge(S["ada_used"], 4 * i + j - 3)
                    sp.dma_start(adax[:, j, :], w_ada[bass.ds(4 * i + j, 1), :, :].rearrange("a p n -> p (a n)"))\
                      .then_inc(S[f"adax_landed{j}"], 16)
            ada_group(0, True)
            sp.dma_start(x[:, :, :], xT).then_inc(S["ld_x"], 16)
            with sp.Fori(1, 2 * KT // 4) as i:
                ada_group(i, False)

            def slot(seg, j, i):
                n, r = seg.n0 + j, (seg.n0 + j) % 2
                if isinstance(i, int) and n + 2 * i < 2:
                    pass
                else:
                    sp.wait_ge(S["lo_ready"], 2 * (n - 1) + 4 * i)
                src = WS[seg.src]
                if seg.kind == "up":
                    ap = src[bass.ds(2 * (seg.ff0 + i) + j, 1), :, :]
                elif seg.kind == "down":
                    ap = src[bass.ds(seg.d0 + 2 * i + j, 1), :, seg.k0 * P:(seg.k0 + seg.nk) * P]
                elif seg.kind == "win":
                    ap = src[bass.ds(1 + seg.z0 + 2 * i + j, 1), :, :]
                else:
                    ap = src[0:1, :, :]
                sp.dma_start(raw[:, r, 0:seg.nk * P], ap.rearrange("a p n -> p (a n)"))\
                  .then_inc(S[f"w_landed{r}"], 16)

            def ada_pair(seg, i):
                for j in range(2):
                    if not (isinstance(i, int) and seg.pair0 + i == 0):
                        sp.wait_ge(S["ada_used"], 2 * KT + 2 * seg.pair0 + j - 1 + 2 * i)
                    sp.dma_start(adaw[:, j, :], w_ada[bass.ds(2 * KT + 2 * seg.pair0 + 2 * i + j, 1), :, :]
                                 .rearrange("a p n -> p (a n)")).then_inc(S[f"ada_landed{j}"], 16)

            def stream(some):
                for seg in some:
                    def body(i, seg=seg):
                        slot(seg, 0, i)
                        if seg.ada:
                            ada_pair(seg, i)
                        slot(seg, 1, i)
                    peel = 1 if seg.b0 == 0 else 0
                    if peel:
                        body(0)
                    run(seg, sp, body, peel)

            def store_heads(n, z0, s_done, v_done):
                sp.wait_ge(s_done, v_done)
                sp.dma_start(kv_out[n], z[:, z0:z0 + HEADS, :]).then_inc(S["st_done"], 16)

            stream(ffn1)
            slot(fa, 0, 0)
            win = segs[segs.index(fa) + 1:segs.index(fa) + 3]
            stream(win)
            store_heads(0, 8, S["head_ready"], 16)
            store_heads(1, 24, S["head_ready"], 16)
            sp.wait_ge(S["rev_stored"], 16)
            sp.dma_start(toe[:, :, :], bass.AP(rev_dram.tensor, P - 1, [[REV - 1, P], [P * REV, HEADS], [1, 2 * P]]))\
              .then_inc(S["toe_landed"], 16)
            store_heads(2, 32, S["acc_b_read"], out.rb)
            store_heads(3, 40, S["acc_b_read"], out.rb)
            sp.wait_ge(S["lf_ready"], 1)
            sp.dma_start(lf_out, lf[:, :]).then_inc(S["st_done"], 16)
            sp.wait_ge(S["ld_pages"], 16)
            sp.wait_ge(S["w_used"], 2 * out.n0)
            for kind in (0, 1):
                n = KIND[kind]["n"]

                def tiles(g, kind=kind, n=n):
                    for v in (0, 1):
                        for p in range(n):
                            m = v * n + p
                            if kind == 0:
                                pg = [sp.value_load(pages[0:1, bass.ds((GB * g + j) * PAGES + p, 1)],
                                                    min_val=0, max_val=POOL - 1) for j in range(GB)]
                            sp.wait_ge(S["kv_used"], quad0[kind] + m + 1 + 2 * n * g)
                            for j in range(GB):
                                if kind == 0:
                                    src = (vpool if v else kpool)[bass.ds(pg[j], 1), :, :]
                                else:
                                    src = (winv if v else wink)[bass.ds(GB * g + j, 1), p, :, :]
                                sp.dma_start(kv[:, m % 2, j, :], src.rearrange("a p n -> p (a n)"))\
                                  .then_inc(S[f"kv_landed{m % 2}"], 16)
                with sp.Fori(0, GROUPS) as g:
                    tiles(g)
            sp.wait_ge(S["ol_ready"], 2 * GROUPS + 1)
            stream([out])
            stream(segs[segs.index(out) + 1:])
            sp.wait_ge(S["x_done"], 1)
            sp.dma_start(y_out, x[:, :, :]).then_inc(S["st_done"], 16)
            sp.wait_ge(S["st_done"], 6 * 16)

        @block.gpsimd
        def _(pool):
            pool.dma_start(pages[:, :], pt).then_inc(S["ld_pages"], 16)
            pool.dma_start(rbs[:, :], relb).then_inc(S["ld_att"], 16)
            pool.dma_start(ohr[:, :], ohrev).then_inc(S["ld_att"], 16)
            pool.dma_start(adr[:, :], addrev).then_inc(S["ld_att"], 16)
            pool.dma_start(selw[:, :], selh).then_inc(S["ld_att"], 16)
            pool.dma_start(big[:, :], cst2).then_inc(S["ld_att"], 16)
            for q in range(NS):
                pool.dma_start(rbr[32 * q:32 * q + 32, :], relb).then_inc(S["ld_att"], 16)
            pool.wait_ge(S["ld_pages"], 16)
            with pool.Fori(0, NB * PAGES) as i:
                pg = pool.value_load(pages[0:1, bass.ds(i, 1)], min_val=0, max_val=POOL - 1)
                pool.dma_start(lfc[:, bass.ds(i, 1), :], lfpool[bass.ds(pg, 1), :, :].rearrange("a p h -> p a h"))\
                    .then_inc(S["lf_landed"], 16)
            pool.wait_ge(S["rev_ready"], 1)
            pool.dma_start(rev_dram, rev[:, :].unsqueeze(1).to_broadcast([HEADS, P, REV])).then_inc(S["rev_stored"], 16)
            pool.wait_ge(S["rev_stored"], 16)

        @block.tensor
        def _(pe):
            def ada_tile(w, col, scoped):
                for kt in range(KT):
                    j = kt % 4
                    last = pe.matmul(ada_part[32 * j:32 * j + 32, col * P:(col + 1) * P], sc32[:, kt, :],
                                     w[:, kt * P:(kt + 1) * P], start=kt < 4, stop=kt >= KT - 4,
                                     tile_position=(0, 32 * j))
                last.then_inc(S["ada_used"], 1)

            def ada_select(group, n):
                pe.wait_ge(S["ada_sb"], group + 1)
                if not (isinstance(group, int) and group == 0):
                    pe.wait_ge(S["ada_fin"], group)
                for c in range(n):
                    last = pe.matmul(ada_selp[:, c * NC:(c + 1) * NC], part_sb[:, c * P:(c + 1) * P], sel9,
                                     start=True, stop=True)
                last.then_inc(S["ada_sel"], 1)

            def square_sum(r):
                for c in range(SQR):
                    pe.wait_ge(S["sq_ready"], SQR * r + c + 1)
                    for k in range(SQL):
                        last = pe.matmul(ssb[:, 0:T], ones, sq[:, c % 2, k, :], start=c == 0 and k == 0,
                                         stop=c == SQR - 1 and k == SQL - 1)
                    last.then_inc(S["sq_used"], 1)

            pe.sem_inc(S["kv_used"], 2)
            pe.wait_ge(S["c_ready"], 1)
            square_sum(0)
            pe.wait_ge(S["ld_att"], 9 * 16)
            pe.matmul(bank[5][0:HEADS, 0:REV], rbs[:, :], ohr[:, :], start=True, stop=True).then_inc(S["rev_sum"], 1)

            def ada_group(i, first):
                if not first:
                    pe.wait_ge(S["ada_sb"], i)
                for j in range(4):
                    pe.wait_ge(S[f"adax_landed{j}"], 16 + 16 * i)
                    ada_tile(adax[:, j, :], j, None)
                ada_select(i, 4)
            ada_group(0, True)
            with pe.Fori(1, 2 * KT // 4) as i:
                ada_group(i, False)

            def tile(seg, j, i, bank, mid=None):
                n, r = seg.n0 + j, (seg.n0 + j) % 2
                m_hi, m_lo = (h_hi, h_lo) if seg.moving == "h" else (g_hi, g_lo)
                half = KT // 2
                for q, (a, b) in enumerate(((0, half), (half, seg.nk))):
                    pe.wait_ge(S["lo_ready"], 2 * n + q + 1 + 4 * i)
                    for k in range(a, b):
                        hi, lo = w_hi[:, r, k * P:(k + 1) * P], w_lo[:, r, k * P:(k + 1) * P]
                        pe.matmul(bank[:, 0:T], hi, m_hi[:, k, :], start=k == 0, stop=False)
                        pe.matmul(bank[:, 0:T], hi, m_lo[:, k, :], start=False, stop=False)
                        last = pe.matmul(bank[:, 0:T], lo, m_hi[:, k, :], start=False, stop=k == seg.nk - 1)
                    if q == 0:
                        last.then_inc(S["w_used"], 1)
                        if mid:
                            mid()
                last.then_inc(S["w_used"], 1)

            def pair(seg, i, mid=None):
                if seg.ada:
                    g = 8 + seg.pair0 + i
                    pe.wait_ge(S["ada_sb"], g)
                    for j in range(2):
                        pe.wait_ge(S[f"ada_landed{j}"], 16 * (seg.pair0 + 1) + 16 * i)
                        ada_tile(adaw[:, j, :], j, None)
                if not (isinstance(i, int) and seg.b0 + i == 0):
                    pe.wait_ge(S["acc_a_read"], seg.ra + i)
                tile(seg, 0, i, acc_a, mid)
                if seg.ada:
                    ada_select(g, 2)
                if not (isinstance(i, int) and seg.b0 + i == 0):
                    pe.wait_ge(S["acc_b_read"], seg.rb + i)
                tile(seg, 1, i, acc_b)

            def segments(some):
                for seg in some:
                    if seg.kind == "down" and seg.moving == "g":
                        pe.wait_ge(S["g_ready"], seg.up0)
                    peel = 1 if seg.b0 == 0 else 0
                    if peel:
                        pair(seg, 0)
                    run(seg, pe, lambda i, seg=seg: pair(seg, i), peel)

            pe.wait_ge(S["h_ready"], SQR)
            segments(ffn1)
            square_sum(1)
            pe.wait_ge(S["h_ready"], 2 * SQR)
            tile(fa, 0, 0, bank[2])

            def head_sums(b):
                pe.wait_ge(S["hsq_ready"], 2 * b + 2)
                if not (isinstance(b, int) and b == 0):
                    pe.wait_ge(S["head_ready"], b)
                for j in range(2):
                    last = pe.matmul(ss2[:, j, 0:T], ones, sq[:, j, 0, :], start=True, stop=True)
                last.then_inc(S["hss_ready"], 1)

            qk, vv = segs[segs.index(fa) + 1:segs.index(fa) + 3]

            def win_body(b, j):
                seg, i = (qk, b) if j < 16 else (vv, b - 16)
                pair(seg, i, (lambda: head_sums(b - 1)) if 1 <= j <= 16 else None)
            win_bodies(pe, win_body)

            def turn(dst, src, done=None):
                return pe.transpose(dst, src, ident[0:src.shape[0], 0:src.shape[0]])

            pe.wait_ge(S["lf_ready"], 1)
            for t in range(2):
                turn(bank[7][:, t * HEADS:(t + 1) * HEADS], lf[:, t * P:(t + 1) * P])
            turn(bank[7][0:TS, 2 * HEADS:3 * HEADS], lf[:, TP:T]).then_inc(S["lft_sum"], 1)
            pe.wait_ge(S["lft_ready"], 1)
            negtri = big[:, C_NEGTRI:C_NEGTRI + 2 * P]
            pe.matmul(bank[6][0:HEADS, 0:TP], lft[:, 0, :], negtri, start=True, stop=False)
            pe.matmul(bank[6][0:HEADS, P:TP], lft[:, 1, :], negtri[:, 0:P], start=False, stop=True)\
              .then_inc(S["ncum_sum"], 1)
            pe.wait_ge(S["head_ready"], 16)
            pe.wait_ge(S["acc_b_read"], out.rb)
            pe.wait_ge(S["ncum_ready"], 1)

            def p_scores(t):
                kd, h = KIND[t // HEADS], t % HEADS
                q, k, s_bank = z[:, kd["q"] + h, :], z[:, kd["k"] + h, :], bank[t % 2]
                if t >= 2:
                    pe.wait_ge(S["p_max"], t - 1)
                for c, (a, n) in enumerate(((0, P), (P, 2 * P))):
                    fox = t < HEADS
                    last = pe.matmul(s_bank[:, a:a + n], q[:, c * P:(c + 1) * P], k[:, 0:n], start=True, stop=not fox)
                    if fox:
                        last = pe.matmul(s_bank[:, a:a + n], selw[:, h * P:(h + 1) * P], ncum[:, 0:n],
                                         start=False, stop=True)
                last.then_inc(S["p_s"], 1)

            def p_values(t):
                v = z[:, KIND[t // HEADS]["v"] + t % HEADS, :]
                if t:
                    pe.wait_ge(S["p_vcopy"], t)
                turn(bank[6][:, 0:P], v[:, 0:P])
                turn(bank[6][:, P:2 * P], v[:, P:2 * P]).then_inc(S["p_v"], 1)

            def p_turn(t):
                pe.wait_ge(S["p_scaled"], t + 1)
                if t >= 2:
                    pe.wait_ge(S["p_tcopy"], t - 1)
                for c in range(3):
                    last = turn(bank[2 + t % 2][:, c * P:(c + 1) * P], pr[:, t % 2, c * P:(c + 1) * P])
                last.then_inc(S["p_t"], 1)

            def p_outputs(t):
                pe.wait_ge(S["p_tcopy"], t + 1)
                pe.wait_ge(S["p_vcopy"], t + 1)
                if t >= 2:
                    pe.wait_ge(S["p_low"], t - 1)
                o = bank[4 + t % 2]
                pe.matmul(o[:, 0:TP], vnat[:, t % 2, 0:P], prt[:, t % 2, 0:2 * P], start=True, stop=False)
                pe.matmul(o[:, P:TP], vnat[:, t % 2, P:2 * P], prt[:, t % 2, 2 * P:3 * P], start=False, stop=True)\
                  .then_inc(S["p_o"], 1)

            for t in range(2 * HEADS + 2):
                if t < 2 * HEADS:
                    p_scores(t)
                    p_values(t)
                if 1 <= t <= 2 * HEADS:
                    p_turn(t - 1)
                if t >= 2:
                    p_outputs(t - 2)

            for c in range(4):
                pe.wait_ge(S["vn_ready"], c) if c else pe.wait_ge(S["p_vcopy"], 2 * HEADS)
                for h in range(4):
                    last = turn(bank[6][0:TS, h * P:(h + 1) * P], z[:, 32 + 4 * c + h, TP:T])
                last.then_inc(S["vn_sum"], 1)

            def group(kind, g):
                kd = KIND[kind]
                n, G = kd["n"], GROUPS * kind + 1
                main, new = pairs[0], bank[2]
                pe.wait_ge(S["qbd_ready"], G + g)
                pe.wait_ge(S["exp_ready"], G + g)
                skip = dict(skip_group_check=True)
                if kind == 0:
                    for p in range(PAGES - 1, -1, -1):
                        b = (PAGES - 1 - p) * PAGE
                        pe.matmul(main[:, 0, 0:min(512, (p + 1) * P)], lfr[:, p, :], big[:, b:b + min(512, (p + 1) * P)],
                                  start=p == PAGES - 1, stop=False, **skip)
                        if p >= 4:
                            pe.matmul(main[:, 1, 0:(p - 3) * P], lfr[:, p, :], big[:, b + 512:b + (p + 1) * P],
                                      start=p == PAGES - 1, stop=False, **skip)
                    pe.matmul(new[:, 0:TS], lfn_w[:, :], big[0:TS, C_NTRI:C_NTRI + TS], start=True, stop=False, **skip)
                else:
                    for dst, a, b in ((main[:, 0, :], 0, 512), (main[:, 1, 0:P], 512, W_MAIN), (new[:, 0:TS], W_MAIN, W_MAIN + TS)):
                        pe.matmul(dst, bias_w[:, :], big[:, C_BUCKET + a:C_BUCKET + b], start=True, stop=False, **skip)

                def scores(dst, moving, last):
                    for h in range(HEADS):
                        for j in range(GB):
                            r = pe.matmul(dst(j), qbd[:, j, 32 * h:32 * h + 32], moving(j, h), start=False,
                                          stop=h == HEADS - 1, tile_position=(0, 32 * j), **skip)
                    return r
                scores(lambda j: new[32 * j:32 * j + 32, 0:TS], lambda j, h: z[:, kd["k"] + h, TP:T], True)

                def landed(m):
                    pe.wait_ge(S[f"kv_landed{m % 2}"], 64 * ((quad0[kind] + m) // 2 + 1) + 64 * n * g)
                for p in range(n):
                    landed(p)
                    scores(lambda j: main[32 * j:32 * j + 32, p // 4, (p % 4) * P:(p % 4 + 1) * P],
                           lambda j, h: kv[:, p % 2, j, h * P:(h + 1) * P], False)\
                        .then_inc(S["kv_used"], 1)
                pe.wait_ge(S["exp_ready"], G + 1 + g)
                pe.wait_ge(S["ol_ready"], G + g)
                for p in range(n):
                    turn(bank[3 + p // 4][:, (p % 4) * P:(p % 4 + 1) * P], ps[:, p * P:(p + 1) * P])
                turn(bank[5][0:TS, 0:P], ps[:, 1024:1024 + TS]).then_inc(S["pt_sum"], 1)
                pe.wait_ge(S["vn_ready"], 4)
                pe.wait_ge(S["pt_ready"], G + g)
                pe.wait_ge(S["os_ready"], G + g)
                o = pairs[3]
                for c in range(2):
                    for j in range(GB):
                        a = (kind * 2 + c) * 512
                        pe.matmul(o[32 * j:32 * j + 32, c, :], pst[0:TS, 8, 32 * j:32 * j + 32], v_new[:, a:a + 512],
                                  start=True, stop=False, tile_position=(0, 32 * j), **skip)
                for p in range(n):
                    landed(n + p)
                    for c in range(2):
                        for j in range(GB):
                            last = pe.matmul(o[32 * j:32 * j + 32, c, :], pst[:, p, 32 * j:32 * j + 32],
                                             kv[:, (n + p) % 2, j, 512 * c:512 * c + 512], start=False,
                                             stop=p == n - 1, tile_position=(0, 32 * j), **skip)
                    last.then_inc(S["kv_used"], 1)
                pe.wait_ge(S["os_ready"], G + 1 + g)
                for h in range(HEADS):
                    last = turn(bank[3 + h // 4][:, (h % 4) * P:(h % 4 + 1) * P], ps[:, h * P:(h + 1) * P])
                last.then_inc(S["ot_ready"], 1)

            pe.wait_ge(S["vn_ready"], 4)
            for kind in (0, 1):
                with pe.Fori(0, GROUPS) as g:
                    group(kind, g)

            pe.wait_ge(S["ol_ready"], 2 * GROUPS + 1)
            segments([out])
            square_sum(2)
            pe.wait_ge(S["h_ready"], 3 * SQR)
            segments(segs[segs.index(out) + 1:])

        @block.scalar
        def _(act):
            ch = Chain(act, S["act_chain"])

            def split_high(seg, j, i):
                n, r = seg.n0 + j, (seg.n0 + j) % 2
                half = KT // 2 * P
                for q, (a, b) in enumerate(((0, half), (half, seg.nk * P))):
                    if q == 0:
                        act.wait_ge(S[f"w_landed{r}"], 16 * (n // 2 + 1) + 16 * i)
                    if not (isinstance(i, int) and n + 2 * i < 2):
                        act.wait_ge(S["w_used"], 2 * (n - 2) + q + 1 + 4 * i)
                    act.activation(w_hi[:, r, a:b], raw[:, r, a:b], ACT.Copy).then_inc(S["hi_ready"], 1)

            def squares(r):
                for c in range(SQR):
                    if SQR * r + c >= 2:
                        act.wait_ge(S["sq_used"], SQR * r + c - 1)
                    act.activation(sq[:, c % 2, :, :], x[:, SQL * c:SQL * (c + 1), :], ACT.Square)\
                       .then_inc(S["sq_ready"], 1)

            def inverse_root(r):
                act.wait_ge(S["sq_used"], SQR * (r + 1))
                ch.link(act.activation(y0[:, :], ssb[:, 0:T], ACT.Ln, bias=eps[:, 0:1], scale=1.0 / D))
                act.activation(y0[:, :], y0[:, :], ACT.Exp, scale=-0.5).then_inc(S["y0_ready"], 1)

            def high_of_h(r):
                for c in range(SQR):
                    act.wait_ge(S["hf_ready"], SQR * r + c + 1)
                    act.activation(h_hi[:, SQL * c:SQL * (c + 1), :], hf[:, c % 2, :, :], ACT.Copy)\
                       .then_inc(S["hhi_ready"], 1)

            def ada_copy(group, n):
                act.wait_ge(S["ada_used"], 4 * (group + 1) if n == 4 else 2 * KT + 2 * (group - 7))
                if not (isinstance(group, int) and group == 0):
                    act.wait_ge(S["ada_sel"], group)
                act.activation(part_sb[:, 0:n * P], ada_part[:, 0:n * P], ACT.Copy).then_inc(S["ada_sb"], 1)

            act.wait_ge(S["ld_small"], 96)
            act.wait_ge(S["dve_chain"], 2)
            act.activation(sc32[:, :, 0:NC], sc32[:, :, 0:NC], ACT.Silu).then_inc(S["c_ready"], 1)
            act.wait_ge(S["ld_x"], 16)
            squares(0)
            inverse_root(0)
            ada_copy(0, 4)
            with act.Fori(1, 2 * KT // 4) as i:
                ada_copy(i, 4)
            high_of_h(0)

            def body(seg, i):
                split_high(seg, 0, i)
                if seg.ada:
                    ada_copy(8 + seg.pair0 + i, 2)
                split_high(seg, 1, i)
                if seg.kind == "up":
                    act.wait_ge(S["w_used"], 2 * (seg.n0 + 1) + 4 * i)
                    if not (isinstance(i, int) and seg.up0 + i == 0):
                        act.wait_ge(S["g_ready"], seg.up0 + i)
                    act.activation(su[:, :], acc_a[:, 0:T], ACT.Silu).then_inc(S["acc_a_read"], 1)

            def segments(some):
                for seg in some:
                    peel = 1 if seg.b0 == 0 else 0
                    if peel:
                        body(seg, 0)
                    run(seg, act, lambda i, seg=seg: body(seg, i), peel)

            segments(ffn1)
            act.wait_ge(S["acc_b_read"], fa.rb)
            act.wait_ge(S["rev_stored"], 16)
            squares(1)
            inverse_root(1)
            high_of_h(1)

            qk, vv = segs[segs.index(fa) + 1:segs.index(fa) + 3]
            split_high(fa, 0, 0)

            def head_square(b, j):
                act.wait_ge(S["acc_b_read" if j else "acc_a_read"], (qk.rb if j else qk.ra) + 1 + b)
                act.activation(sq[:, j, 0:1, :], z[:, bass.ds(2 * b + j, 1), :], ACT.Square).then_inc(S["hsq_ready"], 1)

            def win_body(b, j):
                seg, i = (qk, b) if j < 16 else (vv, b - 16)
                split_high(seg, 0, i)
                if 1 <= j <= 16:
                    head_square(b - 1, 1)
                split_high(seg, 1, i)
                if 1 <= j <= 16:
                    act.wait_ge(S["hss_ready"], b)
                    if j > 1:
                        act.wait_ge(S["head_ready"], b - 1)
                    ch.link(act.activation(yh[:, :, :], ss2[:, :, 0:T], ACT.Ln, bias=eps[:, 0:1], scale=1.0 / HD))
                    act.activation(yh[:, :, :], yh[:, :, :], ACT.Exp, scale=-0.5).then_inc(S["hy_ready"], 1)
                if j < 16:
                    head_square(b, 0)

            def log_forget():
                act.wait_ge(S["fa_ready"], 1)
                ch.link(act.activation(fe[:, :], fa_sb[:, :], ACT.Abs))
                ch.link(act.activation(fe[:, :], fe[:, :], ACT.Exp, scale=-1.0))
                act.activation(fe[:, :], fe[:, :], ACT.Ln, bias=ones[0:HEADS, 0:1]).then_inc(S["fe_ready"], 1)
            win_bodies(act, win_body, ch, (1, 0), log_forget)

            def p_exp(t):
                act.wait_ge(S["p_max"], t + 1)
                for c, (a, n) in enumerate(((0, P), (P, 2 * P))):
                    v = pr[:, t % 2, a:a + n]
                    last = act.activation(v, v, ACT.Exp, bias=pmx[:, t % 2, c:c + 1], accum_out=psm[:, t % 2, c:c + 1])
                last.then_inc(S["p_exp"], 1)

            for t in range(2 * HEADS + 2):
                if t < 2 * HEADS:
                    act.wait_ge(S["p_v"], t + 1)
                    if t >= 2:
                        act.wait_ge(S["p_o"], t - 1)
                    act.activation(vnat[:, t % 2, :], bank[6][:, 0:2 * P], ACT.Copy).then_inc(S["p_vcopy"], 1)
                    p_exp(t)
                if 1 <= t <= 2 * HEADS:
                    act.wait_ge(S["p_t"], t)
                    act.activation(prt[:, (t - 1) % 2, :], bank[2 + (t - 1) % 2][:, 0:3 * P], ACT.Copy)\
                       .then_inc(S["p_tcopy"], 1)
                if t >= 2:
                    act.wait_ge(S["p_o"], t - 1)
                    act.activation(h_hi[:, t - 2, 0:TP], bank[4 + t % 2][:, 0:TP], ACT.Copy).then_inc(S["p_high"], 1)

            for c in range(4):
                act.wait_ge(S["vn_sum"], c + 1)
                act.activation(v_new[:, c * 512:(c + 1) * 512], bank[6][0:TS, :], ACT.Copy).then_inc(S["vn_ready"], 1)
            act.sem_inc(S["exp_ready"], 1)
            act.sem_inc(S["os_ready"], 1)

            def group(kind, g):
                kd = KIND[kind]
                n, G = kd["n"], GROUPS * kind + 1
                act.wait_ge(S["nm_ready"], G + g)
                if kind == 0:
                    dst = ps[:, 0:1024].rearrange("p (a b) -> p a b", a=2)
                    act.activation(dst, pairs[0][:, :, :], ACT.Exp, bias=nm[:, 0:1], accum_out=sm[:, 0:1])
                else:
                    act.activation(ps[:, 0:W_MAIN], ps[:, 0:W_MAIN], ACT.Exp, bias=nm[:, 0:1], accum_out=sm[:, 0:1])
                act.activation(ps[:, 1024:1024 + TS], ps[:, 1024:1024 + TS], ACT.Exp, bias=nm[:, 0:1],
                               accum_out=sm[:, 1:2]).then_inc(S["exp_ready"], 1)
                act.wait_ge(S["pt_sum"], G + g)
                act.activation(pst[:, 0:4, :].rearrange("p a b -> p (a b)"), bank[3], ACT.Copy)
                act.activation(pst[:, 4:n, :].rearrange("p a b -> p (a b)"), bank[4][:, 0:(n - 4) * P], ACT.Copy)
                act.activation(pst[0:TS, 8, :], bank[5][0:TS, 0:P], ACT.Copy).then_inc(S["pt_ready"], 1)
                act.wait_ge(S["kv_used"], quad0[kind] + 2 + 2 * n + 2 * n * g)
                act.wait_ge(S["r_ready"], G + g)
                act.activation(ps[:, 0:1024].rearrange("p (a b) -> p a b", a=2), pairs[3][:, :, :], ACT.Copy,
                               scale=rs[:, 0:1]).then_inc(S["os_ready"], 1)
                act.wait_ge(S["ot_ready"], G + g)
                for c in range(2):
                    dst = h_hi[:, kind * HEADS + 4 * c:kind * HEADS + 4 * c + 4, bass.ds(TP + 16 * g, 16)]
                    last = act.activation(dst.rearrange("p h (j s) -> p h j s", s=NS), own_rows(c), ACT.Copy)
                last.then_inc(S["oh_ready"], 1)

            for kind in (0, 1):
                with act.Fori(0, GROUPS) as g:
                    group(kind, g)

            act.wait_ge(S["ol_ready"], 2 * GROUPS + 1)
            segments([out])
            act.wait_ge(S["acc_b_read"], ffn2.rb)
            squares(2)
            inverse_root(2)
            high_of_h(2)
            segments(segs[segs.index(out) + 1:])

        @block.vector
        def _(dve):
            ch = Chain(dve, S["dve_chain"])
            par3 = par[:, :].rearrange("p (t c) -> p t c", c=NC)

            def split_low(seg, j, i):
                n, r = seg.n0 + j, (seg.n0 + j) % 2
                half = KT // 2 * P
                for q, (a, b) in enumerate(((0, half), (half, seg.nk * P))):
                    dve.wait_ge(S["hi_ready"], 2 * n + q + 1 + 4 * i)
                    dve.tensor_tensor(w_lo[:, r, a:b], raw[:, r, a:b], w_hi[:, r, a:b].bitcast(F32),
                                      ALU.subtract).then_inc(S["lo_ready"], 1)

            def refine(ssum, y, m, t, scale):
                ch.link(dve.tensor_scalar(m, ssum, scale, EPS, ALU.mult, ALU.add))
                ch.link(dve.tensor_tensor(t, y, y, ALU.mult))
                ch.link(dve.scalar_tensor_tensor(t, t, -0.5, m, ALU.mult, ALU.mult))
                ch.link(dve.scalar_tensor_tensor(y, t, 1.5, y, ALU.add, ALU.mult))

            def samples(ap):
                return ap.rearrange("p k (b s) -> p k b s", s=NS)

            def modulate(r):
                dve.wait_ge(S["y0_ready"], r + 1)
                refine(ssb[:, 0:T], y0[:, :], ms[:, :], tt[:, :], 1.0 / D)
                sh, a = 3 * r * KT, (3 * r + 1) * KT

                def low(c):
                    dve.wait_ge(S["hhi_ready"], SQR * r + c + 1)
                    dve.tensor_tensor(h_lo[:, SQL * c:SQL * (c + 1), :], hf[:, c % 2, :, :],
                                      h_hi[:, SQL * c:SQL * (c + 1), :].bitcast(F32), ALU.subtract)\
                       .then_inc(S["h_ready"], 1)
                for c in range(SQR):
                    k0 = SQL * c
                    if c >= 2:
                        dve.wait_ge(S["h_ready"], SQR * r + c - 1)
                    ch.link(dve.tensor_tensor(hf[:, c % 2, :, :], x[:, k0:k0 + SQL, :],
                                              y0[:, :].unsqueeze(1).to_broadcast([P, SQL, T]), ALU.mult))
                    hs = samples(hf[:, c % 2, :, TP:T])
                    for k in range(SQL):
                        q = hf[:, c % 2, k, 0:TP]
                        last = dve.tensor_scalar(q, q, par[:, (a + k0 + k) * NC:(a + k0 + k) * NC + 1],
                                                 par[:, (sh + k0 + k) * NC:(sh + k0 + k) * NC + 1],
                                                 ALU.mult, ALU.add)
                    ch.link(dve.tensor_tensor(hs, hs, par3[:, a + k0:a + k0 + SQL, 1:NC].unsqueeze(3)
                                              .to_broadcast([P, SQL, NB, NS]), ALU.mult))
                    dve.tensor_tensor(hs, hs, par3[:, sh + k0:sh + k0 + SQL, 1:NC].unsqueeze(3)
                                      .to_broadcast([P, SQL, NB, NS]), ALU.add).then_inc(S["hf_ready"], 1)
                    if c:
                        low(c - 1)
                low(SQR - 1)

            def ada_finish(group, t0, n):
                dve.wait_ge(S["ada_sel"], group + 1)
                dve.tensor_tensor(par3[:, bass.ds(t0, n), :],
                                  ada_selp[:, 0:n * NC].rearrange("p (t c) -> p t c", c=NC),
                                  ba[:, bass.ds(t0, n)].unsqueeze(2).to_broadcast([P, n, NC]), ALU.add)\
                   .then_inc(S["ada_fin"], 1)

            def gain(r, groups):
                dve.wait_ge(S["ada_fin"], groups)
                a = par3[:, (3 * r + 1) * KT:(3 * r + 2) * KT, :]
                ch.link(dve.scalar_tensor_tensor(a, a, 1.0, gv[:, r, :].unsqueeze(2).to_broadcast([P, KT, NC]),
                                                 ALU.add, ALU.mult))

            def half_gate(p, groups):
                dve.wait_ge(S["ada_fin"], groups)
                a = par[:, p * KT * NC:(p + 1) * KT * NC]
                ch.link(dve.tensor_scalar(a, a, 0.5, None, ALU.mult))

            ch.link(dve.memset(sc32[:, :, NC:32], 0.0))
            ch.link(dve.memset(eps[:, :], EPS))
            dve.wait_ge(S["ld_small"], 96)
            ada_finish(0, 0, 4)
            with dve.Fori(1, 2 * KT // 4) as i:
                ada_finish(i, 4 * i, 4)
            gain(0, 8)
            modulate(0)
            for k in range(4):
                dve.tensor_scalar(nw[:, 8 * k:8 * k + 8], nw4[:, k:k + 1].to_broadcast([P, 8]), SCALE if k % 2 == 0 else 1.0,
                                  None, ALU.mult)
            dve.wait_ge(S["rev_sum"], 1)
            dve.tensor_tensor(rev[:, :], bank[5][0:HEADS, 0:REV], adr[:, :], ALU.add).then_inc(S["rev_ready"], 1)
            ch.link(dve.tensor_tensor(bias_w[:, :].rearrange("p (j h q) -> p j h q", j=GB, q=NS),
                                      rbr[:, :].unsqueeze(1).unsqueeze(3).to_broadcast([P, GB, HEADS, NS]),
                                      big[:, C_DELTA:C_DELTA + NS].unsqueeze(1).unsqueeze(1)
                                      .to_broadcast([P, GB, HEADS, NS]), ALU.mult))

            def add_gated(seg, j, i):
                bank = (acc_a, acc_b)[j]
                n = seg.n0 + j
                dve.wait_ge(S["w_used"], 2 * (n + 1) + 4 * i)
                d = seg.d0 + j + 2 * i
                gate = seg.gate * KT + d
                xs = x[:, bass.ds(d, 1), TP:T].rearrange("p k (b s) -> p (k b) s", s=NS)
                xp = x[:, bass.ds(d, 1), 0:TP].rearrange("p k t -> p (k t)")
                ch.link(dve.tensor_tensor(tmps[:, j, :, :], bank[:, TP:T].rearrange("p (b s) -> p b s", s=NS),
                                          par[:, bass.ds(gate * NC + 1, NB)].unsqueeze(2).to_broadcast([P, NB, NS]),
                                          ALU.mult))
                ch.link(dve.tensor_tensor(xs, xs, tmps[:, j, :, :], ALU.add))
                dve.scalar_tensor_tensor(xp, bank[:, 0:TP], par[:, bass.ds(gate * NC, 1)], xp,
                                         ALU.mult, ALU.add).then_inc(S["acc_b_read" if j else "acc_a_read"], 1)

            def gated_unit(seg, i):
                dve.wait_ge(S["w_used"], 2 * (seg.n0 + 2) + 4 * i)
                dve.wait_ge(S["acc_a_read"], seg.ra + 1 + i)
                dve.tensor_tensor(gf[:, :], su[:, :], acc_b[:, 0:T], ALU.mult).then_inc(S["acc_b_read"], 1)
                dve.wait_ge(S["acc_b_read"], seg.rb + 1 + i)
                gh, gl = g_hi[:, bass.ds(i, 1), :], g_lo[:, bass.ds(i, 1), :]
                gg = gf[:, :].unsqueeze(1)
                ch.link(dve.tensor_copy(gh, gg))
                dve.tensor_tensor(gl, gg, gh.bitcast(F32), ALU.subtract).then_inc(S["g_ready"], 1)

            def after_b(seg, i):
                if seg.kind == "up":
                    gated_unit(seg, i)
                elif seg.kind == "down":
                    add_gated(seg, 1, i)

            LINKS = {"up": 1, "down": 4}

            def body(seg, i, lag):
                split_low(seg, 0, i)
                if lag:
                    after_b(seg, i - 1)
                split_low(seg, 1, i)
                if seg.ada:
                    ada_finish(8 + seg.pair0 + i, 2 * KT + 2 * seg.pair0 + 2 * i, 2)
                if seg.kind == "down":
                    add_gated(seg, 0, i)

            def segments(some):
                for seg in some:
                    if seg.gate == 2 and seg.b0 == CHUNKS[0][1]:
                        half_gate(2, 8 + 8)
                    body(seg, 0, False)
                    run(seg, dve, lambda i, seg=seg: body(seg, i, True), 1, ch, LINKS[seg.kind])
                    after_b(seg, seg.bodies - 1)

            segments(ffn1)
            gain(1, PAIRS)
            modulate(1)

            qk, vv = segs[segs.index(fa) + 1:segs.index(fa) + 3]
            split_low(fa, 0, 0)

            def z_copy(b, j):
                dve.wait_ge(S["w_used"], 2 * (qk.n0 + j + 1) + 4 * b)
                dve.tensor_copy(z[:, bass.ds(2 * b + j, 1), :], (acc_a, acc_b)[j][:, 0:T].unsqueeze(1))\
                   .then_inc(S["acc_b_read" if j else "acc_a_read"], 1)

            def head_norm(b):
                dve.wait_ge(S["hy_ready"], b + 1)
                refine(ss2[:, :, 0:T], yh[:, :, :], mh[:, :, :], th[:, :, :], 1.0 / HD)
                for j in range(2):
                    zt = z[:, bass.ds(2 * b + j, 1), :]
                    last = dve.scalar_tensor_tensor(zt, zt, nw[:, bass.ds(2 * b + j, 1)], yh[:, j, :].unsqueeze(1),
                                                    ALU.mult, ALU.mult)
                last.then_inc(S["head_ready"], 1)

            def win_body(b, j):
                seg, i = (qk, b) if j < 16 else (vv, b - 16)
                split_low(seg, 0, i)
                if 2 <= j <= 17:
                    head_norm(b - 2)
                if j >= 1:
                    z_copy(b - 1, 1)
                split_low(seg, 1, i)
                z_copy(b, 0)

            def gate_sum():
                dve.wait_ge(S["w_used"], 2 * (fa.n0 + 1))
                dve.tensor_scalar(fa_sb[:, :], bank[2][0:HEADS, 0:T], bfs[:, 0:1], None, ALU.add)\
                   .then_inc(S["fa_ready"], 1)
            win_bodies(dve, win_body, ch, (4, 0), gate_sum)
            z_copy(23, 1)
            dve.wait_ge(S["fe_ready"], 1)
            dve.scalar_tensor_tensor(lf[:, :], fa_sb[:, :], 0.0, fe[:, :], ALU.min, ALU.subtract)\
               .then_inc(S["lf_ready"], 1)
            dve.wait_ge(S["lft_sum"], 1)
            dve.tensor_copy(lft[:, 0:2, :], bank[7][:, 0:2 * HEADS].rearrange("p (t h) -> p t h", t=2))
            ch.link(dve.tensor_copy(lft[0:TS, 2, :], bank[7][0:TS, 2 * HEADS:3 * HEADS]))
            dve.tensor_copy(lfn_w[:, :].rearrange("p (j h q) -> p j h q", j=GB, q=NS),
                            lft[0:TS, 2, :].unsqueeze(1).unsqueeze(3).to_broadcast([TS, GB, HEADS, NS]))\
               .then_inc(S["lft_ready"], 1)
            dve.wait_ge(S["ncum_sum"], 1)
            dve.tensor_copy(ncum[:, :], bank[6][0:HEADS, 0:TP]).then_inc(S["ncum_ready"], 1)

            def p_low(t):
                dve.wait_ge(S["p_high"], t + 1)
                dve.tensor_tensor(h_lo[:, t, 0:TP], bank[4 + t % 2][:, 0:TP], h_hi[:, t, 0:TP].bitcast(F32),
                                  ALU.subtract).then_inc(S["p_low"], 1)

            for t in range(2 * HEADS + 2):
                if 1 <= t <= 2 * HEADS:
                    r = (t - 1) % 2
                    dve.wait_ge(S["p_exp"], t)
                    ch.link(dve.reciprocal(psm[:, r, :], psm[:, r, :]))
                    dve.tensor_scalar(pr[:, r, 0:P], pr[:, r, 0:P], psm[:, r, 0:1], None, ALU.mult)
                    dve.tensor_scalar(pr[:, r, P:3 * P], pr[:, r, P:3 * P], psm[:, r, 1:2], None, ALU.mult)\
                       .then_inc(S["p_scaled"], 1)
                if t < 2 * HEADS:
                    r = t % 2
                    if t == HEADS:
                        dve.wait_ge(S["toe_landed"], 16)
                    bias = big[:, C_CAUSAL:C_CAUSAL + 2 * P] if t < HEADS else toe[:, t % HEADS, :]
                    dve.wait_ge(S["p_s"], t + 1)
                    if t >= 2:
                        dve.wait_ge(S["p_t"], t - 1)
                    dve.tensor_tensor(pr[:, r, 0:P], bank[r][:, 0:P], bias[:, P:2 * P], ALU.add)
                    ch.link(dve.tensor_tensor(pr[:, r, P:3 * P], bank[r][:, P:3 * P], bias, ALU.add))
                    dve.tensor_reduce(pmx[:, r, 0:1], pr[:, r, 0:P], AX.X, ALU.max, negate=True)
                    dve.tensor_reduce(pmx[:, r, 1:2], pr[:, r, P:3 * P], AX.X, ALU.max, negate=True)\
                       .then_inc(S["p_max"], 1)
                if t >= 2:
                    p_low(t - 2)

            dve.sem_inc(S["ol_ready"], 1)
            dve.wait_ge(S["lf_landed"], 16 * NB * PAGES)
            ch.link(dve.memset(qbd[:, :, :], 0.0))

            def group(kind, g):
                kd = KIND[kind]
                n, G = kd["n"], GROUPS * kind + 1
                for j in range(GB):
                    last = dve.tensor_copy(qbd[:, j, :].rearrange("p (h x) -> p h x", x=32 + NS)[:, :, 0:NS],
                                           z[:, kd["q"]:kd["q"] + HEADS, bass.ds(TP + 16 * g + NS * j, NS)])
                    if kind == 0:
                        last = dve.tensor_copy(lfr[:, :, 32 * j:32 * j + 32].rearrange("p a (h q) -> p a h q", q=NS),
                                               lfc[:, bass.ds((GB * g + j) * PAGES, PAGES), :].unsqueeze(3)
                                               .to_broadcast([P, PAGES, HEADS, NS]))
                last.then_inc(S["qbd_ready"], 1)
                dve.wait_ge(S["kv_used"], quad0[kind] + 2 + n + 2 * n * g)
                ch.link(dve.tensor_tensor(ps[:, 1024:1024 + TS], bank[2][:, 0:TS],
                                          big[:, bass.ds(kd["new"] + TS * g, TS)], ALU.add))
                dve.tensor_reduce(mx[:, 1:2], ps[:, 1024:1024 + TS], AX.X, ALU.max)
                if kind == 0:
                    ch.link(dve.tensor_reduce(mx[:, 0:1], pairs[0][:, :, :], AX.XY, ALU.max))
                else:
                    dve.tensor_tensor(ps[:, 0:512], bank[0], big[:, C_LOGN:C_LOGN + 512], ALU.add)
                    ch.link(dve.tensor_tensor(ps[:, 512:W_MAIN], bank[1][:, 0:P], big[:, C_LOGN + 512:C_LOGN + W_MAIN],
                                              ALU.add))
                    ch.link(dve.tensor_reduce(mx[:, 0:1], ps[:, 0:W_MAIN], AX.X, ALU.max))
                dve.tensor_reduce(nm[:, 0:1], mx[:, :], AX.X, ALU.max, negate=True).then_inc(S["nm_ready"], 1)
                dve.wait_ge(S["exp_ready"], G + 1 + g)
                ch.link(dve.tensor_reduce(sm[:, 0:1], sm[:, :], AX.X, ALU.add))
                dve.reciprocal(rs[:, 0:1], sm[:, 0:1]).then_inc(S["r_ready"], 1)
                dve.wait_ge(S["oh_ready"], G + g)
                for c in range(2):
                    sl = (slice(None), slice(kind * HEADS + 4 * c, kind * HEADS + 4 * c + 4), bass.ds(TP + 16 * g, 16))
                    last = dve.tensor_tensor(h_lo[sl].rearrange("p h (j s) -> p h j s", s=NS), own_rows(c),
                                             h_hi[sl].bitcast(F32).rearrange("p h (j s) -> p h j s", s=NS), ALU.subtract)
                last.then_inc(S["ol_ready"], 1)

            for kind, per in ((0, 3), (1, 4)):
                with dve.Fori(0, GROUPS) as g:
                    ch.loop(g, 0, per)
                    group(kind, g)
                ch.end(GROUPS)

            segments([out])
            gain(2, PAIRS)
            half_gate(8, PAIRS)
            modulate(2)
            dve.wait_ge(S["st_done"], 5 * 16)
            segments(segs[segs.index(out) + 1:])
            dve.wait_ge(S["acc_b_read"], segs[-1].rb + segs[-1].bodies)
            dve.memset(tmps[:, 1, 0, 0:1], 0.0).then_inc(S["x_done"], 1)


def _tiles(w, k, n):
    return np.ascontiguousarray(w.reshape(k, P, n, P).transpose(2, 1, 0, 3).reshape(n, P, k * P))


def _bucket(dist):
    d = np.maximum(dist, 16).astype(np.float64)
    log_b = np.minimum((16 + np.log(d / 16) / np.log(128.0) * 16).astype(np.int64), 31)
    return np.where(dist < 16, np.maximum(dist, 0), log_b)


def _log_patterns(dist):
    n = sum(((dist >= 0) & (dist % r == 0) & (dist <= w)).astype(np.int64) for w, r in ((128, 1), (512, 4), (2048, 16)))
    return np.where(n > 0, np.log(np.maximum(n, 1)), NEG).astype(np.float32)


def _window_keys():
    early = (16 * np.arange(32)[:, None] + np.arange(NS)[None, :]).reshape(-1)
    return np.concatenate([early, 512 + np.arange(512)]).reshape(WT, P)


def _constants():
    f = np.float32
    eye = np.eye(P, dtype=f)
    sel = np.zeros((P, 16), f)
    for j in range(4):
        sel[32 * j + np.arange(NC), np.arange(NC)] = 1
    small = np.concatenate([eye, np.ones((P, P), f), sel], 1)
    k = np.arange(P)
    band = np.concatenate([np.ones((P, (PAGES - 1) * P), f), (k[:, None] > k[None, :]).astype(f)], 1)
    pos = _window_keys().reshape(-1)
    s = np.arange(NS)
    new = np.arange(TS) % NS
    dist = 1024 + s[:, None] - pos[None, :]
    dist_new = s[:, None] - new[None, :]
    d = np.concatenate([dist, dist_new], 1)
    onehot = np.zeros((NS, 32, d.shape[1]), f)
    onehot[:, :, :] = (_bucket(d)[:, None, :] == np.arange(32)[None, :, None])
    row_q = np.arange(P) % NS
    row_b = np.arange(P) // 32
    addc = _log_patterns(dist)[row_q]
    same = [(np.arange(TS)[None, :] // NS == GB * g + row_b[:, None]) for g in range(2)]
    new_dil = [np.where(m, _log_patterns(dist_new)[row_q], f(NEG)) for m in same]
    new_fox = [np.where(m & (dist_new[row_q] >= 0), f(0), f(NEG)) for m in same]
    causal = np.concatenate([np.zeros((P, P), f), np.where(k[None, :] <= k[:, None], f(0), f(NEG))], 1)
    negtri = np.concatenate([-(k[:, None] <= k[None, :]).astype(f), -np.ones((P, P), f)], 1)
    delta = (np.arange(P)[:, None] // 32 == s[None, :]).astype(f)
    t = np.arange(TS)
    ntri = np.zeros((P, TS), f)
    ntri[:TS] = -((t[:, None] // NS == t[None, :] // NS) & (t[:, None] <= t[None, :])).astype(f)
    big = np.concatenate([band, onehot.reshape(P, -1), addc, *new_dil, *new_fox, causal, negtri, delta, ntri], 1)
    back = 255 - np.arange(383)
    oh_rev = (_bucket(back)[None, :] == np.arange(32)[:, None]).astype(f) * (back >= 0)[None, :].astype(f)
    lp = _log_patterns(back)
    add_rev = np.broadcast_to(lp, (HEADS, 383)).astype(f)
    selh = np.zeros((HEADS, HEADS, P), f)
    selh[np.arange(HEADS), np.arange(HEADS)] = 1
    return small.astype(f), np.ascontiguousarray(big.astype(f)), np.ascontiguousarray(oh_rev.astype(f)), \
        np.ascontiguousarray(add_rev), selh.reshape(HEADS, HEADS * P)


def _lay_out(i):
    a = {k: np.asarray(v) for k, v in i.items()}
    cat = np.concatenate

    def feat(v):
        return np.ascontiguousarray(v.reshape(-1, KT, P).transpose(2, 1, 0))

    def up(w1, w3):
        return np.ascontiguousarray(np.stack([_tiles(w1[0], KT, FF), _tiles(w3[0], KT, FF)], 1).reshape(2 * FF, P, KT * P))

    w = a["w_in"][0]
    W = HEADS * HD
    fa = 3 * W
    cols = [w[:, fa:fa + P]] + [w[:, o:o + W] for o in (0, W, fa + HEADS, fa + HEADS + W, 2 * W, fa + HEADS + 2 * W)]
    small, big, ohrev, addrev, selh = _constants()
    keys = _window_keys()
    out = dict(
        xT=feat(cat([a["x_prompt"].reshape(TP, D), a["x_sample"].reshape(TS, D)])),
        cT=feat(cat([a["c_prompt"], a["c_sample"]])),
        gT=np.ascontiguousarray(np.stack([a[n][0].reshape(KT, P).T for n in ("g_ffn1", "g_mix", "g_ffn2")], 1)),
        bada=np.ascontiguousarray(a["b_ada"][0].reshape(ADA, P).T),
        nwT=np.ascontiguousarray(np.stack([a[n][0] for n in ("qn_fox", "kn_fox", "qn_dil", "kn_dil")], 1)),
        bfg=np.ascontiguousarray(a["b_forget"].reshape(HEADS, 1)),
        relb=np.ascontiguousarray(a["rel_bias"]),
        pt=np.ascontiguousarray(a["page_table"].reshape(1, NB * PAGES)),
        cst=small, cst2=big, ohrev=ohrev, addrev=addrev, selh=selh,
        w_ada=_tiles(a["w_ada"][0], KT, ADA),
        w13_1=up(a["w1_ffn1"], a["w3_ffn1"]), w2_1=_tiles(a["w2_ffn1"][0], FF, KT),
        w_in=_tiles(cat(cols, 1), KT, 49), w_out=_tiles(a["w_out"][0], KT, KT),
        w13_2=up(a["w1_ffn2"], a["w3_ffn2"]), w2_2=_tiles(a["w2_ffn2"][0], FF, KT),
        kpool=np.ascontiguousarray(a["cache_fox_k"][0].transpose(0, 3, 2, 1).reshape(POOL, HD, HEADS * PAGE)),
        vpool=np.ascontiguousarray(a["cache_fox_v"][0].reshape(POOL, PAGE, W)),
        lfpool=np.ascontiguousarray(a["cache_fox_logf"][0]),
        wink=np.ascontiguousarray(a["cache_win_k"][0][:, keys].transpose(0, 1, 4, 3, 2).reshape(NB, WT, HD, HEADS * P)),
        winv=np.ascontiguousarray(a["cache_win_v"][0][:, keys].reshape(NB, WT, P, W)),
    )
    return out


_OUTS = dict(y_out=(P, KT, T), kv_out=(4, P, HEADS, T), lf_out=(HEADS, T))


def kernel(**inputs):
    import concourse.bacc as _bacc
    from concourse.bass_utils import run_bass_kernel_spmd as _run

    arrays = _lay_out(inputs)
    nc = _bacc.Bacc("TRN2", target_bir_lowering=False, num_devices=1)
    args = [nc.dram_tensor(f"in_{n}_dram", v.shape, mybir.dt.from_np(v.dtype), kind="ExternalInput").ap()
            for n, v in arrays.items()]
    args += [nc.dram_tensor(f"out_{n}_dram", s, F32, kind="ExternalOutput").ap() for n, s in _OUTS.items()]
    decoder_layer(nc, *args)
    r = _run(nc, [{f"in_{n}_dram": v for n, v in arrays.items()}], core_ids=[0])
    y, kv, lf = (r.results[0][f"out_{n}_dram"] for n in _OUTS)
    y = y.transpose(2, 1, 0).reshape(T, D)
    kv = kv.transpose(0, 3, 2, 1)
    lf = lf.T

    def prompt(v):
        return np.ascontiguousarray(v[None, None, :TP])

    def sample(v):
        return np.ascontiguousarray(v[TP:].reshape((1, NB, NS) + v.shape[1:]))

    kf, kd, vf, vd = kv
    return (np.ascontiguousarray(y[None, :TP]), np.ascontiguousarray(y[TP:].reshape(NB, NS, D)),
            prompt(kf), prompt(vf), prompt(lf), prompt(kd), prompt(vd),
            sample(kf), sample(vf), sample(lf), sample(kd), sample(vd))
```

```python
from contextlib import ExitStack

import numpy as np

import concourse.bass as bass
from concourse import mybir

F32 = mybir.dt.float32
F32R = mybir.dt.float32r
I32 = mybir.dt.int32
ALU = mybir.AluOpType
ACT = mybir.ActivationFunctionType
AX = mybir.AxisListType

P = 128
D = 2048
KT = D // P
HEADS, HD = 8, 128
TP, NB, NS = 256, 8, 4
TS = NB * NS
T = TP + TS
FF = 43
CHUNKS = ((0, 15), (15, 14), (29, 14))
NPAR = 9
ADA = NPAR * KT
NC = NB + 1
PAGE, PAGES = 128, 8
POOL = 80
WT = 5
GB = 4
EPS = 1e-6
SCALE = HD ** -0.5
NEG = -1.0e30
SQR, SQL = KT // 4, 4
SHIFT, SCL, GATE = 0, 1, 2

C_ID, C_ONE, C_SEL, C_SMALL = 0, 128, 256, 272
W_MAIN = WT * P
C_BAND = 0
C_BUCKET = C_BAND + PAGES * PAGE
C_LOGN = C_BUCKET + W_MAIN + TS
C_NEW_DIL = C_LOGN + W_MAIN
C_NEW_FOX = C_NEW_DIL + 2 * TS
C_CAUSAL = C_NEW_FOX + 2 * TS
C_NEGTRI = C_CAUSAL + 2 * P
C_DELTA = C_NEGTRI + 2 * P
C_NTRI = C_DELTA + NS
C_BIG = C_NTRI + TS
REV = 383
GROUPS = NB // GB


class Seg:

    def __init__(self, kind, bodies, src, f=0, c=0, nk=KT, ada=False, moving="h", gate=None, ff0=0, d0=0,
                 k0=0, z0=0):
        self.kind, self.bodies, self.src = kind, bodies, src
        self.f, self.c, self.nk, self.ada = f, c, nk, ada
        self.moving, self.gate = moving, gate
        self.ff0, self.d0, self.k0, self.z0 = ff0, d0, k0, z0


def plan():
    segs = []

    def ffn(f):
        for c, (t0, n) in enumerate(CHUNKS):
            segs.append(Seg("up", n, f=f, c=c, ff0=t0, ada=f == 0, src=("w13", f)))
            runs = [(0, 8, False)] if f or c == 2 else [(0, 8, True)] if c == 0 else [(0, 5, True), (5, 3, False)]
            for b, m, ada in runs:
                segs.append(Seg("down", m, f=f, c=c, nk=n, moving="g", ada=ada, d0=2 * b, k0=t0,
                                gate=2 if f == 0 else 8, src=("w2", f)))

    ffn(0)
    segs.append(Seg("fa", 0, src=("w_in", 0)))
    segs.append(Seg("win", 16, src=("w_in", 0), z0=0))
    segs.append(Seg("win", 8, src=("w_in", 0), z0=32))
    segs.append(Seg("down", 8, f=0, gate=5, src=("w_out", 0), k0=0))
    ffn(1)
    slot = body = ra = rb = pair = ups = 0
    for s in segs:
        s.n0, s.b0, s.ra, s.rb, s.pair0, s.up0 = slot, body, ra, rb, pair, ups
        slot += 2 * s.bodies + (s.kind == "fa")
        body += s.bodies
        ra += s.bodies
        rb += s.bodies
        pair += s.bodies if s.ada else 0
        ups += s.bodies if s.kind == "up" else 0
    assert 2 * pair == ADA - 2 * KT
    return segs


class Chain:

    def __init__(self, eng, sem):
        self.eng, self.sem, self.n, self.i, self.per = eng, sem, 0, None, 0

    def link(self, ins):
        ins.then_inc(self.sem, 1)
        self.n += 1
        self.eng.wait_ge(self.sem, self.n if self.i is None else self.n + self.i * self.per)

    def loop(self, i, first, per):
        self.i, self.per, self.first, self.start = i, per, first, self.n
        self.n = self.start - first * per if not isinstance(i, int) else self.n
        return self

    def end(self, last):
        assert self.n - (self.start - self.first * self.per) == self.per, (self.n, self.start, self.per)
        self.n = self.start + self.per * (last - self.first)
        self.i = None


def decoder_layer(nc, xT, cT, gT, bada, nwT, bfg, relb, pt, cst, cst2, ohrev, addrev, selh,
                  w_ada, w13_1, w2_1, w_in, w_out, w13_2, w2_2, kpool, vpool, lfpool, wink, winv,
                  y_out, kv_out, lf_out):
    segs = plan()
    ffn1 = [s for s in segs if s.kind in ("up", "down") and s.b0 < 67]
    WS = {("w13", 0): w13_1, ("w13", 1): w13_2, ("w2", 0): w2_1, ("w2", 1): w2_2,
          ("w_in", 0): w_in, ("w_out", 0): w_out}

    with ExitStack() as ctx:
        base = 16512
        top = [base]

        def at(name, shape, dt, off):
            return nc.alloc_sbuf_tensor_at(name, shape, dt, offset=off)

        def sb(name, shape, dt=F32):
            n = int(np.prod(shape[1:])) * 4
            t = at(name, shape, dt, top[0])
            top[0] += -(-n // 32) * 32
            return t

        def sem(name):
            return ctx.enter_context(nc.semaphore(name))

        x = sb("x", [P, KT, T])
        h0 = top[0]
        h_hi, h_lo = sb("h_hi", [P, KT, T], F32R), sb("h_lo", [P, KT, T], F32R)
        par = sb("par", [P, ADA * NC])
        c0 = top[0]
        sc32 = sb("sc32", [P, KT, 32])
        lf = at("lf", [HEADS, T], F32, c0)
        cs = sb("cs", [P, C_SMALL])
        gv = sb("gv", [P, 3, KT])
        ba = sb("ba", [P, ADA])
        nw4 = sb("nw4", [P, 4])
        nw = sb("nw", [P, 32])
        eps = sb("eps", [P, 1])
        ident, ones, sel9 = cs[:, C_ID:C_ID + P], cs[:, C_ONE:C_ONE + P], cs[:, C_SEL:C_SEL + NC]
        rings0 = top[0]
        raw = sb("raw", [P, 2, KT * P])
        w_hi, w_lo = sb("w_hi", [P, 2, KT * P], F32R), sb("w_lo", [P, 2, KT * P], F32R)
        mix0 = top[0]
        g_hi, g_lo = sb("g_hi", [P, 15, T], F32R), sb("g_lo", [P, 15, T], F32R)
        adaw = sb("adaw", [P, 2, KT * P])
        part_sb = sb("part_sb", [P, 4 * P])
        su, gf = sb("su", [P, T]), sb("gf", [P, T])
        hf = sb("hf", [P, 2, SQL, T])
        sq = sb("sq", [P, 2, SQL, T])
        tmps = sb("tmps", [P, 2, NB, NS])
        sq0 = top[0] - 2 * SQL * T * 4 - 2 * TS * 4
        y0, ms, tt = (at(n, [P, T], F32, sq0 + k * T * 4) for k, n in enumerate(("y0", "ms", "tt")))
        rev = at("rev", [HEADS, REV], F32, sq0 + 3 * T * 4)
        fa_sb, fe = at("fa_sb", [HEADS, T], F32, sq0 + 5 * T * 4), at("fe", [HEADS, T], F32, sq0 + 6 * T * 4)
        adax = at("adax", [P, 4, KT * P], F32, mix0)
        assert 4 * KT * P * 4 <= 2 * 15 * T * 4
        big = sb("big", [P, C_BIG])
        lfc = sb("lfc", [P, NB * PAGES, HEADS])
        pages = sb("pages", [1, NB * PAGES], I32)
        rbr = sb("rbr", [P, HEADS])
        v_new = sb("v_new", [TS, 2 * HEADS * HD])
        vn0 = top[0] - 2 * HEADS * HD * 4
        ohr = at("ohr", [32, REV], F32, vn0 + 4096)
        adr = at("adr", [HEADS, REV], F32, vn0 + 5632)
        z = at("z", [P, 6 * HEADS, T], F32, mix0)
        hf0 = mix0 + 6 * HEADS * T * 4
        assert hf0 <= top[0]
        small = [hf0 + 2 * 2 * SQL * T * 4]
        yh = at("yh", [P, 2, T], F32, hf0)
        mh = at("mh", [P, 2, T], F32, hf0 + 2 * T * 4)
        th = at("th", [P, 2, T], F32, hf0 + 4 * T * 4)
        pr = at("pr", [P, 2, 3 * P], F32, hf0)
        prt = at("prt", [P, 2, 3 * P], F32, hf0 + 3072)
        sel0 = hf0 + 6 * T * 4
        selw = at("selw", [HEADS, HEADS * P], F32, sel0)
        ncum = at("ncum", [HEADS, TP], F32, sel0 + 4096)
        toe = at("toe", [P, HEADS, 2 * P], F32, sel0)
        vnat = at("vnat", [P, 2, 2 * P], F32, sel0 + 8192)
        bias_w = at("bias_w", [P, P], F32, sel0 + 10240)
        assert sel0 + 10752 <= hf0 + 2 * 2 * SQL * T * 4
        def quad(name, *offs):
            n = GB // len(offs)
            parts = [at(f"{name}_{i}", [P, n, HEADS * P], F32, o) for i, o in enumerate(offs)]
            return [parts[j // n][:, j % n, :] for j in range(GB)]
        half = HEADS * T * 4
        ring = [quad("kv_raw", rings0), quad("kv_high", rings0 + 16384)]
        third = [quad("kv_h", h0 + half, h0 + 3 * half), quad("kv_z", mix0)]
        assert GB // 2 * HEADS * P * 4 <= half

        def kv(m, j):
            return (ring + [third[m >= GROUPS * 2 * PAGES]])[m % 3][j]
        over = rings0 + 32768
        ps = at("ps", [P, 1024 + TS], F32, over)
        pst = at("pst", [P, 9, P], F32, over + 4224)
        lfr = at("lfr", [P, PAGES, P], F32, over + 8832)
        lfn_w = at("lfn_w", [TS, P], F32, over + 12928)
        qbd = [sb("qbd0", [P, 2, 288]), at("qbd1", [P, 2, 288], F32, over + 13440)]
        assert 32768 + 13440 + 2304 <= 6 * KT * P * 4
        lft = at("lft", [P, 3, HEADS], F32, c0 + T * 4)
        bfs = sb("bfs", [HEADS, 1])
        rbs = sb("rbs", [32, HEADS])
        mx, nm, sm, rs = sb("mx", [P, 2]), sb("nm", [P, 2]), sb("sm", [P, 2]), sb("rs", [P, 2])
        pmx, psm = sb("pmx", [P, 2, 2]), sb("psm", [P, 2, 2])
        rev_dram = nc.dram_tensor("rev_dram", [HEADS, P, REV], F32).ap()

        pairs = [ctx.enter_context(nc.psum_tensor(f"banks{i}", [P, 2, 512], F32)) for i in range(4)]
        bank = [pairs[i // 2][:, i % 2, :] for i in range(8)]
        acc_a, acc_b, ada_part, ada_selp, ssb = bank[0], bank[1], bank[2], bank[3], bank[4]
        ss2 = pairs[2]

        print(top[0])
        names = """ld_small ld_x w_landed0 w_landed1 hi_ready lo_ready w_used acc_a_ready acc_b_ready
            acc_a_read acc_b_read ada_landed0 ada_landed1 adax_landed0 adax_landed1 adax_landed2
            adax_landed3 ada_used ada_sb ada_sel ada_fin c_ready par_ready sq_ready sq_used ss_ready
            y0_ready hf_ready hhi_ready h_ready su_ready g_ready act_chain dve_chain y_stored heads_stored x_done
            ld_att ld_selw ld_pages lf_landed rev_sum rev_ready rev_stored toe_landed fa_ready fe_ready lf_ready
            hsq_ready hss_ready hy_ready head_ready lft_sum lft_ready ncum_sum ncum_ready
            p_s p_max p_exp p_scaled p_v p_vcopy p_t p_tcopy p_o p_high p_low
            vn_sum vn_ready kv_landed0 kv_landed1 kv_landed2 kv_used qbd_ready sc_ready nm_ready exp_ready
            r_ready pt_sum pt_ready o_ready os_ready ot_ready oh_ready ol_ready"""
        S = {n: sem(n) for n in names.split()}
        block = ctx.enter_context(nc.Block())

        def run(seg, eng, body, first=0, chain=None, per=0):
            if first >= seg.bodies:
                return
            with eng.Fori(first, seg.bodies) as i:
                if chain:
                    chain.loop(i, first, per)
                body(i)
            if chain:
                chain.end(seg.bodies)

        KIND = (dict(n=PAGES, q=0, k=8, v=32, new=C_NEW_FOX), dict(n=WT, q=16, k=24, v=40, new=C_NEW_DIL))
        quad0 = (0, GROUPS * 2 * PAGES)
        QUADS = GROUPS * 2 * (PAGES + WT)
        RING = 3
        fa = next(s for s in segs if s.kind == "fa")
        out = next(s for s in segs if s.kind == "down" and s.moving == "h")
        ffn2 = segs[segs.index(out) + 1]
        PAIRS = 8 + (ADA - 2 * KT) // 2
        WIN = (("one", 0, 1), ("one", 1, 2), ("one", 2, 3), ("loop", 3, 16), ("one", 16, 17), ("one", 17, 18), ("loop", 18, 24))

        def win_bodies(eng, body, chain=None, per=(0, 0), extra=None):
            for n, (how, a, b) in enumerate(WIN):
                if how == "one":
                    body(a, a)
                else:
                    with eng.Fori(a, b) as i:
                        if chain:
                            chain.loop(i, a, per[0] if a < 16 else per[1])
                        body(i, a)
                    if chain:
                        chain.end(b)
                if extra and a == 1:
                    extra()

        P_BANKS = ((5, 7, 6, 3), (0, 1, 2, 5))
        STEPS = (((0, 2, 4, 7), (-1, 1, 4, 7)), ((-1, 1, 2, 4), (-1, 0, 2, 4)))

        def p_bank(t, use):
            return bank[P_BANKS[t // 2 % 2][use]]

        def own_rows(c):
            b = bank[3 + c]
            return bass.AP(b.tensor, b.offset + 16 * c, [[1024, P], [P + NS, 4], [32, GB], [1, NS]])

        @block.sync
        def _(sp):
            sp.dma_start(sc32[:, :, 0:NC], cT).then_inc(S["ld_small"], 16)
            sp.dma_start(cs[:, :], cst).then_inc(S["ld_small"], 16)
            sp.dma_start(gv[:, :, :], gT).then_inc(S["ld_small"], 16)
            sp.dma_start(ba[:, :], bada).then_inc(S["ld_small"], 16)
            sp.dma_start(nw4[:, :], nwT).then_inc(S["ld_small"], 16)
            sp.dma_start(bfs[:, :], bfg).then_inc(S["ld_small"], 16)

            def ada_group(i, first):
                for j in range(4):
                    if not first:
                        sp.wait_ge(S["ada_used"], 4 * i + j - 3)
                    sp.dma_start(adax[:, j, :], w_ada[bass.ds(4 * i + j, 1), :, :].rearrange("a p n -> p (a n)"))\
                      .then_inc(S[f"adax_landed{j}"], 16)
            ada_group(0, True)
            sp.dma_start(x[:, :, :], xT).then_inc(S["ld_x"], 16)
            with sp.Fori(1, 2 * KT // 4) as i:
                ada_group(i, False)

            def slot(seg, j, i):
                n, r = seg.n0 + j, (seg.n0 + j) % 2
                if isinstance(i, int) and n + 2 * i < 2:
                    pass
                else:
                    sp.wait_ge(S["lo_ready"], 2 * (n - 1) + 4 * i)
                src = WS[seg.src]
                if seg.kind == "up":
                    ap = src[bass.ds(2 * (seg.ff0 + i) + j, 1), :, :]
                elif seg.kind == "down":
                    ap = src[bass.ds(seg.d0 + 2 * i + j, 1), :, seg.k0 * P:(seg.k0 + seg.nk) * P]
                elif seg.kind == "win":
                    ap = src[bass.ds(1 + seg.z0 + 2 * i + j, 1), :, :]
                else:
                    ap = src[0:1, :, :]
                sp.dma_start(raw[:, r, 0:seg.nk * P], ap.rearrange("a p n -> p (a n)"))\
                  .then_inc(S[f"w_landed{r}"], 16)

            def ada_pair(seg, i):
                for j in range(2):
                    if not (isinstance(i, int) and seg.pair0 + i == 0):
                        sp.wait_ge(S["ada_used"], 2 * KT + 2 * seg.pair0 + j - 1 + 2 * i)
                    sp.dma_start(adaw[:, j, :], w_ada[bass.ds(2 * KT + 2 * seg.pair0 + 2 * i + j, 1), :, :]
                                 .rearrange("a p n -> p (a n)")).then_inc(S[f"ada_landed{j}"], 16)

            def stream(some):
                for seg in some:
                    def body(i, seg=seg):
                        slot(seg, 0, i)
                        if seg.ada:
                            ada_pair(seg, i)
                        slot(seg, 1, i)
                    peel = 1 if seg.b0 == 0 else 0
                    if peel:
                        body(0)
                    run(seg, sp, body, peel)

            stream(ffn1)
            slot(fa, 0, 0)
            win = segs[segs.index(fa) + 1:segs.index(fa) + 3]
            stream(win)
            sp.wait_ge(S["ld_pages"], 16)
            for m in range(QUADS):
                kind = 0 if m < quad0[1] else 1
                n = KIND[kind]["n"]
                g, v, p = (m - quad0[kind]) // (2 * n), (m - quad0[kind]) // n % 2, (m - quad0[kind]) % n
                if m == 0:
                    sp.wait_ge(S["lo_ready"], 2 * out.n0)
                if m == 1:
                    sp.wait_ge(S["w_used"], 2 * out.n0)
                if kind == 1 and m % RING == 2:
                    sp.wait_ge(S["heads_stored"], 5 * 16)
                    sp.wait_ge(S["p_s"], HEADS)
                if kind == 0:
                    pg = [sp.value_load(pages[0:1, (GB * g + j) * PAGES + p:(GB * g + j) * PAGES + p + 1],
                                        min_val=0, max_val=POOL - 1) for j in range(GB)]
                sp.wait_ge(S["kv_used"], m + 1)
                for j in range(GB):
                    if kind == 0:
                        src = (vpool if v else kpool)[bass.ds(pg[j], 1), :, :]
                    else:
                        src = (winv if v else wink)[GB * g + j:GB * g + j + 1, p, :, :]
                    sp.dma_start(kv(m, j), src.rearrange("a p n -> p (a n)"))\
                      .then_inc(S[f"kv_landed{m % RING}"], 16)
            sp.wait_ge(S["kv_used"], max(m for m in range(QUADS) if m % RING == 0) + RING + 1)
            stream([out])
            stream(segs[segs.index(out) + 1:])
            sp.wait_ge(S["x_done"], 1)
            sp.dma_start(y_out, x[:, :, :]).then_inc(S["y_stored"], 16)
            sp.wait_ge(S["y_stored"], 16)

        @block.gpsimd
        def _(pool):
            pool.dma_start(pages[:, :], pt).then_inc(S["ld_pages"], 16)
            pool.dma_start(rbs[:, :], relb).then_inc(S["ld_att"], 16)
            pool.dma_start(ohr[:, :], ohrev).then_inc(S["ld_att"], 16)
            pool.dma_start(adr[:, :], addrev).then_inc(S["ld_att"], 16)
            pool.dma_start(big[:, :], cst2).then_inc(S["ld_att"], 16)
            for q in range(NS):
                pool.dma_start(rbr[32 * q:32 * q + 32, :], relb).then_inc(S["ld_att"], 16)
            pool.wait_ge(S["ld_pages"], 16)
            with pool.Fori(0, NB * PAGES) as i:
                pg = pool.value_load(pages[0:1, bass.ds(i, 1)], min_val=0, max_val=POOL - 1)
                pool.dma_start(lfc[:, bass.ds(i, 1), :], lfpool[bass.ds(pg, 1), :, :].rearrange("a p h -> p a h"))\
                    .then_inc(S["lf_landed"], 16)
            pool.wait_ge(S["rev_ready"], 1)
            pool.dma_start(rev_dram, rev[:, :].unsqueeze(1).to_broadcast([HEADS, P, REV])).then_inc(S["rev_stored"], 16)
            pool.wait_ge(S["rev_stored"], 16)
            pool.wait_ge(S["h_ready"], 2 * SQR)
            pool.dma_start(selw[:, :], selh).then_inc(S["ld_selw"], 16)

            def store_heads(n, z0):
                pool.dma_start(kv_out[n], z[:, z0:z0 + HEADS, :]).then_inc(S["heads_stored"], 16)

            pool.wait_ge(S["lf_ready"], 1)
            pool.dma_start(lf_out, lf[:, :]).then_inc(S["heads_stored"], 16)
            pool.wait_ge(S["head_ready"], 16)
            store_heads(0, 8)
            store_heads(1, 24)
            pool.wait_ge(S["acc_b_read"], out.rb)
            store_heads(2, 32)
            store_heads(3, 40)
            pool.wait_ge(S["p_s"], HEADS)
            pool.dma_start(toe[:, :, :], bass.AP(rev_dram.tensor, P - 1, [[REV - 1, P], [P * REV, HEADS], [1, 2 * P]]))\
                .then_inc(S["toe_landed"], 16)

        @block.tensor
        def _(pe):
            def ada_tile(w, col, scoped):
                for kt in range(KT):
                    j = kt % 4
                    last = pe.matmul(ada_part[32 * j:32 * j + 32, col * P:(col + 1) * P], sc32[:, kt, :],
                                     w[:, kt * P:(kt + 1) * P], start=kt < 4, stop=kt >= KT - 4,
                                     tile_position=(0, 32 * j))
                last.then_inc(S["ada_used"], 1)

            def ada_select(group, n):
                pe.wait_ge(S["ada_sb"], group + 1)
                if not (isinstance(group, int) and group == 0):
                    pe.wait_ge(S["ada_fin"], group)
                for c in range(n):
                    last = pe.matmul(ada_selp[:, c * NC:(c + 1) * NC], part_sb[:, c * P:(c + 1) * P], sel9,
                                     start=True, stop=True)
                last.then_inc(S["ada_sel"], 1)

            def square_sum(r):
                for c in range(SQR):
                    pe.wait_ge(S["sq_ready"], SQR * r + c + 1)
                    for k in range(SQL):
                        last = pe.matmul(ssb[:, 0:T], ones, sq[:, c % 2, k, :], start=c == 0 and k == 0,
                                         stop=c == SQR - 1 and k == SQL - 1)
                    last.then_inc(S["sq_used"], 1)

            pe.sem_inc(S["kv_used"], RING)
            pe.wait_ge(S["c_ready"], 1)
            square_sum(0)
            pe.wait_ge(S["ld_att"], 8 * 16)
            pe.matmul(bank[5][0:HEADS, 0:REV], rbs[:, :], ohr[:, :], start=True, stop=True).then_inc(S["rev_sum"], 1)

            def ada_group(i, first):
                if not first:
                    pe.wait_ge(S["ada_sb"], i)
                for j in range(4):
                    pe.wait_ge(S[f"adax_landed{j}"], 16 + 16 * i)
                    ada_tile(adax[:, j, :], j, None)
                ada_select(i, 4)
            ada_group(0, True)
            with pe.Fori(1, 2 * KT // 4) as i:
                ada_group(i, False)

            def tile(seg, j, i, bank, mid=None):
                n, r = seg.n0 + j, (seg.n0 + j) % 2
                m_hi, m_lo = (h_hi, h_lo) if seg.moving == "h" else (g_hi, g_lo)
                half = KT // 2
                for q, (a, b) in enumerate(((0, half), (half, seg.nk))):
                    pe.wait_ge(S["lo_ready"], 2 * n + q + 1 + 4 * i)
                    for k in range(a, b):
                        hi, lo = w_hi[:, r, k * P:(k + 1) * P], w_lo[:, r, k * P:(k + 1) * P]
                        pe.matmul(bank[:, 0:T], hi, m_hi[:, k, :], start=k == 0, stop=False)
                        pe.matmul(bank[:, 0:T], hi, m_lo[:, k, :], start=False, stop=False)
                        last = pe.matmul(bank[:, 0:T], lo, m_hi[:, k, :], start=False, stop=k == seg.nk - 1)
                    if q == 0:
                        last.then_inc(S["w_used"], 1)
                        if mid:
                            mid()
                last.then_inc(S["w_used"], 1)

            def pair(seg, i, mid_b=None):
                if seg.ada:
                    g = 8 + seg.pair0 + i
                    pe.wait_ge(S["ada_sb"], g)
                    for j in range(2):
                        pe.wait_ge(S[f"ada_landed{j}"], 16 * (seg.pair0 + 1) + 16 * i)
                        ada_tile(adaw[:, j, :], j, None)
                if not (isinstance(i, int) and seg.b0 + i == 0):
                    pe.wait_ge(S["acc_a_read"], seg.ra + i)
                tile(seg, 0, i, acc_a)
                if seg.ada:
                    ada_select(g, 2)
                if not (isinstance(i, int) and seg.b0 + i == 0):
                    pe.wait_ge(S["acc_b_read"], seg.rb + i)
                tile(seg, 1, i, acc_b, mid_b)

            def segments(some):
                for seg in some:
                    if seg.kind == "down" and seg.moving == "g":
                        pe.wait_ge(S["g_ready"], seg.up0)
                    peel = 1 if seg.b0 == 0 else 0
                    if peel:
                        pair(seg, 0)
                    run(seg, pe, lambda i, seg=seg: pair(seg, i), peel)

            pe.wait_ge(S["h_ready"], SQR)
            segments(ffn1)
            square_sum(1)
            pe.wait_ge(S["h_ready"], 2 * SQR)
            tile(fa, 0, 0, bank[2])

            def head_sums(b):
                pe.wait_ge(S["hsq_ready"], b + 1)
                if not (isinstance(b, int) and b == 0):
                    pe.wait_ge(S["head_ready"], b)
                for j in range(2):
                    last = pe.matmul(ss2[:, j, 0:T], ones, sq[:, j, SQL - 1, :], start=True, stop=True)
                last.then_inc(S["hss_ready"], 1)

            qk, vv = segs[segs.index(fa) + 1:segs.index(fa) + 3]

            def win_body(b, j):
                seg, i = (qk, b) if j < 16 else (vv, b - 16)
                pair(seg, i, (lambda: head_sums(b - 1)) if 1 <= j <= 16 else None)
            win_bodies(pe, win_body)

            def turn(dst, src, done=None):
                return pe.transpose(dst, src, ident[0:src.shape[0], 0:src.shape[0]])

            pe.wait_ge(S["lf_ready"], 1)
            for t in range(2):
                turn(bank[7][:, t * HEADS:(t + 1) * HEADS], lf[:, t * P:(t + 1) * P])
            turn(bank[7][0:TS, 2 * HEADS:3 * HEADS], lf[:, TP:T]).then_inc(S["lft_sum"], 1)
            pe.wait_ge(S["lft_ready"], 1)
            negtri = big[:, C_NEGTRI:C_NEGTRI + 2 * P]
            pe.matmul(bank[6][0:HEADS, 0:TP], lft[:, 0, :], negtri, start=True, stop=False)
            pe.matmul(bank[6][0:HEADS, P:TP], lft[:, 1, :], negtri[:, 0:P], start=False, stop=True)\
              .then_inc(S["ncum_sum"], 1)
            pe.wait_ge(S["head_ready"], 16)
            pe.wait_ge(S["acc_b_read"], out.rb)
            pe.wait_ge(S["ncum_ready"], 1)
            pe.wait_ge(S["ld_selw"], 16)

            def p_scores(t):
                kd, h = KIND[t // HEADS], t % HEADS
                q, k, s_bank = z[:, kd["q"] + h, :], z[:, kd["k"] + h, :], p_bank(t, 0)
                if t:
                    pe.wait_ge(S["p_max"], t)
                if t and t % 4 == 0:
                    pe.wait_ge(S["p_low"], t)
                for c, (a, n) in enumerate(((0, P), (P, 2 * P))):
                    fox = t < HEADS
                    last = pe.matmul(s_bank[:, a:a + n], q[:, c * P:(c + 1) * P], k[:, 0:n], start=True, stop=not fox)
                    if fox:
                        last = pe.matmul(s_bank[:, a:a + n], selw[:, h * P:(h + 1) * P], ncum[:, 0:n],
                                         start=False, stop=True)
                last.then_inc(S["p_s"], 1)

            def p_values(t):
                v = z[:, KIND[t // HEADS]["v"] + t % HEADS, :]
                if t:
                    pe.wait_ge(S["p_vcopy"], t)
                turn(p_bank(t, 1)[:, 0:P], v[:, 0:P])
                turn(p_bank(t, 1)[:, P:2 * P], v[:, P:2 * P]).then_inc(S["p_v"], 1)

            def p_turn(t):
                pe.wait_ge(S["p_scaled"], t + 1)
                if t:
                    pe.wait_ge(S["p_tcopy"], t)
                for c in range(3):
                    last = turn(p_bank(t, 2)[:, c * P:(c + 1) * P], pr[:, t % 2, c * P:(c + 1) * P])
                last.then_inc(S["p_t"], 1)

            def p_outputs(t):
                pe.wait_ge(S["p_tcopy"], t + 1)
                pe.wait_ge(S["p_vcopy"], t + 1)
                if t:
                    pe.wait_ge(S["p_low"], t)
                o = p_bank(t, 3)
                pe.matmul(o[:, 0:TP], vnat[:, t % 2, 0:P], prt[:, t % 2, 0:2 * P], start=True, stop=False)
                pe.matmul(o[:, P:TP], vnat[:, t % 2, P:2 * P], prt[:, t % 2, 2 * P:3 * P], start=False, stop=True)\
                  .then_inc(S["p_o"], 1)

            def step(t, i):
                if i == 1:
                    p_turn(t)
                if i < 2:
                    p_scores(t + i)
                    p_values(t + i)
                if i >= 2:
                    p_outputs(t + i - 2)
                if i == 2:
                    p_turn(t + 1)

            for c in range(4):
                if c:
                    pe.wait_ge(S["vn_ready"], c)
                for h in range(4):
                    last = turn(bank[6][0:TS, h * P:(h + 1) * P], z[:, 32 + 4 * c + h, TP:T])
                last.then_inc(S["vn_sum"], 1)

            def group(kind, g):
                kd = KIND[kind]
                n, G = kd["n"], GROUPS * kind + g + 1
                t0, m0 = 4 * (G - 1), quad0[kind] + 2 * kd["n"] * g
                main, new = pairs[0], bank[2]
                pe.wait_ge(S["qbd_ready"], G)
                if G > 1:
                    pe.wait_ge(S["exp_ready"], G - 1)
                    pe.wait_ge(S["p_max"], t0)
                    pe.wait_ge(S["p_vcopy"], t0)
                    pe.wait_ge(S["p_tcopy"], t0)
                skip = dict(skip_group_check=True)
                if kind == 0:
                    for p in range(PAGES - 1, -1, -1):
                        b = (PAGES - 1 - p) * PAGE
                        pe.matmul(main[:, 0, 0:min(512, (p + 1) * P)], lfr[:, p, :], big[:, b:b + min(512, (p + 1) * P)],
                                  start=p == PAGES - 1, stop=False, **skip)
                        if p >= 4:
                            pe.matmul(main[:, 1, 0:(p - 3) * P], lfr[:, p, :], big[:, b + 512:b + (p + 1) * P],
                                      start=p == PAGES - 1, stop=False, **skip)
                    pe.matmul(new[:, 0:TS], lfn_w[:, :], big[0:TS, C_NTRI:C_NTRI + TS], start=True, stop=False, **skip)
                else:
                    for dst, a, b in ((main[:, 0, :], 0, 512), (main[:, 1, 0:P], 512, W_MAIN), (new[:, 0:TS], W_MAIN, W_MAIN + TS)):
                        pe.matmul(dst, bias_w[:, :], big[:, C_BUCKET + a:C_BUCKET + b], start=True, stop=False, **skip)

                def scores(dst, moving, last):
                    for h in range(HEADS):
                        for j in range(GB):
                            r = pe.matmul(dst(j), qbd[j // 2][:, j % 2, 32 * h:32 * h + 32], moving(j, h), start=False,
                                          stop=h == HEADS - 1, tile_position=(0, 32 * j), **skip)
                    return r
                scores(lambda j: new[32 * j:32 * j + 32, 0:TS], lambda j, h: z[:, kd["k"] + h, TP:T], True)

                def landed(m):
                    pe.wait_ge(S[f"kv_landed{m % RING}"], 64 * (m // RING + 1))

                def steps(phase, p):
                    for i, after in enumerate(STEPS[kind][phase]):
                        if after == p:
                            step(t0 + 2 * phase, i)

                if G > 1:
                    pe.wait_ge(S["ol_ready"], G - 1)
                steps(0, -1)
                for p in range(n):
                    landed(m0 + p)
                    scores(lambda j: main[32 * j:32 * j + 32, p // 4, (p % 4) * P:(p % 4 + 1) * P],
                           lambda j, h: kv(m0 + p, j)[:, h * P:(h + 1) * P], False)\
                        .then_inc(S["kv_used"], 1)
                    steps(0, p)
                pe.wait_ge(S["exp_ready"], G)
                pe.wait_ge(S["p_low"], t0 + 2)
                pe.wait_ge(S["p_max"], t0 + 2)
                for p in range(n):
                    turn(bank[3 + p // 4][:, (p % 4) * P:(p % 4 + 1) * P], ps[:, p * P:(p + 1) * P])
                turn(bank[5][0:TS, 0:P], ps[:, 1024:1024 + TS]).then_inc(S["pt_sum"], 1)
                steps(1, -1)
                pe.wait_ge(S["pt_ready"], G)
                pe.wait_ge(S["p_vcopy"], t0 + 2)
                pe.wait_ge(S["p_tcopy"], t0 + 2)
                o = pairs[3]
                for c in range(2):
                    for j in range(GB):
                        a = (kind * 2 + c) * 512
                        pe.matmul(o[32 * j:32 * j + 32, c, :], pst[0:TS, 8, 32 * j:32 * j + 32], v_new[:, a:a + 512],
                                  start=True, stop=False, tile_position=(0, 32 * j), **skip)
                for p in range(n):
                    m = m0 + n + p
                    landed(m)
                    for c in range(2):
                        for j in range(GB):
                            last = pe.matmul(o[32 * j:32 * j + 32, c, :], pst[:, p, 32 * j:32 * j + 32],
                                             kv(m, j)[:, 512 * c:512 * c + 512], start=False,
                                             stop=p == n - 1, tile_position=(0, 32 * j), **skip)
                    last.then_inc(S["kv_used"], 1)
                    steps(1, p)
                pe.wait_ge(S["os_ready"], G)
                for h in range(HEADS):
                    last = turn(bank[3 + h // 4][:, (h % 4) * P:(h % 4 + 1) * P], ps[:, h * P:(h + 1) * P])
                last.then_inc(S["ot_ready"], 1)

            pe.wait_ge(S["vn_ready"], 4)
            for kind in (0, 1):
                for g in range(GROUPS):
                    group(kind, g)

            pe.wait_ge(S["ol_ready"], 2 * GROUPS)
            segments([out])
            square_sum(2)
            pe.wait_ge(S["h_ready"], 3 * SQR)
            segments(segs[segs.index(out) + 1:])

        @block.scalar
        def _(act):
            ch = Chain(act, S["act_chain"])

            def split_high(seg, j, i):
                n, r = seg.n0 + j, (seg.n0 + j) % 2
                half = KT // 2 * P
                for q, (a, b) in enumerate(((0, half), (half, seg.nk * P))):
                    if q == 0:
                        act.wait_ge(S[f"w_landed{r}"], 16 * (n // 2 + 1) + 16 * i)
                    if not (isinstance(i, int) and n + 2 * i < 2):
                        act.wait_ge(S["w_used"], 2 * (n - 2) + q + 1 + 4 * i)
                    act.activation(w_hi[:, r, a:b], raw[:, r, a:b], ACT.Copy).then_inc(S["hi_ready"], 1)

            def squares(r):
                for c in range(SQR):
                    if SQR * r + c >= 2:
                        act.wait_ge(S["sq_used"], SQR * r + c - 1)
                    act.activation(sq[:, c % 2, :, :], x[:, SQL * c:SQL * (c + 1), :], ACT.Square)\
                       .then_inc(S["sq_ready"], 1)

            def inverse_root(r):
                act.wait_ge(S["sq_used"], SQR * (r + 1))
                ch.link(act.activation(y0[:, :], ssb[:, 0:T], ACT.Ln, bias=eps[:, 0:1], scale=1.0 / D))
                act.activation(y0[:, :], y0[:, :], ACT.Exp, scale=-0.5).then_inc(S["y0_ready"], 1)

            def high_of_h(r):
                for c in range(SQR):
                    act.wait_ge(S["hf_ready"], SQR * r + c + 1)
                    act.activation(h_hi[:, SQL * c:SQL * (c + 1), :], hf[:, c % 2, :, :], ACT.Copy)\
                       .then_inc(S["hhi_ready"], 1)

            def ada_copy(group, n):
                act.wait_ge(S["ada_used"], 4 * (group + 1) if n == 4 else 2 * KT + 2 * (group - 7))
                if not (isinstance(group, int) and group == 0):
                    act.wait_ge(S["ada_sel"], group)
                act.activation(part_sb[:, 0:n * P], ada_part[:, 0:n * P], ACT.Copy).then_inc(S["ada_sb"], 1)

            act.wait_ge(S["ld_small"], 96)
            act.wait_ge(S["dve_chain"], 2)
            act.activation(sc32[:, :, 0:NC], sc32[:, :, 0:NC], ACT.Silu).then_inc(S["c_ready"], 1)
            act.wait_ge(S["ld_x"], 16)
            squares(0)
            inverse_root(0)
            ada_copy(0, 4)
            with act.Fori(1, 2 * KT // 4) as i:
                ada_copy(i, 4)
            high_of_h(0)

            def body(seg, i):
                split_high(seg, 0, i)
                if seg.ada:
                    ada_copy(8 + seg.pair0 + i, 2)
                split_high(seg, 1, i)
                if seg.kind == "up":
                    act.wait_ge(S["w_used"], 2 * (seg.n0 + 1) + 4 * i)
                    if not (isinstance(i, int) and seg.up0 + i == 0):
                        act.wait_ge(S["g_ready"], seg.up0 + i)
                    act.activation(su[:, :], acc_a[:, 0:T], ACT.Silu).then_inc(S["acc_a_read"], 1)

            def segments(some):
                for seg in some:
                    peel = 1 if seg.b0 == 0 else 0
                    if peel:
                        body(seg, 0)
                    run(seg, act, lambda i, seg=seg: body(seg, i), peel)

            segments(ffn1)
            act.wait_ge(S["acc_b_read"], fa.rb)
            act.wait_ge(S["rev_stored"], 16)
            squares(1)
            inverse_root(1)
            high_of_h(1)

            qk, vv = segs[segs.index(fa) + 1:segs.index(fa) + 3]
            split_high(fa, 0, 0)

            def head_squares(b):
                act.wait_ge(S["acc_b_read"], qk.rb + 1 + b)
                if not (isinstance(b, int) and b == 0):
                    act.wait_ge(S["hss_ready"], b)
                act.activation(sq[:, :, SQL - 1, :], z[:, bass.ds(2 * b, 2), :], ACT.Square).then_inc(S["hsq_ready"], 1)

            def win_body(b, j):
                seg, i = (qk, b) if j < 16 else (vv, b - 16)
                split_high(seg, 0, i)
                if 2 <= j <= 17:
                    act.wait_ge(S["hss_ready"], b - 1)
                    if j > 2:
                        act.wait_ge(S["head_ready"], b - 2)
                    ch.link(act.activation(yh[:, :, :], ss2[:, :, 0:T], ACT.Ln, bias=eps[:, 0:1], scale=1.0 / HD))
                    act.activation(yh[:, :, :], yh[:, :, :], ACT.Exp, scale=-0.5).then_inc(S["hy_ready"], 1)
                if 1 <= j <= 16:
                    head_squares(b - 1)
                split_high(seg, 1, i)

            def log_forget():
                act.wait_ge(S["fa_ready"], 1)
                ch.link(act.activation(fe[:, :], fa_sb[:, :], ACT.Abs))
                ch.link(act.activation(fe[:, :], fe[:, :], ACT.Exp, scale=-1.0))
                act.activation(fe[:, :], fe[:, :], ACT.Ln, bias=ones[0:HEADS, 0:1]).then_inc(S["fe_ready"], 1)
            win_bodies(act, win_body, ch, (1, 0), log_forget)

            def p_exp(t):
                act.wait_ge(S["p_max"], t + 1)
                for c, (a, n) in enumerate(((0, P), (P, 2 * P))):
                    v = pr[:, t % 2, a:a + n]
                    last = act.activation(v, v, ACT.Exp, bias=pmx[:, t % 2, c:c + 1], accum_out=psm[:, t % 2, c:c + 1])
                last.then_inc(S["p_exp"], 1)

            def p_vcopy(t):
                act.wait_ge(S["p_v"], t + 1)
                if t >= 2:
                    act.wait_ge(S["p_o"], t - 1)
                act.activation(vnat[:, t % 2, :], p_bank(t, 1)[:, 0:2 * P], ACT.Copy).then_inc(S["p_vcopy"], 1)

            def p_tcopy(t):
                act.wait_ge(S["p_t"], t + 1)
                act.activation(prt[:, t % 2, :], p_bank(t, 2)[:, 0:3 * P], ACT.Copy).then_inc(S["p_tcopy"], 1)

            def p_high(t):
                act.wait_ge(S["p_o"], t + 1)
                act.activation(h_hi[:, t, 0:TP], p_bank(t, 3)[:, 0:TP], ACT.Copy).then_inc(S["p_high"], 1)

            def steps(t):
                p_vcopy(t)
                p_exp(t)
                p_tcopy(t)
                p_vcopy(t + 1)
                p_exp(t + 1)
                p_high(t)
                p_tcopy(t + 1)

            for c in range(4):
                act.wait_ge(S["vn_sum"], c + 1)
                act.activation(v_new[:, c * 512:(c + 1) * 512], bank[6][0:TS, :], ACT.Copy).then_inc(S["vn_ready"], 1)

            def group(kind, g):
                kd = KIND[kind]
                n, G = kd["n"], GROUPS * kind + g + 1
                t0 = 4 * (G - 1)
                steps(t0)
                p_high(t0 + 1)
                act.wait_ge(S["nm_ready"], G)
                if kind == 0:
                    dst = ps[:, 0:1024].rearrange("p (a b) -> p a b", a=2)
                    act.activation(dst, pairs[0][:, :, :], ACT.Exp, bias=nm[:, 0:1], accum_out=sm[:, 0:1])
                else:
                    act.activation(ps[:, 0:W_MAIN], ps[:, 0:W_MAIN], ACT.Exp, bias=nm[:, 0:1], accum_out=sm[:, 0:1])
                act.activation(ps[:, 1024:1024 + TS], ps[:, 1024:1024 + TS], ACT.Exp, bias=nm[:, 0:1],
                               accum_out=sm[:, 1:2]).then_inc(S["exp_ready"], 1)
                act.wait_ge(S["pt_sum"], G)
                act.activation(pst[:, 0:4, :].rearrange("p a b -> p (a b)"), bank[3], ACT.Copy)
                act.activation(pst[:, 4:n, :].rearrange("p a b -> p (a b)"), bank[4][:, 0:(n - 4) * P], ACT.Copy)
                act.activation(pst[0:TS, 8, :], bank[5][0:TS, 0:P], ACT.Copy).then_inc(S["pt_ready"], 1)
                steps(t0 + 2)
                act.wait_ge(S["kv_used"], quad0[kind] + RING + 2 * n + 2 * n * g)
                act.wait_ge(S["r_ready"], G)
                act.activation(ps[:, 0:1024].rearrange("p (a b) -> p a b", a=2), pairs[3][:, :, :], ACT.Copy,
                               scale=rs[:, 0:1]).then_inc(S["os_ready"], 1)
                p_high(t0 + 3)
                act.wait_ge(S["ot_ready"], G)
                for c in range(2):
                    dst = h_hi[:, kind * HEADS + 4 * c:kind * HEADS + 4 * c + 4, TP + 16 * g:TP + 16 * g + 16]
                    last = act.activation(dst.rearrange("p h (j s) -> p h j s", s=NS), own_rows(c), ACT.Copy)
                last.then_inc(S["oh_ready"], 1)

            for kind in (0, 1):
                for g in range(GROUPS):
                    group(kind, g)

            act.wait_ge(S["ol_ready"], 2 * GROUPS)
            segments([out])
            act.wait_ge(S["acc_b_read"], ffn2.rb)
            squares(2)
            inverse_root(2)
            high_of_h(2)
            segments(segs[segs.index(out) + 1:])

        @block.vector
        def _(dve):
            ch = Chain(dve, S["dve_chain"])
            par3 = par[:, :].rearrange("p (t c) -> p t c", c=NC)

            def split_low(seg, j, i):
                n, r = seg.n0 + j, (seg.n0 + j) % 2
                half = KT // 2 * P
                for q, (a, b) in enumerate(((0, half), (half, seg.nk * P))):
                    dve.wait_ge(S["hi_ready"], 2 * n + q + 1 + 4 * i)
                    dve.tensor_tensor(w_lo[:, r, a:b], raw[:, r, a:b], w_hi[:, r, a:b].bitcast(F32),
                                      ALU.subtract).then_inc(S["lo_ready"], 1)

            def refine(ssum, y, m, t, scale):
                ch.link(dve.tensor_scalar(m, ssum, scale, EPS, ALU.mult, ALU.add))
                ch.link(dve.tensor_tensor(t, y, y, ALU.mult))
                ch.link(dve.scalar_tensor_tensor(t, t, -0.5, m, ALU.mult, ALU.mult))
                ch.link(dve.scalar_tensor_tensor(y, t, 1.5, y, ALU.add, ALU.mult))

            def samples(ap):
                return ap.rearrange("p k (b s) -> p k b s", s=NS)

            def modulate(r):
                dve.wait_ge(S["y0_ready"], r + 1)
                refine(ssb[:, 0:T], y0[:, :], ms[:, :], tt[:, :], 1.0 / D)
                sh, a = 3 * r * KT, (3 * r + 1) * KT

                def low(c):
                    dve.wait_ge(S["hhi_ready"], SQR * r + c + 1)
                    dve.tensor_tensor(h_lo[:, SQL * c:SQL * (c + 1), :], hf[:, c % 2, :, :],
                                      h_hi[:, SQL * c:SQL * (c + 1), :].bitcast(F32), ALU.subtract)\
                       .then_inc(S["h_ready"], 1)
                for c in range(SQR):
                    k0 = SQL * c
                    if c >= 2:
                        dve.wait_ge(S["h_ready"], SQR * r + c - 1)
                    ch.link(dve.tensor_tensor(hf[:, c % 2, :, :], x[:, k0:k0 + SQL, :],
                                              y0[:, :].unsqueeze(1).to_broadcast([P, SQL, T]), ALU.mult))
                    hs = samples(hf[:, c % 2, :, TP:T])
                    for k in range(SQL):
                        q = hf[:, c % 2, k, 0:TP]
                        last = dve.tensor_scalar(q, q, par[:, (a + k0 + k) * NC:(a + k0 + k) * NC + 1],
                                                 par[:, (sh + k0 + k) * NC:(sh + k0 + k) * NC + 1],
                                                 ALU.mult, ALU.add)
                    ch.link(dve.tensor_tensor(hs, hs, par3[:, a + k0:a + k0 + SQL, 1:NC].unsqueeze(3)
                                              .to_broadcast([P, SQL, NB, NS]), ALU.mult))
                    dve.tensor_tensor(hs, hs, par3[:, sh + k0:sh + k0 + SQL, 1:NC].unsqueeze(3)
                                      .to_broadcast([P, SQL, NB, NS]), ALU.add).then_inc(S["hf_ready"], 1)
                    if c:
                        low(c - 1)
                low(SQR - 1)

            def ada_finish(group, t0, n):
                dve.wait_ge(S["ada_sel"], group + 1)
                dve.tensor_tensor(par3[:, bass.ds(t0, n), :],
                                  ada_selp[:, 0:n * NC].rearrange("p (t c) -> p t c", c=NC),
                                  ba[:, bass.ds(t0, n)].unsqueeze(2).to_broadcast([P, n, NC]), ALU.add)\
                   .then_inc(S["ada_fin"], 1)

            def gain(r, groups):
                dve.wait_ge(S["ada_fin"], groups)
                a = par3[:, (3 * r + 1) * KT:(3 * r + 2) * KT, :]
                ch.link(dve.scalar_tensor_tensor(a, a, 1.0, gv[:, r, :].unsqueeze(2).to_broadcast([P, KT, NC]),
                                                 ALU.add, ALU.mult))

            def half_gate(p, groups):
                dve.wait_ge(S["ada_fin"], groups)
                a = par[:, p * KT * NC:(p + 1) * KT * NC]
                ch.link(dve.tensor_scalar(a, a, 0.5, None, ALU.mult))

            ch.link(dve.memset(sc32[:, :, NC:32], 0.0))
            ch.link(dve.memset(eps[:, :], EPS))
            dve.wait_ge(S["ld_small"], 96)
            ada_finish(0, 0, 4)
            with dve.Fori(1, 2 * KT // 4) as i:
                ada_finish(i, 4 * i, 4)
            gain(0, 8)
            modulate(0)
            for k in range(4):
                dve.tensor_scalar(nw[:, 8 * k:8 * k + 8], nw4[:, k:k + 1].to_broadcast([P, 8]), SCALE if k % 2 == 0 else 1.0,
                                  None, ALU.mult)
            dve.wait_ge(S["rev_sum"], 1)
            dve.tensor_tensor(rev[:, :], bank[5][0:HEADS, 0:REV], adr[:, :], ALU.add).then_inc(S["rev_ready"], 1)
            def add_gated(seg, j, i):
                bank = (acc_a, acc_b)[j]
                n = seg.n0 + j
                dve.wait_ge(S["w_used"], 2 * (n + 1) + 4 * i)
                d = seg.d0 + j + 2 * i
                gate = seg.gate * KT + d
                xs = x[:, bass.ds(d, 1), TP:T].rearrange("p k (b s) -> p (k b) s", s=NS)
                xp = x[:, bass.ds(d, 1), 0:TP].rearrange("p k t -> p (k t)")
                ch.link(dve.tensor_tensor(tmps[:, j, :, :], bank[:, TP:T].rearrange("p (b s) -> p b s", s=NS),
                                          par[:, bass.ds(gate * NC + 1, NB)].unsqueeze(2).to_broadcast([P, NB, NS]),
                                          ALU.mult))
                ch.link(dve.tensor_tensor(xs, xs, tmps[:, j, :, :], ALU.add))
                dve.scalar_tensor_tensor(xp, bank[:, 0:TP], par[:, bass.ds(gate * NC, 1)], xp,
                                         ALU.mult, ALU.add).then_inc(S["acc_b_read" if j else "acc_a_read"], 1)

            def gated_unit(seg, i):
                dve.wait_ge(S["w_used"], 2 * (seg.n0 + 2) + 4 * i)
                dve.wait_ge(S["acc_a_read"], seg.ra + 1 + i)
                dve.tensor_tensor(gf[:, :], su[:, :], acc_b[:, 0:T], ALU.mult).then_inc(S["acc_b_read"], 1)
                dve.wait_ge(S["acc_b_read"], seg.rb + 1 + i)
                gh, gl = g_hi[:, bass.ds(i, 1), :], g_lo[:, bass.ds(i, 1), :]
                gg = gf[:, :].unsqueeze(1)
                ch.link(dve.tensor_copy(gh, gg))
                dve.tensor_tensor(gl, gg, gh.bitcast(F32), ALU.subtract).then_inc(S["g_ready"], 1)

            def after_b(seg, i):
                if seg.kind == "up":
                    gated_unit(seg, i)
                elif seg.kind == "down":
                    add_gated(seg, 1, i)

            LINKS = {"up": 1, "down": 4}

            def body(seg, i, lag):
                split_low(seg, 0, i)
                if lag:
                    after_b(seg, i - 1)
                split_low(seg, 1, i)
                if seg.ada:
                    ada_finish(8 + seg.pair0 + i, 2 * KT + 2 * seg.pair0 + 2 * i, 2)
                if seg.kind == "down":
                    add_gated(seg, 0, i)

            def segments(some):
                for seg in some:
                    if seg.gate == 2 and seg.b0 == CHUNKS[0][1]:
                        half_gate(2, 8 + 8)
                    body(seg, 0, False)
                    run(seg, dve, lambda i, seg=seg: body(seg, i, True), 1, ch, LINKS[seg.kind])
                    after_b(seg, seg.bodies - 1)

            segments(ffn1)
            gain(1, PAIRS)
            modulate(1)

            qk, vv = segs[segs.index(fa) + 1:segs.index(fa) + 3]
            split_low(fa, 0, 0)

            def z_copy(b, j):
                dve.wait_ge(S["w_used"], 2 * (qk.n0 + j + 1) + 4 * b)
                dve.tensor_copy(z[:, bass.ds(2 * b + j, 1), :], (acc_a, acc_b)[j][:, 0:T].unsqueeze(1))\
                   .then_inc(S["acc_b_read" if j else "acc_a_read"], 1)

            def head_norm(b):
                dve.wait_ge(S["hy_ready"], b + 1)
                refine(ss2[:, :, 0:T], yh[:, :, :], mh[:, :, :], th[:, :, :], 1.0 / HD)
                for j in range(2):
                    zt = z[:, bass.ds(2 * b + j, 1), :]
                    last = dve.scalar_tensor_tensor(zt, zt, nw[:, bass.ds(2 * b + j, 1)], yh[:, j, :].unsqueeze(1),
                                                    ALU.mult, ALU.mult)
                last.then_inc(S["head_ready"], 1)

            def win_body(b, j):
                seg, i = (qk, b) if j < 16 else (vv, b - 16)
                split_low(seg, 0, i)
                if j >= 1:
                    z_copy(b - 1, 1)
                split_low(seg, 1, i)
                if 2 <= j <= 17:
                    head_norm(b - 2)
                z_copy(b, 0)

            def gate_sum():
                dve.wait_ge(S["w_used"], 2 * (fa.n0 + 1))
                dve.tensor_scalar(fa_sb[:, :], bank[2][0:HEADS, 0:T], bfs[:, 0:1], None, ALU.add)\
                   .then_inc(S["fa_ready"], 1)
            win_bodies(dve, win_body, ch, (4, 0), gate_sum)
            z_copy(23, 1)
            dve.wait_ge(S["fe_ready"], 1)
            dve.scalar_tensor_tensor(lf[:, :], fa_sb[:, :], 0.0, fe[:, :], ALU.min, ALU.subtract)\
               .then_inc(S["lf_ready"], 1)
            dve.wait_ge(S["lft_sum"], 1)
            dve.tensor_copy(lft[:, 0:2, :], bank[7][:, 0:2 * HEADS].rearrange("p (t h) -> p t h", t=2))
            ch.link(dve.tensor_copy(lft[0:TS, 2, :], bank[7][0:TS, 2 * HEADS:3 * HEADS]))
            dve.tensor_copy(lfn_w[:, :].rearrange("p (j h q) -> p j h q", j=GB, q=NS),
                            lft[0:TS, 2, :].unsqueeze(1).unsqueeze(3).to_broadcast([TS, GB, HEADS, NS]))\
               .then_inc(S["lft_ready"], 1)
            dve.wait_ge(S["ncum_sum"], 1)
            dve.tensor_copy(ncum[:, :], bank[6][0:HEADS, 0:TP]).then_inc(S["ncum_ready"], 1)

            def p_low(t):
                dve.wait_ge(S["p_high"], t + 1)
                dve.tensor_tensor(h_lo[:, t, 0:TP], p_bank(t, 3)[:, 0:TP], h_hi[:, t, 0:TP].bitcast(F32),
                                  ALU.subtract).then_inc(S["p_low"], 1)

            def p_max(t):
                r = t % 2
                if t == HEADS:
                    dve.wait_ge(S["toe_landed"], 16)
                bias = big[:, C_CAUSAL:C_CAUSAL + 2 * P] if t < HEADS else toe[:, t % HEADS, :]
                dve.wait_ge(S["p_s"], t + 1)
                if t >= 2:
                    dve.wait_ge(S["p_t"], t - 1)
                scores = p_bank(t, 0)
                dve.tensor_tensor(pr[:, r, 0:P], scores[:, 0:P], bias[:, P:2 * P], ALU.add)
                ch.link(dve.tensor_tensor(pr[:, r, P:3 * P], scores[:, P:3 * P], bias, ALU.add))
                dve.tensor_reduce(pmx[:, r, 0:1], pr[:, r, 0:P], AX.X, ALU.max, negate=True)
                dve.tensor_reduce(pmx[:, r, 1:2], pr[:, r, P:3 * P], AX.X, ALU.max, negate=True)\
                   .then_inc(S["p_max"], 1)

            def p_scale(t):
                r = t % 2
                dve.wait_ge(S["p_exp"], t + 1)
                ch.link(dve.reciprocal(psm[:, r, :], psm[:, r, :]))
                dve.tensor_scalar(pr[:, r, 0:P], pr[:, r, 0:P], psm[:, r, 0:1], None, ALU.mult)
                dve.tensor_scalar(pr[:, r, P:3 * P], pr[:, r, P:3 * P], psm[:, r, 1:2], None, ALU.mult)\
                   .then_inc(S["p_scaled"], 1)

            def steps(t):
                p_max(t)
                p_scale(t)
                p_max(t + 1)
                p_scale(t + 1)
                p_low(t)

            dve.wait_ge(S["lf_landed"], 16 * NB * PAGES)
            ch.link(dve.tensor_tensor(bias_w[:, :].rearrange("p (j h q) -> p j h q", j=GB, q=NS),
                                      rbr[:, :].unsqueeze(1).unsqueeze(3).to_broadcast([P, GB, HEADS, NS]),
                                      big[:, C_DELTA:C_DELTA + NS].unsqueeze(1).unsqueeze(1)
                                      .to_broadcast([P, GB, HEADS, NS]), ALU.mult))
            dve.memset(qbd[0][:, :, :], 0.0)
            ch.link(dve.memset(qbd[1][:, :, :], 0.0))

            def moving_parts(kind, g):
                kd = KIND[kind]
                for j in range(GB):
                    b = TP + 16 * g + NS * j
                    last = dve.tensor_copy(qbd[j // 2][:, j % 2, :].rearrange("p (h x) -> p h x", x=32 + NS)[:, :, 0:NS],
                                           z[:, kd["q"]:kd["q"] + HEADS, b:b + NS])
                    if kind == 0:
                        a = (GB * g + j) * PAGES
                        last = dve.tensor_copy(lfr[:, :, 32 * j:32 * j + 32].rearrange("p a (h q) -> p a h q", q=NS),
                                               lfc[:, a:a + PAGES, :].unsqueeze(3).to_broadcast([P, PAGES, HEADS, NS]))
                last.then_inc(S["qbd_ready"], 1)

            def group(kind, g):
                kd = KIND[kind]
                n, G = kd["n"], GROUPS * kind + g + 1
                t0 = 4 * (G - 1)
                steps(t0)
                dve.wait_ge(S["kv_used"], quad0[kind] + RING + n + 2 * n * g)
                ch.link(dve.tensor_tensor(ps[:, 1024:1024 + TS], bank[2][:, 0:TS],
                                          big[:, kd["new"] + TS * g:kd["new"] + TS * g + TS], ALU.add))
                dve.tensor_reduce(mx[:, 1:2], ps[:, 1024:1024 + TS], AX.X, ALU.max)
                if kind == 0:
                    ch.link(dve.tensor_reduce(mx[:, 0:1], pairs[0][:, :, :], AX.XY, ALU.max))
                else:
                    dve.tensor_tensor(ps[:, 0:512], bank[0], big[:, C_LOGN:C_LOGN + 512], ALU.add)
                    ch.link(dve.tensor_tensor(ps[:, 512:W_MAIN], bank[1][:, 0:P], big[:, C_LOGN + 512:C_LOGN + W_MAIN],
                                              ALU.add))
                    ch.link(dve.tensor_reduce(mx[:, 0:1], ps[:, 0:W_MAIN], AX.X, ALU.max))
                dve.tensor_reduce(nm[:, 0:1], mx[:, :], AX.X, ALU.max, negate=True).then_inc(S["nm_ready"], 1)
                p_low(t0 + 1)
                dve.wait_ge(S["exp_ready"], G)
                ch.link(dve.tensor_reduce(sm[:, 0:1], sm[:, :], AX.X, ALU.add))
                dve.reciprocal(rs[:, 0:1], sm[:, 0:1]).then_inc(S["r_ready"], 1)
                if G < 2 * GROUPS:
                    moving_parts(G // GROUPS, G % GROUPS)
                steps(t0 + 2)
                p_low(t0 + 3)
                dve.wait_ge(S["oh_ready"], G)
                for c in range(2):
                    sl = (slice(None), slice(kind * HEADS + 4 * c, kind * HEADS + 4 * c + 4),
                          slice(TP + 16 * g, TP + 16 * g + 16))
                    last = dve.tensor_tensor(h_lo[sl].rearrange("p h (j s) -> p h j s", s=NS), own_rows(c),
                                             h_hi[sl].bitcast(F32).rearrange("p h (j s) -> p h j s", s=NS), ALU.subtract)
                last.then_inc(S["ol_ready"], 1)

            moving_parts(0, 0)
            for kind in (0, 1):
                for g in range(GROUPS):
                    group(kind, g)

            segments([out])
            gain(2, PAIRS)
            half_gate(8, PAIRS)
            modulate(2)
            dve.wait_ge(S["heads_stored"], 5 * 16)
            segments(segs[segs.index(out) + 1:])
            dve.wait_ge(S["acc_b_read"], segs[-1].rb + segs[-1].bodies)
            dve.memset(tmps[:, 1, 0, 0:1], 0.0).then_inc(S["x_done"], 1)


def _tiles(w, k, n):
    return np.ascontiguousarray(w.reshape(k, P, n, P).transpose(2, 1, 0, 3).reshape(n, P, k * P))


def _bucket(dist):
    d = np.maximum(dist, 16).astype(np.float64)
    log_b = np.minimum((16 + np.log(d / 16) / np.log(128.0) * 16).astype(np.int64), 31)
    return np.where(dist < 16, np.maximum(dist, 0), log_b)


def _log_patterns(dist):
    n = sum(((dist >= 0) & (dist % r == 0) & (dist <= w)).astype(np.int64) for w, r in ((128, 1), (512, 4), (2048, 16)))
    return np.where(n > 0, np.log(np.maximum(n, 1)), NEG).astype(np.float32)


def _window_keys():
    early = (16 * np.arange(32)[:, None] + np.arange(NS)[None, :]).reshape(-1)
    return np.concatenate([early, 512 + np.arange(512)]).reshape(WT, P)


def _constants():
    f = np.float32
    eye = np.eye(P, dtype=f)
    sel = np.zeros((P, 16), f)
    for j in range(4):
        sel[32 * j + np.arange(NC), np.arange(NC)] = 1
    small = np.concatenate([eye, np.ones((P, P), f), sel], 1)
    k = np.arange(P)
    band = np.concatenate([np.ones((P, (PAGES - 1) * P), f), (k[:, None] > k[None, :]).astype(f)], 1)
    pos = _window_keys().reshape(-1)
    s = np.arange(NS)
    new = np.arange(TS) % NS
    dist = 1024 + s[:, None] - pos[None, :]
    dist_new = s[:, None] - new[None, :]
    d = np.concatenate([dist, dist_new], 1)
    onehot = np.zeros((NS, 32, d.shape[1]), f)
    onehot[:, :, :] = (_bucket(d)[:, None, :] == np.arange(32)[None, :, None])
    row_q = np.arange(P) % NS
    row_b = np.arange(P) // 32
    addc = _log_patterns(dist)[row_q]
    same = [(np.arange(TS)[None, :] // NS == GB * g + row_b[:, None]) for g in range(2)]
    new_dil = [np.where(m, _log_patterns(dist_new)[row_q], f(NEG)) for m in same]
    new_fox = [np.where(m & (dist_new[row_q] >= 0), f(0), f(NEG)) for m in same]
    causal = np.concatenate([np.zeros((P, P), f), np.where(k[None, :] <= k[:, None], f(0), f(NEG))], 1)
    negtri = np.concatenate([-(k[:, None] <= k[None, :]).astype(f), -np.ones((P, P), f)], 1)
    delta = (np.arange(P)[:, None] // 32 == s[None, :]).astype(f)
    t = np.arange(TS)
    ntri = np.zeros((P, TS), f)
    ntri[:TS] = -((t[:, None] // NS == t[None, :] // NS) & (t[:, None] <= t[None, :])).astype(f)
    big = np.concatenate([band, onehot.reshape(P, -1), addc, *new_dil, *new_fox, causal, negtri, delta, ntri], 1)
    back = 255 - np.arange(383)
    oh_rev = (_bucket(back)[None, :] == np.arange(32)[:, None]).astype(f) * (back >= 0)[None, :].astype(f)
    lp = _log_patterns(back)
    add_rev = np.broadcast_to(lp, (HEADS, 383)).astype(f)
    selh = np.zeros((HEADS, HEADS, P), f)
    selh[np.arange(HEADS), np.arange(HEADS)] = 1
    return small.astype(f), np.ascontiguousarray(big.astype(f)), np.ascontiguousarray(oh_rev.astype(f)), \
        np.ascontiguousarray(add_rev), selh.reshape(HEADS, HEADS * P)


def _lay_out(i):
    a = {k: np.asarray(v) for k, v in i.items()}
    cat = np.concatenate

    def feat(v):
        return np.ascontiguousarray(v.reshape(-1, KT, P).transpose(2, 1, 0))

    def up(w1, w3):
        return np.ascontiguousarray(np.stack([_tiles(w1[0], KT, FF), _tiles(w3[0], KT, FF)], 1).reshape(2 * FF, P, KT * P))

    w = a["w_in"][0]
    W = HEADS * HD
    fa = 3 * W
    cols = [w[:, fa:fa + P]] + [w[:, o:o + W] for o in (0, W, fa + HEADS, fa + HEADS + W, 2 * W, fa + HEADS + 2 * W)]
    small, big, ohrev, addrev, selh = _constants()
    keys = _window_keys()
    out = dict(
        xT=feat(cat([a["x_prompt"].reshape(TP, D), a["x_sample"].reshape(TS, D)])),
        cT=feat(cat([a["c_prompt"], a["c_sample"]])),
        gT=np.ascontiguousarray(np.stack([a[n][0].reshape(KT, P).T for n in ("g_ffn1", "g_mix", "g_ffn2")], 1)),
        bada=np.ascontiguousarray(a["b_ada"][0].reshape(ADA, P).T),
        nwT=np.ascontiguousarray(np.stack([a[n][0] for n in ("qn_fox", "kn_fox", "qn_dil", "kn_dil")], 1)),
        bfg=np.ascontiguousarray(a["b_forget"].reshape(HEADS, 1)),
        relb=np.ascontiguousarray(a["rel_bias"]),
        pt=np.ascontiguousarray(a["page_table"].reshape(1, NB * PAGES)),
        cst=small, cst2=big, ohrev=ohrev, addrev=addrev, selh=selh,
        w_ada=_tiles(a["w_ada"][0], KT, ADA),
        w13_1=up(a["w1_ffn1"], a["w3_ffn1"]), w2_1=_tiles(a["w2_ffn1"][0], FF, KT),
        w_in=_tiles(cat(cols, 1), KT, 49), w_out=_tiles(a["w_out"][0], KT, KT),
        w13_2=up(a["w1_ffn2"], a["w3_ffn2"]), w2_2=_tiles(a["w2_ffn2"][0], FF, KT),
        kpool=np.ascontiguousarray(a["cache_fox_k"][0].transpose(0, 3, 2, 1).reshape(POOL, HD, HEADS * PAGE)),
        vpool=np.ascontiguousarray(a["cache_fox_v"][0].reshape(POOL, PAGE, W)),
        lfpool=np.ascontiguousarray(a["cache_fox_logf"][0]),
        wink=np.ascontiguousarray(a["cache_win_k"][0][:, keys].transpose(0, 1, 4, 3, 2).reshape(NB, WT, HD, HEADS * P)),
        winv=np.ascontiguousarray(a["cache_win_v"][0][:, keys].reshape(NB, WT, P, W)),
    )
    return out


_OUTS = dict(y_out=(P, KT, T), kv_out=(4, P, HEADS, T), lf_out=(HEADS, T))


def kernel(**inputs):
    import concourse.bacc as _bacc
    from concourse.bass_utils import run_bass_kernel_spmd as _run

    arrays = _lay_out(inputs)
    nc = _bacc.Bacc("TRN2", target_bir_lowering=False, num_devices=1)
    args = [nc.dram_tensor(f"in_{n}_dram", v.shape, mybir.dt.from_np(v.dtype), kind="ExternalInput").ap()
            for n, v in arrays.items()]
    args += [nc.dram_tensor(f"out_{n}_dram", s, F32, kind="ExternalOutput").ap() for n, s in _OUTS.items()]
    decoder_layer(nc, *args)
    r = _run(nc, [{f"in_{n}_dram": v for n, v in arrays.items()}], core_ids=[0])
    y, kv, lf = (r.results[0][f"out_{n}_dram"] for n in _OUTS)
    y = y.transpose(2, 1, 0).reshape(T, D)
    kv = kv.transpose(0, 3, 2, 1)
    lf = lf.T

    def prompt(v):
        return np.ascontiguousarray(v[None, None, :TP])

    def sample(v):
        return np.ascontiguousarray(v[TP:].reshape((1, NB, NS) + v.shape[1:]))

    kf, kd, vf, vd = kv
    return (np.ascontiguousarray(y[None, :TP]), np.ascontiguousarray(y[TP:].reshape(NB, NS, D)),
            prompt(kf), prompt(vf), prompt(lf), prompt(kd), prompt(vd),
            sample(kf), sample(vf), sample(lf), sample(kd), sample(vd))
```

```python
from contextlib import ExitStack

import numpy as np

import concourse.bass as bass
from concourse import mybir

F32 = mybir.dt.float32
F32R = mybir.dt.float32r
I32 = mybir.dt.int32
ALU = mybir.AluOpType
ACT = mybir.ActivationFunctionType
AX = mybir.AxisListType

P = 128
D = 2048
KT = D // P
HEADS, HD = 8, 128
TP, NB, NS = 256, 8, 4
TS = NB * NS
T = TP + TS
FF = 43
CHUNKS = ((0, 15), (15, 14), (29, 14))
NPAR = 9
ADA = NPAR * KT
NC = NB + 1
PAGE, PAGES = 128, 8
POOL = 80
WT = 5
GB = 4
EPS = 1e-6
SCALE = HD ** -0.5
NEG = -1.0e30
SQR, SQL = KT // 4, 4

C_ID, C_ONE, C_SEL, C_SMALL = 0, 128, 256, 272
W_MAIN = WT * P
C_BAND = 0
C_BUCKET = C_BAND + PAGES * PAGE
C_LOGN = C_BUCKET + W_MAIN + TS
C_NEW_DIL = C_LOGN + W_MAIN
C_NEW_FOX = C_NEW_DIL + 2 * TS
C_CAUSAL = C_NEW_FOX + 2 * TS
C_NEGTRI = C_CAUSAL + 2 * P
C_DELTA = C_NEGTRI + 2 * P
C_NTRI = C_DELTA + NS
C_BIG = C_NTRI + TS
REV = 383
GROUPS = NB // GB


class Seg:

    def __init__(self, kind, bodies, src, f=0, c=0, nk=KT, ada=False, moving="h", gate=None, ff0=0, d0=0,
                 k0=0, z0=0, norm=None, squares=False):
        self.kind, self.bodies, self.src = kind, bodies, src
        self.f, self.c, self.nk, self.ada = f, c, nk, ada
        self.moving, self.gate = moving, gate
        self.ff0, self.d0, self.k0, self.z0 = ff0, d0, k0, z0
        self.norm, self.squares = norm, squares


def plan():
    segs = []

    def ffn(f):
        for c, (t0, n) in enumerate(CHUNKS):
            segs.append(Seg("up", n, f=f, c=c, ff0=t0, ada=f == 0, src=("w13", f),
                            norm=(0, 2)[f] if c == 0 else None))
            runs = [(0, 8, False)] if f or c == 2 else [(0, 8, True)] if c == 0 else [(0, 5, True), (5, 3, False)]
            for b, m, ada in runs:
                segs.append(Seg("down", m, f=f, c=c, nk=n, moving="g", ada=ada, d0=2 * b, k0=t0,
                                gate=2 if f == 0 else 8, src=("w2", f), squares=f == 0 and c == 2))

    ffn(0)
    segs.append(Seg("win", 16, src=("w_in", 0), z0=0, norm=1))
    segs.append(Seg("fa", 0, src=("w_in", 0)))
    segs.append(Seg("win", 8, src=("w_in", 0), z0=32))
    segs.append(Seg("down", 8, f=0, gate=5, src=("w_out", 0), squares=True))
    ffn(1)
    slot = body = ra = rb = pair = ups = 0
    sqs = SQR
    for s in segs:
        s.n0, s.b0, s.ra, s.rb, s.pair0, s.up0, s.sq0 = slot, body, ra, rb, pair, ups, sqs
        sqs += s.bodies if s.squares else 0
        slot += 2 * s.bodies + (s.kind == "fa")
        body += s.bodies
        ra += s.bodies
        rb += s.bodies
        pair += s.bodies if s.ada else 0
        ups += s.bodies if s.kind == "up" else 0
    assert 2 * pair == ADA - 2 * KT
    return segs


class Chain:

    def __init__(self, eng, sem):
        self.eng, self.sem, self.n, self.i, self.per = eng, sem, 0, None, 0

    def link(self, ins):
        ins.then_inc(self.sem, 1)
        self.n += 1
        self.eng.wait_ge(self.sem, self.n if self.i is None else self.n + self.i * self.per)

    def loop(self, i, first, per):
        self.i, self.per, self.first, self.start = i, per, first, self.n
        self.n = self.start - first * per if not isinstance(i, int) else self.n
        return self

    def end(self, last):
        assert self.n - (self.start - self.first * self.per) == self.per, (self.n, self.start, self.per)
        self.n = self.start + self.per * (last - self.first)
        self.i = None


def decoder_layer(nc, xT, cT, gT, bada, nwT, bfg, relb, pt, cst, cst2, ohrev, addrev, selh,
                  w_ada, w13_1, w2_1, w_in, w_out, w13_2, w2_2, kpool, vpool, lfpool, wink, winv,
                  y_out, kv_out, lf_out):
    segs = plan()
    ffn1 = [s for s in segs if s.kind in ("up", "down") and s.b0 < 67]
    WS = {("w13", 0): w13_1, ("w13", 1): w13_2, ("w2", 0): w2_1, ("w2", 1): w2_2,
          ("w_in", 0): w_in, ("w_out", 0): w_out}

    with ExitStack() as ctx:
        top = [16512]

        def at(name, shape, dt, off):
            return nc.alloc_sbuf_tensor_at(name, shape, dt, offset=off)

        def sb(name, shape, dt=F32):
            n = int(np.prod(shape[1:])) * 4
            t = at(name, shape, dt, top[0])
            top[0] += -(-n // 32) * 32
            return t

        def sem(name):
            return ctx.enter_context(nc.semaphore(name))

        x = sb("x", [P, KT, T])
        h0 = top[0]
        h_hi, h_lo = sb("h_hi", [P, KT, T], F32R), sb("h_lo", [P, KT, T], F32R)
        par = sb("par", [P, ADA * NC])
        c0 = top[0]
        sc32 = sb("sc32", [P, KT, 32])
        lf = at("lf", [HEADS, T], F32, c0)
        cs = sb("cs", [P, C_SMALL])
        gv = sb("gv", [P, 3, KT])
        ba = sb("ba", [P, ADA])
        nw4 = sb("nw4", [P, 4])
        nw = sb("nw", [P, 32])
        eps = sb("eps", [P, 1])
        ident, ones, sel9 = cs[:, C_ID:C_ID + P], cs[:, C_ONE:C_ONE + P], cs[:, C_SEL:C_SEL + NC]
        rings0 = top[0]
        raw = sb("raw", [P, 2, KT * P])
        w_hi, w_lo = sb("w_hi", [P, 2, KT * P], F32R), sb("w_lo", [P, 2, KT * P], F32R)
        mix0 = top[0]
        g_hi, g_lo = sb("g_hi", [P, 15, T], F32R), sb("g_lo", [P, 15, T], F32R)
        adaw = sb("adaw", [P, 2, KT * P])
        part_sb = sb("part_sb", [P, 4 * P])
        su, gf = sb("su", [P, T]), sb("gf", [P, T])
        hf = sb("hf", [P, 2, SQL, T])
        sq = sb("sq", [P, 2, SQL, T])
        tmps = sb("tmps", [P, 2, NB, NS])
        sq0 = top[0] - 2 * SQL * T * 4 - 2 * TS * 4
        sq_sum = at("sq_sum", [P, T], F32, sq0 + T * 4)
        y0, ms, tt = (at(n, [P, T], F32, sq0 + k * T * 4) for k, n in enumerate(("y0", "ms", "tt")))
        rev = at("rev", [HEADS, REV], F32, sq0 + 3 * T * 4)
        fa_sb, fe = at("fa_sb", [HEADS, T], F32, sq0 + 5 * T * 4), at("fe", [HEADS, T], F32, sq0 + 6 * T * 4)
        adax = at("adax", [P, 4, KT * P], F32, mix0)
        assert 4 * KT * P * 4 <= 2 * 15 * T * 4
        big = sb("big", [P, C_BIG])
        lfc = sb("lfc", [P, NB * PAGES, HEADS])
        pages = sb("pages", [1, NB * PAGES], I32)
        rbr = sb("rbr", [P, HEADS])
        v_new = sb("v_new", [TS, 2 * HEADS * HD])
        vn0 = top[0] - 2 * HEADS * HD * 4
        ohr = at("ohr", [32, REV], F32, vn0 + 4096)
        adr = at("adr", [HEADS, REV], F32, vn0 + 5632)
        z = at("z", [P, 6 * HEADS, T], F32, mix0)
        hf0 = mix0 + 6 * HEADS * T * 4
        assert hf0 <= top[0]
        yh = at("yh", [P, 2, T], F32, hf0)
        mh = at("mh", [P, 2, T], F32, hf0 + 2 * T * 4)
        th = at("th", [P, 2, T], F32, hf0 + 4 * T * 4)
        pr = at("pr", [P, 2, 3 * P], F32, hf0)
        prt = at("prt", [P, 2, 3 * P], F32, hf0 + 3072)
        sel0 = hf0 + 6 * T * 4
        selw = at("selw", [HEADS, HEADS * P], F32, sel0)
        ncum = at("ncum", [HEADS, TP], F32, sel0 + 4096)
        toe = at("toe", [P, HEADS, 2 * P], F32, sel0)
        vnat = at("vnat", [P, 2, 2 * P], F32, sel0 + 8192)
        bias_w = at("bias_w", [P, P], F32, sel0 + 10240)
        assert sel0 + 10752 <= hf0 + 2 * 2 * SQL * T * 4
        def quad(name, *offs):
            n = GB // len(offs)
            parts = [at(f"{name}_{i}", [P, n, HEADS * P], F32, o) for i, o in enumerate(offs)]
            return [parts[j // n][:, j % n, :] for j in range(GB)]
        half = HEADS * T * 4
        ring = [quad("kv_raw", rings0), quad("kv_high", rings0 + 16384)]
        first_v = at("kv_first_v", [P, 2, HEADS * P], F32, vn0)
        first = [first_v[:, 0, :], first_v[:, 1, :], at("kv_first_a", [P, HEADS * P], F32, hf0)[:, :],
                 at("kv_first_b", [P, HEADS * P], F32, sel0 + 5120)[:, :]]
        third = [quad("kv_h", h0 + half, h0 + 3 * half), quad("kv_z", mix0)]
        assert GB // 2 * HEADS * P * 4 <= half

        def kv(m, j):
            return (ring + [third[m >= GROUPS * 2 * PAGES]])[(m - 1) % 3][j] if m else first[j]
        over = rings0 + 32768
        ps = at("ps", [P, 1024 + TS], F32, over)
        pst = at("pst", [P, 9, P], F32, over + 4224)
        lfr = at("lfr", [P, PAGES, P], F32, over + 8832)
        lfn_w = at("lfn_w", [TS, P], F32, over + 12928)
        qbd = [sb("qbd0", [P, 2, 288]), at("qbd1", [P, 2, 288], F32, over + 13440)]
        assert 32768 + 13440 + 2304 <= 6 * KT * P * 4
        lft = at("lft", [P, 3, HEADS], F32, c0 + T * 4)
        bfs = sb("bfs", [HEADS, 1])
        rbs = sb("rbs", [32, HEADS])
        mx, nm, sm, rs = sb("mx", [P, 2]), sb("nm", [P, 2]), sb("sm", [P, 2]), sb("rs", [P, 2])
        pmx, psm = sb("pmx", [P, 2, 2]), sb("psm", [P, 2, 2])
        rev_dram = nc.dram_tensor("rev_dram", [HEADS, P, REV], F32).ap()

        pairs = [ctx.enter_context(nc.psum_tensor(f"banks{i}", [P, 2, 512], F32)) for i in range(4)]
        bank = [pairs[i // 2][:, i % 2, :] for i in range(8)]
        acc_a, acc_b, ada_part, ada_selp, ssb = bank[0], bank[1], bank[2], bank[3], bank[4]
        ss2 = pairs[2]


        names = """ld_small ld_x w_landed0 w_landed1 hi_ready lo_ready w_used acc_a_read acc_b_read ada_landed0
            ada_landed1 adax_landed0 adax_landed1 adax_landed2 adax_landed3 ada_used ada_sb ada_sel ada_fin
            c_ready sq_ready sq_used y0_ready hf_ready hhi_ready hn_ready gain_ready h_ready g_ready
            act_chain dve_chain y_stored heads_stored v_stored ss_read ld_att ld_rel ld_selw ld_pages
            lf_landed rev_sum rev_ready rev_stored toe_landed fa_ready fe_ready lf_ready hsq_ready hss_ready
            hy_ready head_ready lft_sum lft_ready ncum_sum ncum_ready p_s p_max p_exp p_scaled p_v p_vcopy
            p_t p_tcopy p_o p_high p_low vn_sum vn_ready kv_landed0 kv_landed1 kv_landed2 kv_first_landed
            kv_used qbd_ready nm_ready exp_ready r_ready pt_sum pt_ready os_ready ot_ready oh_ready ol_ready"""
        S = {n: sem(n) for n in names.split()}
        block = ctx.enter_context(nc.Block())

        def run(seg, eng, body, first=0, chain=None, per=0):
            if first >= seg.bodies:
                return
            with eng.Fori(first, seg.bodies) as i:
                if chain:
                    chain.loop(i, first, per)
                body(i)
            if chain:
                chain.end(seg.bodies)

        KIND = (dict(n=PAGES, q=0, k=8, v=32, new=C_NEW_FOX), dict(n=WT, q=16, k=24, v=40, new=C_NEW_DIL))
        quad0 = (0, GROUPS * 2 * PAGES)
        QUADS = GROUPS * 2 * (PAGES + WT)
        RING = 3
        fa = next(s for s in segs if s.kind == "fa")
        out = next(s for s in segs if s.kind == "down" and s.moving == "h")

        PAIRS = 8 + (ADA - 2 * KT) // 2
        qk, vv = segs[segs.index(fa) - 1], segs[segs.index(fa) + 1]
        WIN = (("one", 0, 1), ("one", 1, 2), ("one", 2, 3), ("loop", 3, 16), ("one", 16, 17), ("one", 17, 18), ("loop", 18, 23), ("one", 23, 24))

        def win_bodies(eng, body, gates, chain=None, per=(0, 0), extra=None):
            for n, (how, a, b) in enumerate(WIN):
                if a == 16:
                    gates()
                if how == "one":
                    body(a, a)
                else:
                    with eng.Fori(a, b) as i:
                        if chain:
                            chain.loop(i, a, per[0] if a < 16 else per[1])
                        body(i, a)
                    if chain:
                        chain.end(b)
                if extra:
                    extra(b)

        P_BANKS = ((5, 7, 6, 3), (0, 1, 2, 5))
        STEPS = (((0, 2, 4, 7), (-1, 1, 4, 7)), ((0, 2, 3, 4), (-1, 0, 2, 4)))
        VN_AFTER = (1, 3, 5, 6)

        def p_bank(t, use):
            return bank[P_BANKS[t // 2 % 2][use]]

        after_norm = [next(s for s in segs if s.norm == r) for r in range(3)]
        SPLITS = ({0: ((0, 0), (0, 1), (1, 0)), 1: ((1, 1),)},) + 2 * ({-2: ((0, 0), (0, 1)), -1: ((1, 0),), 0: ((1, 1),)},)

        def splits(split, r, stage):
            for j, q in SPLITS[r].get(stage, ()):
                split(after_norm[r], j, 0, (q,))

        def own_rows(c):
            b = bank[3 + c]
            return bass.AP(b.tensor, b.offset + 16 * c, [[1024, P], [P + NS, 4], [32, GB], [1, NS]])

        @block.sync
        def _(sp):
            sp.dma_start(sc32[:, :, 0:NC], cT).then_inc(S["ld_small"], 16)
            sp.dma_start(cs[:, :], cst).then_inc(S["ld_small"], 16)
            sp.dma_start(gv[:, :, :], gT).then_inc(S["ld_small"], 16)
            sp.dma_start(ba[:, :], bada).then_inc(S["ld_small"], 16)
            sp.dma_start(nw4[:, :], nwT).then_inc(S["ld_small"], 16)
            sp.dma_start(bfs[:, :], bfg).then_inc(S["ld_small"], 16)

            def ada_group(i, first):
                for j in range(4):
                    if not first:
                        sp.wait_ge(S["ada_used"], 4 * i + j - 3)
                    sp.dma_start(adax[:, j, :], w_ada[bass.ds(4 * i + j, 1), :, :].rearrange("a p n -> p (a n)"))\
                      .then_inc(S[f"adax_landed{j}"], 16)
            ada_group(0, True)
            sp.dma_start(x[:, :, :], xT).then_inc(S["ld_x"], 16)
            with sp.Fori(1, 2 * KT // 4) as i:
                ada_group(i, False)

            def slot(seg, j, i):
                n, r = seg.n0 + j, (seg.n0 + j) % 2
                if not (isinstance(i, int) and n + 2 * i < 2):
                    sp.wait_ge(S["lo_ready"], 2 * (n - 1) + 4 * i)
                src = WS[seg.src]
                if seg.kind == "up":
                    ap = src[bass.ds(2 * (seg.ff0 + i) + j, 1), :, :]
                elif seg.kind == "down":
                    ap = src[bass.ds(seg.d0 + 2 * i + j, 1), :, seg.k0 * P:(seg.k0 + seg.nk) * P]
                elif seg.kind == "win":
                    ap = src[bass.ds(1 + seg.z0 + 2 * i + j, 1), :, :]
                else:
                    ap = src[0:1, :, :]
                sp.dma_start(raw[:, r, 0:seg.nk * P], ap.rearrange("a p n -> p (a n)"))\
                  .then_inc(S[f"w_landed{r}"], 16)

            def ada_pair(seg, i):
                for j in range(2):
                    if not (isinstance(i, int) and seg.pair0 + i == 0):
                        sp.wait_ge(S["ada_used"], 2 * KT + 2 * seg.pair0 + j - 1 + 2 * i)
                    sp.dma_start(adaw[:, j, :], w_ada[bass.ds(2 * KT + 2 * seg.pair0 + 2 * i + j, 1), :, :]
                                 .rearrange("a p n -> p (a n)")).then_inc(S[f"ada_landed{j}"], 16)

            def stream(some):
                for seg in some:
                    def body(i, seg=seg):
                        slot(seg, 0, i)
                        if seg.ada:
                            ada_pair(seg, i)
                        slot(seg, 1, i)
                    peel = 1 if seg.b0 == 0 else 0
                    if peel:
                        body(0)
                    run(seg, sp, body, peel)

            stream(ffn1)
            stream([qk])
            slot(fa, 0, 0)
            stream([vv])
            sp.wait_ge(S["ld_pages"], 16)
            for m in range(QUADS):
                kind = 0 if m < quad0[1] else 1
                n = KIND[kind]["n"]
                g, v, p = (m - quad0[kind]) // (2 * n), (m - quad0[kind]) // n % 2, (m - quad0[kind]) % n
                if m == 0:
                    sp.wait_ge(S["head_ready"], 16)
                    sp.wait_ge(S["lf_ready"], 1)
                if m == 1:
                    sp.wait_ge(S["lo_ready"], 2 * out.n0)
                if m == 2:
                    sp.wait_ge(S["w_used"], 2 * out.n0)
                if kind == 1 and (m - 1) % RING == 2:
                    sp.wait_ge(S["heads_stored"], 4 * 16)
                    sp.wait_ge(S["p_s"], HEADS)
                if kind == 0:
                    pg = [sp.value_load(pages[0:1, (GB * g + j) * PAGES + p:(GB * g + j) * PAGES + p + 1],
                                        min_val=0, max_val=POOL - 1) for j in range(GB)]
                if m > RING:
                    sp.wait_ge(S["kv_used"], m + 1)
                for j in range(GB):
                    if kind == 0:
                        src = (vpool if v else kpool)[bass.ds(pg[j], 1), :, :]
                    else:
                        src = (winv if v else wink)[GB * g + j:GB * g + j + 1, p, :, :]
                    sp.dma_start(kv(m, j), src.rearrange("a p n -> p (a n)"))\
                      .then_inc(S[f"kv_landed{(m - 1) % RING}" if m else "kv_first_landed"], 16)
            sp.wait_ge(S["kv_used"], max(m for m in range(QUADS) if (m - 1) % RING == 0) + RING + 1)
            stream([out])
            stream(segs[segs.index(out) + 1:])
            last, k = segs[-1], KT - 2
            sp.wait_ge(S["acc_b_read"], last.rb + last.bodies - 1)
            sp.dma_start(y_out[:, 0:k, :], x[:, 0:k, :]).then_inc(S["y_stored"], 16)
            sp.wait_ge(S["acc_b_read"], last.rb + last.bodies)
            sp.dma_start(y_out[:, k:KT, :], x[:, k:KT, :]).then_inc(S["y_stored"], 16)
            sp.wait_ge(S["y_stored"], 2 * 16)

        @block.gpsimd
        def _(pool):
            pool.dma_start(pages[:, :], pt).then_inc(S["ld_pages"], 16)
            pool.dma_start(rbs[:, :], relb).then_inc(S["ld_rel"], 16)
            pool.dma_start(ohr[:, :], ohrev).then_inc(S["ld_rel"], 16)
            pool.dma_start(adr[:, :], addrev).then_inc(S["ld_rel"], 16)
            pool.wait_ge(S["h_ready"], 1)
            pool.dma_start(big[:, :], cst2).then_inc(S["ld_att"], 16)
            for q in range(NS):
                pool.dma_start(rbr[32 * q:32 * q + 32, :], relb).then_inc(S["ld_att"], 16)
            pool.wait_ge(S["ld_pages"], 16)
            with pool.Fori(0, NB * PAGES) as i:
                pg = pool.value_load(pages[0:1, bass.ds(i, 1)], min_val=0, max_val=POOL - 1)
                pool.dma_start(lfc[:, bass.ds(i, 1), :], lfpool[bass.ds(pg, 1), :, :].rearrange("a p h -> p a h"))\
                    .then_inc(S["lf_landed"], 16)
            pool.wait_ge(S["rev_ready"], 1)
            pool.dma_start(rev_dram, rev[:, :].unsqueeze(1).to_broadcast([HEADS, P, REV])).then_inc(S["rev_stored"], 16)
            pool.wait_ge(S["rev_stored"], 16)
            pool.wait_ge(S["h_ready"], 2 * SQR)
            pool.dma_start(selw[:, :], selh).then_inc(S["ld_selw"], 16)

            def store_heads(n, z0):
                pool.dma_start(kv_out[n], z[:, z0:z0 + HEADS, :]).then_inc(S["heads_stored"], 16)

            pool.wait_ge(S["head_ready"], 16)
            store_heads(0, 8)
            store_heads(1, 24)
            pool.wait_ge(S["acc_b_read"], vv.rb + HEADS // 2)
            store_heads(2, 32)
            pool.wait_ge(S["lf_ready"], 1)
            pool.dma_start(lf_out, lf[:, :]).then_inc(S["heads_stored"], 16)
            pool.wait_ge(S["p_s"], HEADS)
            pool.dma_start(toe[:, :, :], bass.AP(rev_dram.tensor, P - 1, [[REV - 1, P], [P * REV, HEADS], [1, 2 * P]]))\
                .then_inc(S["toe_landed"], 16)
            pool.wait_ge(S["ol_ready"], 2 * GROUPS)
            pool.dma_start(kv_out[3], z[:, 40:48, :]).then_inc(S["v_stored"], 16)

        @block.tensor
        def _(pe):
            def ada_slot(w, n):
                for k in range(KT // 2):
                    kt, j, a = n % 2 * KT // 2 + k, k % 4, n // 2 * 2 * P
                    last = pe.matmul(ada_part[32 * j:32 * j + 32, a:a + 2 * P], sc32[:, kt, :],
                                     w[:, k * 2 * P:(k + 1) * 2 * P], start=kt < 4, stop=kt >= KT - 4,
                                     tile_position=(0, 32 * j))
                last.then_inc(S["ada_used"], 1)

            def ada_select(group, n):
                pe.wait_ge(S["ada_sb"], group + 1)
                if not (isinstance(group, int) and group == 0):
                    pe.wait_ge(S["ada_fin"], group)
                for c in range(n):
                    last = pe.matmul(ada_selp[:, c * NC:(c + 1) * NC], part_sb[:, c * P:(c + 1) * P], sel9,
                                     start=True, stop=True)
                last.then_inc(S["ada_sel"], 1)

            def square_sum():
                for c in range(SQR):
                    pe.wait_ge(S["sq_ready"], c + 1)
                    for k in range(SQL):
                        last = pe.matmul(ssb[:, 0:T], ones, sq[:, c % 2, k, :], start=c == 0 and k == 0,
                                         stop=c == SQR - 1 and k == SQL - 1)
                    last.then_inc(S["sq_used"], 1)

            def sum_squares(seg):
                pe.wait_ge(S["sq_used"], seg.sq0 + seg.bodies - 1)
                pe.matmul(ssb[:, 0:T], ones, sq_sum[:, :], start=True, stop=False)
                pe.wait_ge(S["sq_ready"], seg.sq0 + seg.bodies)
                pe.matmul(ssb[:, 0:T], ones, sq[:, 0, 2, :], start=False, stop=False)
                pe.matmul(ssb[:, 0:T], ones, sq[:, 1, 2, :], start=False, stop=True).then_inc(S["sq_used"], 1)

            pe.sem_inc(S["kv_used"], RING)
            pe.wait_ge(S["c_ready"], 1)
            def ada_group(i, first):
                if not first:
                    pe.wait_ge(S["ada_sb"], i)
                for j in range(4):
                    pe.wait_ge(S[f"adax_landed{j}"], 16 + 16 * i)
                    ada_slot(adax[:, j, :], j)
                ada_select(i, 4)
            ada_group(0, True)
            with pe.Fori(1, 4) as i:
                ada_group(i, False)
            square_sum()
            with pe.Fori(4, 2 * KT // 4) as i:
                ada_group(i, False)
            pe.wait_ge(S["ld_rel"], 3 * 16)
            pe.matmul(bank[5][0:HEADS, 0:REV], rbs[:, :], ohr[:, :], start=True, stop=True).then_inc(S["rev_sum"], 1)


            def products(bank, r, m_hi, m_lo, a, b, nk, late=None):
                for k in range(a, b):
                    if late and k == nk - 1:
                        pe.wait_ge(S["g_ready"], late)
                    hi, lo = w_hi[:, r, k * P:(k + 1) * P], w_lo[:, r, k * P:(k + 1) * P]
                    pe.matmul(bank[:, 0:T], hi, m_hi[:, k, :], start=k == 0, stop=False)
                    pe.matmul(bank[:, 0:T], hi, m_lo[:, k, :], start=False, stop=False)
                    last = pe.matmul(bank[:, 0:T], lo, m_hi[:, k, :], start=False, stop=k == nk - 1)
                return last

            def tile(seg, j, i, bank, mid=None):
                n, r = seg.n0 + j, (seg.n0 + j) % 2
                m_hi, m_lo = (h_hi, h_lo) if seg.moving == "h" else (g_hi, g_lo)
                late = seg.up0 if seg.moving == "g" else None
                half = KT // 2
                for q, (a, b) in enumerate(((0, half), (half, seg.nk))):
                    pe.wait_ge(S["lo_ready"], 2 * n + q + 1 + 4 * i)
                    products(bank, r, m_hi, m_lo, a, b, seg.nk, late).then_inc(S["w_used"], 1)
                    if q == 0 and mid:
                        mid()

            def ada_body(seg, i):
                g = 8 + seg.pair0 + i
                pe.wait_ge(S["ada_sb"], g)
                for j in range(2):
                    pe.wait_ge(S[f"ada_landed{j}"], 16 * (seg.pair0 + 1) + 16 * i)
                    ada_slot(adaw[:, j, :], j)

            def pair(seg, i, mid_b=None):
                if seg.ada:
                    ada_body(seg, i)
                pe.wait_ge(S["acc_a_read"], seg.ra + i)
                tile(seg, 0, i, acc_a)
                if seg.ada:
                    ada_select(8 + seg.pair0 + i, 2)
                pe.wait_ge(S["acc_b_read"], seg.rb + i)
                tile(seg, 1, i, acc_b, mid_b)

            def first_pair(seg, r):
                if seg.ada:
                    ada_body(seg, 0)
                if seg.b0:
                    pe.wait_ge(S["acc_a_read"], seg.ra)
                    pe.wait_ge(S["acc_b_read"], seg.rb)
                for c in range(SQR):
                    pe.wait_ge(S["h_ready"], SQR * r + c + 1)
                    for j in range(2):
                        s = (seg.n0 + j) % 2
                        if c % 2 == 0:
                            pe.wait_ge(S["lo_ready"], 2 * (seg.n0 + j) + c // 2 + 1)
                        last = products((acc_a, acc_b)[j], s, h_hi, h_lo, SQL * c, SQL * (c + 1), KT)
                        if c == SQR - 1:
                            last.then_inc(S["w_used"], 2)
                if seg.ada:
                    ada_select(8 + seg.pair0, 2)

            def out_pair():
                pe.wait_ge(S["p_max"], 2 * HEADS)
                pe.wait_ge(S["p_vcopy"], 2 * HEADS)
                for q in range(2):
                    if q:
                        pe.wait_ge(S["ol_ready"], 2 * GROUPS)
                    for j in range(2):
                        pe.wait_ge(S["lo_ready"], 2 * (out.n0 + j) + q + 1)
                        last = products((acc_a, acc_b)[j], (out.n0 + j) % 2, h_hi, h_lo, HEADS * q, HEADS * (q + 1), KT)
                        if q:
                            last.then_inc(S["w_used"], 2)

            def segments(some):
                for seg in some:
                    if seg.moving == "g":
                        pe.wait_ge(S["g_ready"], seg.up0 - 1)
                    if seg.norm is not None:
                        first_pair(seg, seg.norm)
                        run(seg, pe, lambda i, seg=seg: pair(seg, i), 1)
                    else:
                        out_pair() if seg is out else pair(seg, 0)
                        run(seg, pe, lambda i, seg=seg: pair(seg, i), 1)
                    if seg.squares:
                        sum_squares(seg)

            segments(ffn1)

            def head_sums(b):
                pe.wait_ge(S["hsq_ready"], b + 1)
                if not (isinstance(b, int) and b == 0):
                    pe.wait_ge(S["ss_read"], 2 + b)
                for j in range(2):
                    last = pe.matmul(ss2[:, j, 0:T], ones, sq[:, j, SQL - 1, :], start=True, stop=True)
                last.then_inc(S["hss_ready"], 1)


            def win_body(b, j):
                seg, i = (qk, b) if j < 16 else (vv, b - 16)
                if j:
                    pair(seg, i, (lambda: head_sums(b - 1)) if j <= 16 else None)
                else:
                    first_pair(qk, 1)

            def turn(dst, src):
                return pe.transpose(dst, src, ident[0:src.shape[0], 0:src.shape[0]])

            def log_forget_sums(b):
                if b == 23:
                    pe.wait_ge(S["lf_ready"], 1)
                    for t in range(2):
                        turn(bank[7][:, t * HEADS:(t + 1) * HEADS], lf[:, t * P:(t + 1) * P])
                    turn(bank[7][0:TS, 2 * HEADS:3 * HEADS], lf[:, TP:T]).then_inc(S["lft_sum"], 1)
                elif b == 24:
                    pe.wait_ge(S["lft_ready"], 1)
                    pe.wait_ge(S["ld_att"], 5 * 16)
                    negtri = big[:, C_NEGTRI:C_NEGTRI + 2 * P]
                    pe.matmul(bank[6][0:HEADS, 0:TP], lft[:, 0, :], negtri, start=True, stop=False)
                    pe.matmul(bank[6][0:HEADS, P:TP], lft[:, 1, :], negtri[:, 0:P], start=False, stop=True)\
                      .then_inc(S["ncum_sum"], 1)
            win_bodies(pe, win_body, lambda: tile(fa, 0, 0, bank[2]), None, None, log_forget_sums)

            pe.wait_ge(S["head_ready"], 16)
            pe.wait_ge(S["acc_b_read"], out.rb)

            def p_scores(t):
                kd, h = KIND[t // HEADS], t % HEADS
                q, k, s_bank = z[:, kd["q"] + h, :], z[:, kd["k"] + h, :], p_bank(t, 0)
                if t:
                    pe.wait_ge(S["p_max"], t)
                else:
                    pe.wait_ge(S["ncum_ready"], 1)
                    pe.wait_ge(S["ld_selw"], 16)
                if t and t % 4 == 0:
                    pe.wait_ge(S["p_low"], t)
                for c, (a, n) in enumerate(((0, P), (P, 2 * P))):
                    fox = t < HEADS
                    last = pe.matmul(s_bank[:, a:a + n], q[:, c * P:(c + 1) * P], k[:, 0:n], start=True, stop=not fox)
                    if fox:
                        last = pe.matmul(s_bank[:, a:a + n], selw[:, h * P:(h + 1) * P], ncum[:, 0:n],
                                         start=False, stop=True)
                last.then_inc(S["p_s"], 1)

            def p_values(t):
                v = z[:, KIND[t // HEADS]["v"] + t % HEADS, :]
                if t:
                    pe.wait_ge(S["p_vcopy"], t)
                turn(p_bank(t, 1)[:, 0:P], v[:, 0:P])
                turn(p_bank(t, 1)[:, P:2 * P], v[:, P:2 * P]).then_inc(S["p_v"], 1)

            def p_turn(t):
                pe.wait_ge(S["p_scaled"], t + 1)
                if t:
                    pe.wait_ge(S["p_tcopy"], t)
                for c in range(3):
                    last = turn(p_bank(t, 2)[:, c * P:(c + 1) * P], pr[:, t % 2, c * P:(c + 1) * P])
                last.then_inc(S["p_t"], 1)

            def p_outputs(t):
                pe.wait_ge(S["p_tcopy"], t + 1)
                pe.wait_ge(S["p_vcopy"], t + 1)
                if t:
                    pe.wait_ge(S["p_low"], t)
                o = p_bank(t, 3)
                pe.matmul(o[:, 0:TP], vnat[:, t % 2, 0:P], prt[:, t % 2, 0:2 * P], start=True, stop=False)
                pe.matmul(o[:, P:TP], vnat[:, t % 2, P:2 * P], prt[:, t % 2, 2 * P:3 * P], start=False, stop=True)\
                  .then_inc(S["p_o"], 1)

            def step(t, i):
                if i == 1:
                    p_turn(t)
                if i < 2:
                    p_scores(t + i)
                    p_values(t + i)
                if i == 2 and t and t % 4 == 0:
                    pe.wait_ge(S["ol_ready"], t // 4)
                if i >= 2:
                    p_outputs(t + i - 2)
                if i == 2:
                    p_turn(t + 1)

            def turn_v_new(c):
                if c:
                    pe.wait_ge(S["vn_ready"], c)
                for h in range(4):
                    last = turn(bank[4][0:TS, h * P:(h + 1) * P], z[:, 32 + 4 * c + h, TP:T])
                last.then_inc(S["vn_sum"], 1)

            def turn_outputs(G):
                pe.wait_ge(S["os_ready"], G)
                for h in range(HEADS):
                    last = turn(bank[3 + h // 4][:, (h % 4) * P:(h % 4 + 1) * P], ps[:, h * P:(h + 1) * P])
                last.then_inc(S["ot_ready"], 1)

            def group(kind, g):
                kd = KIND[kind]
                n, G = kd["n"], GROUPS * kind + g + 1
                t0, m0 = 4 * (G - 1), quad0[kind] + 2 * kd["n"] * g
                main, new = pairs[0], bank[2]
                pe.wait_ge(S["qbd_ready"], G)
                if G > 1:
                    pe.wait_ge(S["exp_ready"], G - 1)
                    pe.wait_ge(S["p_max"], t0)
                    pe.wait_ge(S["p_vcopy"], t0)
                    pe.wait_ge(S["p_tcopy"], t0)
                skip = dict(skip_group_check=True)
                if kind == 0:
                    for p in range(PAGES - 1, -1, -1):
                        b = (PAGES - 1 - p) * PAGE
                        pe.matmul(main[:, 0, 0:min(512, (p + 1) * P)], lfr[:, p, :], big[:, b:b + min(512, (p + 1) * P)],
                                  start=p == PAGES - 1, stop=False, **skip)
                        if p >= 4:
                            pe.matmul(main[:, 1, 0:(p - 3) * P], lfr[:, p, :], big[:, b + 512:b + (p + 1) * P],
                                      start=p == PAGES - 1, stop=False, **skip)
                    pe.matmul(new[:, 0:TS], lfn_w[:, :], big[0:TS, C_NTRI:C_NTRI + TS], start=True, stop=False, **skip)
                else:
                    for dst, a, b in ((main[:, 0, :], 0, 512), (main[:, 1, 0:P], 512, W_MAIN), (new[:, 0:TS], W_MAIN, W_MAIN + TS)):
                        pe.matmul(dst, bias_w[:, :], big[:, C_BUCKET + a:C_BUCKET + b], start=True, stop=False, **skip)

                def scores(dst, moving):
                    for h in range(HEADS):
                        for j in range(GB):
                            r = pe.matmul(dst(j), qbd[j // 2][:, j % 2, 32 * h:32 * h + 32], moving(j, h), start=False,
                                          stop=h == HEADS - 1, tile_position=(0, 32 * j), **skip)
                    return r
                def landed(m):
                    if m:
                        pe.wait_ge(S[f"kv_landed{(m - 1) % RING}"], 64 * ((m - 1) // RING + 1))
                    else:
                        pe.wait_ge(S["kv_first_landed"], 64)

                def steps(phase, p):
                    for i, after in enumerate(STEPS[kind][phase]):
                        if after == p:
                            step(t0 + 2 * phase, i)

                for p in range(n):
                    landed(m0 + p)
                    scores(lambda j: main[32 * j:32 * j + 32, p // 4, (p % 4) * P:(p % 4 + 1) * P],
                           lambda j, h: kv(m0 + p, j)[:, h * P:(h + 1) * P])\
                        .then_inc(S["kv_used"], 1)
                    if p == 0 and G > 1:
                        turn_outputs(G - 1)
                    if p == 1:
                        scores(lambda j: new[32 * j:32 * j + 32, 0:TS], lambda j, h: z[:, kd["k"] + h, TP:T])
                    steps(0, p)
                    if G == 1 and p in VN_AFTER:
                        turn_v_new(VN_AFTER.index(p))
                pe.wait_ge(S["exp_ready"], G)
                pe.wait_ge(S["p_low"], t0 + 2)
                pe.wait_ge(S["p_max"], t0 + 2)
                for p in range(n):
                    turn(bank[3 + p // 4][:, (p % 4) * P:(p % 4 + 1) * P], ps[:, p * P:(p + 1) * P])
                turn(bank[5][0:TS, 0:P], ps[:, 1024:1024 + TS]).then_inc(S["pt_sum"], 1)
                steps(1, -1)
                pe.wait_ge(S["pt_ready"], G)
                pe.wait_ge(S["p_vcopy"], t0 + 2)
                pe.wait_ge(S["p_tcopy"], t0 + 2)
                o = pairs[3]
                for p in range(n):
                    m = m0 + n + p
                    landed(m)
                    for c in range(2):
                        for j in range(GB):
                            last = pe.matmul(o[32 * j:32 * j + 32, c, :], pst[:, p, 32 * j:32 * j + 32],
                                             kv(m, j)[:, 512 * c:512 * c + 512], start=p == 0,
                                             stop=p == n - 1, tile_position=(0, 32 * j), **skip)
                    last.then_inc(S["kv_used"], 1)
                    if p == 0:
                        pe.wait_ge(S["vn_ready"], 4)
                        for c in range(2):
                            for j in range(GB):
                                a = (kind * 2 + c) * 512
                                pe.matmul(o[32 * j:32 * j + 32, c, :], pst[0:TS, 8, 32 * j:32 * j + 32],
                                          v_new[:, a:a + 512], start=False, stop=False,
                                          tile_position=(0, 32 * j), **skip)
                    steps(1, p)
                if G == 2 * GROUPS:
                    turn_outputs(G)

            for kind in (0, 1):
                for g in range(GROUPS):
                    group(kind, g)

            segments([out])
            segments(segs[segs.index(out) + 1:])

        @block.scalar
        def _(act):
            ch = Chain(act, S["act_chain"])

            def split_high(seg, j, i, halves=(0, 1)):
                n, r = seg.n0 + j, (seg.n0 + j) % 2
                half = KT // 2 * P
                for q in halves:
                    a, b = (half, seg.nk * P) if q else (0, half)
                    if q == 0:
                        act.wait_ge(S[f"w_landed{r}"], 16 * (n // 2 + 1) + 16 * i)
                    if not (isinstance(i, int) and n + 2 * i < 2):
                        act.wait_ge(S["w_used"], 2 * (n - 2) + q + 1 + 4 * i)
                    act.activation(w_hi[:, r, a:b], raw[:, r, a:b], ACT.Copy).then_inc(S["hi_ready"], 1)

            def squares():
                for c in range(SQR):
                    if c >= 2:
                        act.wait_ge(S["sq_used"], c - 1)
                    act.activation(sq[:, c % 2, :, :], x[:, SQL * c:SQL * (c + 1), :], ACT.Square)\
                       .then_inc(S["sq_ready"], 1)

            def pair_squares(seg, i):
                act.wait_ge(S["acc_b_read"], seg.rb + 1 + i)
                act.wait_ge(S["sq_used"], seg.sq0 + i)
                act.activation(sq[:, :, 2, :], x[:, bass.ds(seg.d0 + 2 * i, 2), :], ACT.Square).then_inc(S["sq_ready"], 1)

            def inverse_root(r):
                act.wait_ge(S["sq_used"], SQR + 8 * r)
                ch.link(act.activation(y0[:, :], ssb[:, 0:T], ACT.Ln, bias=eps[:, 0:1], scale=1.0 / D))
                act.activation(y0[:, :], y0[:, :], ACT.Exp, scale=-0.5).then_inc(S["y0_ready"], 1)

            def high_of_h(r):
                sh, a = 3 * r * KT, (3 * r + 1) * KT
                act.wait_ge(S["gain_ready"], r + 1)
                for c in range(SQR):
                    act.wait_ge(S["hn_ready"], SQR * r + c + 1)
                    for k in range(SQL):
                        q = hf[:, c % 2, k, 0:TP]
                        ka, ks = (a + SQL * c + k) * NC, (sh + SQL * c + k) * NC
                        last = act.activation(q, q, ACT.Identity, scale=par[:, ka:ka + 1], bias=par[:, ks:ks + 1])
                    ch.link(last)
                    act.wait_ge(S["hf_ready"], SQR * r + c + 1)
                    act.activation(h_hi[:, SQL * c:SQL * (c + 1), :], hf[:, c % 2, :, :], ACT.Copy)\
                       .then_inc(S["hhi_ready"], 1)
                    splits(split_high, r, c)

            def ada_copy(group, n):
                act.wait_ge(S["ada_used"], 4 * (group + 1) if n == 4 else 2 * KT + 2 * (group - 7))
                if not (isinstance(group, int) and group == 0):
                    act.wait_ge(S["ada_sel"], group)
                act.activation(part_sb[:, 0:n * P], ada_part[:, 0:n * P], ACT.Copy).then_inc(S["ada_sb"], 1)

            act.wait_ge(S["ld_small"], 96)
            act.wait_ge(S["dve_chain"], 2)
            act.activation(sc32[:, :, 0:NC], sc32[:, :, 0:NC], ACT.Silu).then_inc(S["c_ready"], 1)
            ada_copy(0, 4)
            with act.Fori(1, 4) as i:
                ada_copy(i, 4)
            act.wait_ge(S["ld_x"], 16)
            squares()
            inverse_root(0)
            with act.Fori(4, 2 * KT // 4) as i:
                ada_copy(i, 4)
            high_of_h(0)

            def body(seg, i):
                behind = (seg.norm is not None or seg is out) and isinstance(i, int) and i == 0
                if not behind:
                    split_high(seg, 0, i)
                if seg.ada:
                    ada_copy(8 + seg.pair0 + i, 2)
                if not behind:
                    split_high(seg, 1, i)
                if seg.kind == "up":
                    act.wait_ge(S["w_used"], 2 * (seg.n0 + 1) + 4 * i)
                    if not (isinstance(i, int) and seg.up0 + i == 0):
                        act.wait_ge(S["g_ready"], seg.up0 + i)
                    act.activation(su[:, :], acc_a[:, 0:T], ACT.Silu).then_inc(S["acc_a_read"], 1)

            def squares_body(seg, i):
                body(seg, i)
                pair_squares(seg, i - 1)

            def segments(some):
                for seg in some:
                    peel = 1 if seg.norm is not None or seg.squares else 0
                    if peel:
                        body(seg, 0)
                    if seg.squares:
                        run(seg, act, lambda i, seg=seg: squares_body(seg, i), 1)
                        r = 1 if seg in ffn1 else 2
                        splits(split_high, r, -2)
                        act.activation((nm, rs)[r - 1][:, 1:2], eps[:, 0:1], ACT.Ln, bias=eps[:, 0:1])
                        pair_squares(seg, seg.bodies - 1)
                        splits(split_high, r, -1)
                    else:
                        run(seg, act, lambda i, seg=seg: body(seg, i), peel)

            segments(ffn1)
            inverse_root(1)
            act.wait_ge(S["rev_stored"], 16)
            high_of_h(1)


            def head_squares(b):
                act.wait_ge(S["acc_b_read"], qk.rb + 1 + b)
                if not (isinstance(b, int) and b == 0):
                    act.wait_ge(S["hss_ready"], b)
                act.activation(sq[:, :, SQL - 1, :], z[:, bass.ds(2 * b, 2), :], ACT.Square).then_inc(S["hsq_ready"], 1)

            def win_body(b, j):
                seg, i = (qk, b) if j < 16 else (vv, b - 16)
                if j == 0:
                    return
                split_high(seg, 0, i)
                if 2 <= j <= 17:
                    act.wait_ge(S["hss_ready"], b - 1)
                    if j > 2:
                        act.wait_ge(S["head_ready"], b - 2)
                    ch.link(act.activation(yh[:, :, :], ss2[:, :, 0:T], ACT.Ln, bias=eps[:, 0:1], scale=1.0 / HD))
                    act.activation(yh[:, :, :], yh[:, :, :], ACT.Exp, scale=-0.5).then_inc(S["hy_ready"], 1)
                if j <= 16:
                    head_squares(b - 1)
                split_high(seg, 1, i)

            def log_forget(b):
                if b != 18:
                    return
                act.wait_ge(S["fa_ready"], 1)
                ch.link(act.activation(fe[:, :], fa_sb[:, :], ACT.Abs))
                ch.link(act.activation(fe[:, :], fe[:, :], ACT.Exp, scale=-1.0))
                act.activation(fe[:, :], fe[:, :], ACT.Ln, bias=ones[0:HEADS, 0:1]).then_inc(S["fe_ready"], 1)
            win_bodies(act, win_body, lambda: split_high(fa, 0, 0), ch, (1, 0), log_forget)

            def p_exp(t):
                act.wait_ge(S["p_max"], t + 1)
                for c, (a, n) in enumerate(((0, P), (P, 2 * P))):
                    v = pr[:, t % 2, a:a + n]
                    last = act.activation(v, v, ACT.Exp, bias=pmx[:, t % 2, c:c + 1], accum_out=psm[:, t % 2, c:c + 1])
                last.then_inc(S["p_exp"], 1)

            def p_vcopy(t):
                act.wait_ge(S["p_v"], t + 1)
                if t >= 2:
                    act.wait_ge(S["p_o"], t - 1)
                act.activation(vnat[:, t % 2, :], p_bank(t, 1)[:, 0:2 * P], ACT.Copy).then_inc(S["p_vcopy"], 1)

            def p_tcopy(t):
                act.wait_ge(S["p_t"], t + 1)
                act.activation(prt[:, t % 2, :], p_bank(t, 2)[:, 0:3 * P], ACT.Copy).then_inc(S["p_tcopy"], 1)

            def p_high(t):
                act.wait_ge(S["p_o"], t + 1)
                act.activation(h_hi[:, t, 0:TP], p_bank(t, 3)[:, 0:TP], ACT.Copy).then_inc(S["p_high"], 1)

            def steps(t):
                p_vcopy(t)
                p_exp(t)
                if t == 0:
                    v_new_copy(0)
                p_tcopy(t)
                p_vcopy(t + 1)
                p_exp(t + 1)
                if t == 0:
                    v_new_copy(1)
                p_high(t)
                p_tcopy(t + 1)
                if t == 0:
                    v_new_copy(2)
                    v_new_copy(3)

            def v_new_copy(c):
                act.wait_ge(S["vn_sum"], c + 1)
                act.activation(v_new[:, c * 512:(c + 1) * 512], bank[4][0:TS, :], ACT.Copy).then_inc(S["vn_ready"], 1)

            def group(kind, g):
                kd = KIND[kind]
                n, G = kd["n"], GROUPS * kind + g + 1
                t0 = 4 * (G - 1)
                steps(t0)
                p_high(t0 + 1)
                act.wait_ge(S["nm_ready"], G)
                if kind == 0:
                    dst = ps[:, 0:1024].rearrange("p (a b) -> p a b", a=2)
                    act.activation(dst, pairs[0][:, :, :], ACT.Exp, bias=nm[:, 0:1], accum_out=sm[:, 0:1])
                else:
                    act.activation(ps[:, 0:W_MAIN], ps[:, 0:W_MAIN], ACT.Exp, bias=nm[:, 0:1], accum_out=sm[:, 0:1])
                act.activation(ps[:, 1024:1024 + TS], ps[:, 1024:1024 + TS], ACT.Exp, bias=nm[:, 0:1],
                               accum_out=sm[:, 1:2]).then_inc(S["exp_ready"], 1)
                act.wait_ge(S["pt_sum"], G)
                act.activation(pst[:, 0:4, :].rearrange("p a b -> p (a b)"), bank[3], ACT.Copy)
                act.activation(pst[:, 4:n, :].rearrange("p a b -> p (a b)"), bank[4][:, 0:(n - 4) * P], ACT.Copy)
                act.activation(pst[0:TS, 8, :], bank[5][0:TS, 0:P], ACT.Copy).then_inc(S["pt_ready"], 1)
                steps(t0 + 2)
                act.wait_ge(S["kv_used"], quad0[kind] + RING + 2 * n + 2 * n * g)
                act.wait_ge(S["r_ready"], G)
                act.activation(ps[:, 0:1024].rearrange("p (a b) -> p a b", a=2), pairs[3][:, :, :], ACT.Copy,
                               scale=rs[:, 0:1]).then_inc(S["os_ready"], 1)
                p_high(t0 + 3)
                if G == 2 * GROUPS:
                    split_high(out, 0, 0)
                act.wait_ge(S["ot_ready"], G)
                for c in range(2):
                    dst = h_hi[:, kind * HEADS + 4 * c:kind * HEADS + 4 * c + 4, TP + 16 * g:TP + 16 * g + 16]
                    last = act.activation(dst.rearrange("p h (j s) -> p h j s", s=NS), own_rows(c), ACT.Copy)
                last.then_inc(S["oh_ready"], 1)

            for kind in (0, 1):
                for g in range(GROUPS):
                    group(kind, g)

            split_high(out, 1, 0)
            segments([out])
            inverse_root(2)
            high_of_h(2)
            act.wait_ge(S["v_stored"], 16)
            segments(segs[segs.index(out) + 1:])

        @block.vector
        def _(dve):
            ch = Chain(dve, S["dve_chain"])
            par3 = par[:, :].rearrange("p (t c) -> p t c", c=NC)

            def split_low(seg, j, i, halves=(0, 1)):
                n, r = seg.n0 + j, (seg.n0 + j) % 2
                half = KT // 2 * P
                for q in halves:
                    a, b = (half, seg.nk * P) if q else (0, half)
                    dve.wait_ge(S["hi_ready"], 2 * n + q + 1 + 4 * i)
                    dve.tensor_tensor(w_lo[:, r, a:b], raw[:, r, a:b], w_hi[:, r, a:b].bitcast(F32),
                                      ALU.subtract).then_inc(S["lo_ready"], 1)

            def refine(ssum, y, m, t, scale, n):
                dve.tensor_scalar(m, ssum, scale, EPS, ALU.mult, ALU.add).then_inc(S["ss_read"], 1)
                dve.wait_ge(S["ss_read"], n + 1)
                ch.link(dve.tensor_tensor(t, y, y, ALU.mult))
                ch.link(dve.scalar_tensor_tensor(t, t, -0.5, m, ALU.mult, ALU.mult))
                ch.link(dve.scalar_tensor_tensor(y, t, 1.5, y, ALU.add, ALU.mult))

            def samples(ap):
                return ap.rearrange("p k (b s) -> p k b s", s=NS)

            def norm_root(r):
                dve.wait_ge(S["y0_ready"], r + 1)
                refine(ssb[:, 0:T], y0[:, :], ms[:, :], tt[:, :], 1.0 / D, r if r < 2 else 2 + 16)

            def over_root(r, c):
                if c >= 2:
                    dve.wait_ge(S["h_ready"], SQR * r + c - 1)
                dve.tensor_tensor(hf[:, c % 2, :, :], x[:, SQL * c:SQL * (c + 1), :],
                                  y0[:, :].unsqueeze(1).to_broadcast([P, SQL, T]), ALU.mult).then_inc(S["hn_ready"], 1)

            def modulate(r, done=0):
                sh, a = 3 * r * KT, (3 * r + 1) * KT

                def low(c):
                    dve.wait_ge(S["hhi_ready"], SQR * r + c + 1)
                    dve.tensor_tensor(h_lo[:, SQL * c:SQL * (c + 1), :], hf[:, c % 2, :, :],
                                      h_hi[:, SQL * c:SQL * (c + 1), :].bitcast(F32), ALU.subtract)\
                       .then_inc(S["h_ready"], 1)
                for c in range(done, 1):
                    over_root(r, c)
                for c in range(SQR):
                    k0 = SQL * c
                    hs = samples(hf[:, c % 2, :, TP:T])
                    dve.wait_ge(S["hn_ready"], SQR * r + c + 1)
                    ch.link(dve.tensor_tensor(hs, hs, par3[:, a + k0:a + k0 + SQL, 1:NC].unsqueeze(3)
                                              .to_broadcast([P, SQL, NB, NS]), ALU.mult))
                    dve.tensor_tensor(hs, hs, par3[:, sh + k0:sh + k0 + SQL, 1:NC].unsqueeze(3)
                                      .to_broadcast([P, SQL, NB, NS]), ALU.add).then_inc(S["hf_ready"], 1)
                    if c:
                        low(c - 1)
                        splits(split_low, r, c - 1)
                    if c + 1 >= max(done, 1) and c + 1 < SQR:
                        over_root(r, c + 1)
                low(SQR - 1)

            def ada_finish(group, t0, n):
                dve.wait_ge(S["ada_sel"], group + 1)
                dve.tensor_tensor(par3[:, bass.ds(t0, n), :],
                                  ada_selp[:, 0:n * NC].rearrange("p (t c) -> p t c", c=NC),
                                  ba[:, bass.ds(t0, n)].unsqueeze(2).to_broadcast([P, n, NC]), ALU.add)\
                   .then_inc(S["ada_fin"], 1)

            def gain(r, groups):
                dve.wait_ge(S["ada_fin"], groups)
                a = par3[:, (3 * r + 1) * KT:(3 * r + 2) * KT, :]
                dve.scalar_tensor_tensor(a, a, 1.0, gv[:, r, :].unsqueeze(2).to_broadcast([P, KT, NC]),
                                         ALU.add, ALU.mult).then_inc(S["gain_ready"], 1)
                dve.wait_ge(S["gain_ready"], r + 1)

            def half_gate(p, groups):
                dve.wait_ge(S["ada_fin"], groups)
                a = par[:, p * KT * NC:(p + 1) * KT * NC]
                ch.link(dve.tensor_scalar(a, a, 0.5, None, ALU.mult))

            ch.link(dve.memset(sc32[:, :, NC:32], 0.0))
            ch.link(dve.memset(eps[:, :], EPS))
            dve.wait_ge(S["ld_small"], 96)
            ada_finish(0, 0, 4)
            with dve.Fori(1, 2 * KT // 4 - 1) as i:
                ada_finish(i, 4 * i, 4)
            norm_root(0)
            over_root(0, 0)
            over_root(0, 1)
            ada_finish(7, 4 * 7, 4)
            gain(0, 8)
            modulate(0, 2)
            for k in range(4):
                dve.tensor_scalar(nw[:, 8 * k:8 * k + 8], nw4[:, k:k + 1].to_broadcast([P, 8]), SCALE if k % 2 == 0 else 1.0,
                                  None, ALU.mult)
            dve.wait_ge(S["rev_sum"], 1)
            dve.tensor_tensor(rev[:, :], bank[5][0:HEADS, 0:REV], adr[:, :], ALU.add).then_inc(S["rev_ready"], 1)
            def add_gated(seg, j, i):
                bank = (acc_a, acc_b)[j]
                n = seg.n0 + j
                dve.wait_ge(S["w_used"], 2 * (n + 1) + 4 * i)
                d = seg.d0 + j + 2 * i
                gate = seg.gate * KT + d
                xs = x[:, bass.ds(d, 1), TP:T].rearrange("p k (b s) -> p (k b) s", s=NS)
                xp = x[:, bass.ds(d, 1), 0:TP].rearrange("p k t -> p (k t)")
                ch.link(dve.tensor_tensor(tmps[:, j, :, :], bank[:, TP:T].rearrange("p (b s) -> p b s", s=NS),
                                          par[:, bass.ds(gate * NC + 1, NB)].unsqueeze(2).to_broadcast([P, NB, NS]),
                                          ALU.mult))
                ch.link(dve.tensor_tensor(xs, xs, tmps[:, j, :, :], ALU.add))
                dve.scalar_tensor_tensor(xp, bank[:, 0:TP], par[:, bass.ds(gate * NC, 1)], xp,
                                         ALU.mult, ALU.add).then_inc(S["acc_b_read" if j else "acc_a_read"], 1)

            def gated_unit(seg, i):
                dve.wait_ge(S["w_used"], 2 * (seg.n0 + 2) + 4 * i)
                dve.wait_ge(S["acc_a_read"], seg.ra + 1 + i)
                dve.tensor_tensor(gf[:, :], su[:, :], acc_b[:, 0:T], ALU.mult).then_inc(S["acc_b_read"], 1)
                dve.wait_ge(S["acc_b_read"], seg.rb + 1 + i)
                gh, gl = g_hi[:, bass.ds(i, 1), :], g_lo[:, bass.ds(i, 1), :]
                gg = gf[:, :].unsqueeze(1)
                ch.link(dve.tensor_copy(gh, gg))
                dve.tensor_tensor(gl, gg, gh.bitcast(F32), ALU.subtract).then_inc(S["g_ready"], 1)

            def after_b(seg, i):
                if seg.kind == "up":
                    gated_unit(seg, i)
                elif seg.kind == "down":
                    add_gated(seg, 1, i)

            LINKS = {"up": 1, "down": 4}

            def body(seg, i, late):
                behind = (seg.norm is not None or seg is out) and isinstance(i, int)
                if not behind:
                    split_low(seg, 0, i)
                if late:
                    after_b(*late)
                if not behind:
                    split_low(seg, 1, i)
                if seg.ada:
                    ada_finish(8 + seg.pair0 + i, 2 * KT + 2 * seg.pair0 + 2 * i, 2)
                if seg.kind == "down":
                    add_gated(seg, 0, i)

            def squares_body(seg, i):
                body(seg, i, (seg, i - 1))
                dve.wait_ge(S["sq_ready"], seg.sq0 + i)
                ch.link(dve.tensor_tensor(sq_sum[:, :], sq_sum[:, :], sq[:, 0, 2, :], ALU.add))
                dve.tensor_tensor(sq_sum[:, :], sq_sum[:, :], sq[:, 1, 2, :], ALU.add).then_inc(S["sq_used"], 1)
                dve.wait_ge(S["sq_used"], seg.sq0 + i)

            def segments(some):
                late = None
                for seg in some:
                    if seg.gate == 2 and seg.b0 == CHUNKS[0][1]:
                        half_gate(2, 8 + 8)
                    if seg is ffn1[-1]:
                        gain(1, PAIRS)
                        gain(2, PAIRS)
                        half_gate(8, PAIRS)
                    body(seg, 0, late)
                    if seg.squares:
                        ch.link(dve.memset(sq_sum[:, :], 0.0))
                        run(seg, dve, lambda i, seg=seg: squares_body(seg, i), 1, ch, LINKS[seg.kind] + 1)
                    else:
                        run(seg, dve, lambda i, seg=seg: body(seg, i, (seg, i - 1)), 1, ch, LINKS[seg.kind])
                    late = seg, seg.bodies - 1
                r = 1 if seg in ffn1 else 2
                if seg.squares:
                    splits(split_low, r, -2)
                after_b(*late)
                if seg.squares:
                    splits(split_low, r, -1)

            segments(ffn1)
            norm_root(1)
            modulate(1)

            def z_copy(seg, b, j):
                dve.wait_ge(S["w_used"], 2 * (seg.n0 + j + 1) + 4 * (b if seg is qk else b - 16))
                dve.tensor_copy(z[:, bass.ds(2 * b + j, 1), :], (acc_a, acc_b)[j][:, 0:T].unsqueeze(1))\
                   .then_inc(S["acc_b_read" if j else "acc_a_read"], 1)

            def head_norm(b):
                dve.wait_ge(S["hy_ready"], b + 1)
                refine(ss2[:, :, 0:T], yh[:, :, :], mh[:, :, :], th[:, :, :], 1.0 / HD, 2 + b)
                for j in range(2):
                    zt = z[:, bass.ds(2 * b + j, 1), :]
                    last = dve.scalar_tensor_tensor(zt, zt, nw[:, bass.ds(2 * b + j, 1)], yh[:, j, :].unsqueeze(1),
                                                    ALU.mult, ALU.mult)
                last.then_inc(S["head_ready"], 1)

            def win_body(b, j):
                seg, i = (qk, b) if j < 16 else (vv, b - 16)
                if j:
                    split_low(seg, 0, i)
                    z_copy(qk if j <= 16 else vv, b - 1, 1)
                    split_low(seg, 1, i)
                if 2 <= j <= 17:
                    head_norm(b - 2)
                z_copy(seg, b, 0)

            def gates(b):
                if b == 18:
                    gate_sum()
                elif b == 23:
                    dve.wait_ge(S["fe_ready"], 1)
                    dve.scalar_tensor_tensor(lf[:, :], fa_sb[:, :], 0.0, fe[:, :], ALU.min, ALU.subtract)\
                       .then_inc(S["lf_ready"], 1)
                elif b == 24:
                    dve.wait_ge(S["lft_sum"], 1)
                    dve.tensor_copy(lft[:, 0:2, :], bank[7][:, 0:2 * HEADS].rearrange("p (t h) -> p t h", t=2))
                    dve.tensor_copy(lft[0:TS, 2, :], bank[7][0:TS, 2 * HEADS:3 * HEADS]).then_inc(S["lft_ready"], 1)
                    dve.memset(qbd[0][:, :, :], 0.0)
                    dve.wait_ge(S["ld_att"], 5 * 16)
                    ch.link(dve.tensor_tensor(bias_w[:, :].rearrange("p (j h q) -> p j h q", j=GB, q=NS),
                                              rbr[:, :].unsqueeze(1).unsqueeze(3).to_broadcast([P, GB, HEADS, NS]),
                                              big[:, C_DELTA:C_DELTA + NS].unsqueeze(1).unsqueeze(1)
                                              .to_broadcast([P, GB, HEADS, NS]), ALU.mult))

            def gate_sum():
                dve.wait_ge(S["w_used"], 2 * (fa.n0 + 1))
                dve.tensor_scalar(fa_sb[:, :], bank[2][0:HEADS, 0:T], bfs[:, 0:1], None, ALU.add)\
                   .then_inc(S["fa_ready"], 1)
            win_bodies(dve, win_body, lambda: split_low(fa, 0, 0), ch, (3, 0), gates)
            z_copy(vv, 23, 1)
            def p_low(t):
                dve.wait_ge(S["p_high"], t + 1)
                dve.tensor_tensor(h_lo[:, t, 0:TP], p_bank(t, 3)[:, 0:TP], h_hi[:, t, 0:TP].bitcast(F32),
                                  ALU.subtract).then_inc(S["p_low"], 1)

            def p_max(t):
                r = t % 2
                if t == HEADS:
                    dve.wait_ge(S["toe_landed"], 16)
                bias = big[:, C_CAUSAL:C_CAUSAL + 2 * P] if t < HEADS else toe[:, t % HEADS, :]
                dve.wait_ge(S["p_s"], t + 1)
                if t >= 2:
                    dve.wait_ge(S["p_t"], t - 1)
                scores = p_bank(t, 0)
                dve.tensor_tensor(pr[:, r, 0:P], scores[:, 0:P], bias[:, P:2 * P], ALU.add)
                ch.link(dve.tensor_tensor(pr[:, r, P:3 * P], scores[:, P:3 * P], bias, ALU.add))
                dve.tensor_reduce(pmx[:, r, 0:1], pr[:, r, 0:P], AX.X, ALU.max, negate=True)
                dve.tensor_reduce(pmx[:, r, 1:2], pr[:, r, P:3 * P], AX.X, ALU.max, negate=True)\
                   .then_inc(S["p_max"], 1)

            def p_scale(t):
                r = t % 2
                dve.wait_ge(S["p_exp"], t + 1)
                ch.link(dve.reciprocal(psm[:, r, :], psm[:, r, :]))
                dve.tensor_scalar(pr[:, r, 0:P], pr[:, r, 0:P], psm[:, r, 0:1], None, ALU.mult)
                dve.tensor_scalar(pr[:, r, P:3 * P], pr[:, r, P:3 * P], psm[:, r, 1:2], None, ALU.mult)\
                   .then_inc(S["p_scaled"], 1)

            def steps(t):
                p_max(t)
                p_scale(t)
                p_max(t + 1)
                p_scale(t + 1)
                p_low(t)

            dve.wait_ge(S["lf_landed"], 16 * NB * PAGES)
            dve.wait_ge(S["lft_ready"], 1)
            dve.tensor_copy(lfn_w[:, :].rearrange("p (j h q) -> p j h q", j=GB, q=NS),
                            lft[0:TS, 2, :].unsqueeze(1).unsqueeze(3).to_broadcast([TS, GB, HEADS, NS]))
            ch.link(dve.memset(qbd[1][:, :, :], 0.0))

            def moving_parts(kind, g):
                kd = KIND[kind]
                for j in range(GB):
                    b = TP + 16 * g + NS * j
                    last = dve.tensor_copy(qbd[j // 2][:, j % 2, :].rearrange("p (h x) -> p h x", x=32 + NS)[:, :, 0:NS],
                                           z[:, kd["q"]:kd["q"] + HEADS, b:b + NS])
                    if kind == 0:
                        a = (GB * g + j) * PAGES
                        last = dve.tensor_copy(lfr[:, :, 32 * j:32 * j + 32].rearrange("p a (h q) -> p a h q", q=NS),
                                               lfc[:, a:a + PAGES, :].unsqueeze(3).to_broadcast([P, PAGES, HEADS, NS]))
                last.then_inc(S["qbd_ready"], 1)

            def group(kind, g):
                kd = KIND[kind]
                n, G = kd["n"], GROUPS * kind + g + 1
                t0 = 4 * (G - 1)
                steps(t0)
                dve.wait_ge(S["kv_used"], quad0[kind] + RING + n + 2 * n * g)
                ch.link(dve.tensor_tensor(ps[:, 1024:1024 + TS], bank[2][:, 0:TS],
                                          big[:, kd["new"] + TS * g:kd["new"] + TS * g + TS], ALU.add))
                dve.tensor_reduce(mx[:, 1:2], ps[:, 1024:1024 + TS], AX.X, ALU.max)
                if kind == 0:
                    ch.link(dve.tensor_reduce(mx[:, 0:1], pairs[0][:, :, :], AX.XY, ALU.max))
                else:
                    dve.tensor_tensor(ps[:, 0:512], bank[0], big[:, C_LOGN:C_LOGN + 512], ALU.add)
                    ch.link(dve.tensor_tensor(ps[:, 512:W_MAIN], bank[1][:, 0:P], big[:, C_LOGN + 512:C_LOGN + W_MAIN],
                                              ALU.add))
                    ch.link(dve.tensor_reduce(mx[:, 0:1], ps[:, 0:W_MAIN], AX.X, ALU.max))
                dve.tensor_reduce(nm[:, 0:1], mx[:, :], AX.X, ALU.max, negate=True).then_inc(S["nm_ready"], 1)
                p_low(t0 + 1)
                dve.wait_ge(S["exp_ready"], G)
                ch.link(dve.tensor_reduce(sm[:, 0:1], sm[:, :], AX.X, ALU.add))
                dve.reciprocal(rs[:, 0:1], sm[:, 0:1]).then_inc(S["r_ready"], 1)
                if G < 2 * GROUPS:
                    moving_parts(G // GROUPS, G % GROUPS)
                steps(t0 + 2)
                p_low(t0 + 3)
                if G == 2 * GROUPS:
                    dve.wait_ge(S["ot_ready"], G)
                    split_low(out, 0, 0)
                dve.wait_ge(S["oh_ready"], G)
                for c in range(2):
                    sl = (slice(None), slice(kind * HEADS + 4 * c, kind * HEADS + 4 * c + 4),
                          slice(TP + 16 * g, TP + 16 * g + 16))
                    last = dve.tensor_tensor(h_lo[sl].rearrange("p h (j s) -> p h j s", s=NS), own_rows(c),
                                             h_hi[sl].bitcast(F32).rearrange("p h (j s) -> p h j s", s=NS), ALU.subtract)
                last.then_inc(S["ol_ready"], 1)

            moving_parts(0, 0)
            dve.wait_ge(S["ncum_sum"], 1)
            dve.tensor_copy(ncum[:, :], bank[6][0:HEADS, 0:TP]).then_inc(S["ncum_ready"], 1)
            for kind in (0, 1):
                for g in range(GROUPS):
                    group(kind, g)

            split_low(out, 1, 0)
            segments([out])
            norm_root(2)
            modulate(2)
            dve.wait_ge(S["heads_stored"], 4 * 16)
            dve.wait_ge(S["v_stored"], 16)
            segments(segs[segs.index(out) + 1:])


def _tiles(w, k, n):
    return np.ascontiguousarray(w.reshape(k, P, n, P).transpose(2, 1, 0, 3).reshape(n, P, k * P))


def _bucket(dist):
    d = np.maximum(dist, 16).astype(np.float64)
    log_b = np.minimum((16 + np.log(d / 16) / np.log(128.0) * 16).astype(np.int64), 31)
    return np.where(dist < 16, np.maximum(dist, 0), log_b)


def _log_patterns(dist):
    n = sum(((dist >= 0) & (dist % r == 0) & (dist <= w)).astype(np.int64) for w, r in ((128, 1), (512, 4), (2048, 16)))
    return np.where(n > 0, np.log(np.maximum(n, 1)), NEG).astype(np.float32)


def _window_keys():
    early = (16 * np.arange(32)[:, None] + np.arange(NS)[None, :]).reshape(-1)
    return np.concatenate([early, 512 + np.arange(512)]).reshape(WT, P)


def _constants():
    f = np.float32
    eye = np.eye(P, dtype=f)
    sel = np.zeros((P, 16), f)
    for j in range(4):
        sel[32 * j + np.arange(NC), np.arange(NC)] = 1
    small = np.concatenate([eye, np.ones((P, P), f), sel], 1)
    k = np.arange(P)
    band = np.concatenate([np.ones((P, (PAGES - 1) * P), f), (k[:, None] > k[None, :]).astype(f)], 1)
    pos = _window_keys().reshape(-1)
    s = np.arange(NS)
    new = np.arange(TS) % NS
    dist = 1024 + s[:, None] - pos[None, :]
    dist_new = s[:, None] - new[None, :]
    d = np.concatenate([dist, dist_new], 1)
    onehot = np.zeros((NS, 32, d.shape[1]), f)
    onehot[:, :, :] = (_bucket(d)[:, None, :] == np.arange(32)[None, :, None])
    row_q = np.arange(P) % NS
    row_b = np.arange(P) // 32
    addc = _log_patterns(dist)[row_q]
    same = [(np.arange(TS)[None, :] // NS == GB * g + row_b[:, None]) for g in range(2)]
    new_dil = [np.where(m, _log_patterns(dist_new)[row_q], f(NEG)) for m in same]
    new_fox = [np.where(m & (dist_new[row_q] >= 0), f(0), f(NEG)) for m in same]
    causal = np.concatenate([np.zeros((P, P), f), np.where(k[None, :] <= k[:, None], f(0), f(NEG))], 1)
    negtri = np.concatenate([-(k[:, None] <= k[None, :]).astype(f), -np.ones((P, P), f)], 1)
    delta = (np.arange(P)[:, None] // 32 == s[None, :]).astype(f)
    t = np.arange(TS)
    ntri = np.zeros((P, TS), f)
    ntri[:TS] = -((t[:, None] // NS == t[None, :] // NS) & (t[:, None] <= t[None, :])).astype(f)
    big = np.concatenate([band, onehot.reshape(P, -1), addc, *new_dil, *new_fox, causal, negtri, delta, ntri], 1)
    back = 255 - np.arange(383)
    oh_rev = (_bucket(back)[None, :] == np.arange(32)[:, None]).astype(f) * (back >= 0)[None, :].astype(f)
    lp = _log_patterns(back)
    add_rev = np.broadcast_to(lp, (HEADS, 383)).astype(f)
    selh = np.zeros((HEADS, HEADS, P), f)
    selh[np.arange(HEADS), np.arange(HEADS)] = 1
    return small.astype(f), np.ascontiguousarray(big.astype(f)), np.ascontiguousarray(oh_rev.astype(f)), \
        np.ascontiguousarray(add_rev), selh.reshape(HEADS, HEADS * P)


def _lay_out(i):
    a = {k: np.asarray(v) for k, v in i.items()}
    cat = np.concatenate

    def feat(v):
        return np.ascontiguousarray(v.reshape(-1, KT, P).transpose(2, 1, 0))

    def up(w1, w3):
        return np.ascontiguousarray(np.stack([_tiles(w1[0], KT, FF), _tiles(w3[0], KT, FF)], 1).reshape(2 * FF, P, KT * P))

    w = a["w_in"][0]
    W = HEADS * HD
    fa = 3 * W
    cols = [w[:, fa:fa + P]] + [w[:, o:o + W] for o in (0, W, fa + HEADS, fa + HEADS + W, 2 * W, fa + HEADS + 2 * W)]
    small, big, ohrev, addrev, selh = _constants()
    keys = _window_keys()
    out = dict(
        xT=feat(cat([a["x_prompt"].reshape(TP, D), a["x_sample"].reshape(TS, D)])),
        cT=feat(cat([a["c_prompt"], a["c_sample"]])),
        gT=np.ascontiguousarray(np.stack([a[n][0].reshape(KT, P).T for n in ("g_ffn1", "g_mix", "g_ffn2")], 1)),
        bada=np.ascontiguousarray(a["b_ada"][0].reshape(ADA, P).T),
        nwT=np.ascontiguousarray(np.stack([a[n][0] for n in ("qn_fox", "kn_fox", "qn_dil", "kn_dil")], 1)),
        bfg=np.ascontiguousarray(a["b_forget"].reshape(HEADS, 1)),
        relb=np.ascontiguousarray(a["rel_bias"]),
        pt=np.ascontiguousarray(a["page_table"].reshape(1, NB * PAGES)),
        cst=small, cst2=big, ohrev=ohrev, addrev=addrev, selh=selh,
        w_ada=np.ascontiguousarray(a["w_ada"][0].reshape(2, KT // 2, P, ADA // 2, 2 * P).transpose(3, 0, 2, 1, 4)
                                   .reshape(ADA, P, KT * P)),
        w13_1=up(a["w1_ffn1"], a["w3_ffn1"]), w2_1=_tiles(a["w2_ffn1"][0], FF, KT),
        w_in=_tiles(cat(cols, 1), KT, 49), w_out=_tiles(a["w_out"][0], KT, KT),
        w13_2=up(a["w1_ffn2"], a["w3_ffn2"]), w2_2=_tiles(a["w2_ffn2"][0], FF, KT),
        kpool=np.ascontiguousarray(a["cache_fox_k"][0].transpose(0, 3, 2, 1).reshape(POOL, HD, HEADS * PAGE)),
        vpool=np.ascontiguousarray(a["cache_fox_v"][0].reshape(POOL, PAGE, W)),
        lfpool=np.ascontiguousarray(a["cache_fox_logf"][0]),
        wink=np.ascontiguousarray(a["cache_win_k"][0][:, keys].transpose(0, 1, 4, 3, 2).reshape(NB, WT, HD, HEADS * P)),
        winv=np.ascontiguousarray(a["cache_win_v"][0][:, keys].reshape(NB, WT, P, W)),
    )
    return out


_OUTS = dict(y_out=(P, KT, T), kv_out=(4, P, HEADS, T), lf_out=(HEADS, T))


def kernel(**inputs):
    import concourse.bacc as _bacc
    from concourse.bass_utils import run_bass_kernel_spmd as _run

    arrays = _lay_out(inputs)
    nc = _bacc.Bacc("TRN2", target_bir_lowering=False, num_devices=1)
    args = [nc.dram_tensor(f"in_{n}_dram", v.shape, mybir.dt.from_np(v.dtype), kind="ExternalInput").ap()
            for n, v in arrays.items()]
    args += [nc.dram_tensor(f"out_{n}_dram", s, F32, kind="ExternalOutput").ap() for n, s in _OUTS.items()]
    decoder_layer(nc, *args)
    r = _run(nc, [{f"in_{n}_dram": v for n, v in arrays.items()}], core_ids=[0])
    y, kv, lf = (r.results[0][f"out_{n}_dram"] for n in _OUTS)
    y = y.transpose(2, 1, 0).reshape(T, D)
    kv = kv.transpose(0, 3, 2, 1)
    lf = lf.T

    def prompt(v):
        return np.ascontiguousarray(v[None, None, :TP])

    def sample(v):
        return np.ascontiguousarray(v[TP:].reshape((1, NB, NS) + v.shape[1:]))

    kf, kd, vf, vd = kv
    return (np.ascontiguousarray(y[None, :TP]), np.ascontiguousarray(y[TP:].reshape(NB, NS, D)),
            prompt(kf), prompt(vf), prompt(lf), prompt(kd), prompt(vd),
            sample(kf), sample(vf), sample(lf), sample(kd), sample(vd))
```
